# Optimizing a Trainium2 kernel written in Bass

```python
import jax
import jax.numpy as jnp
from jax import lax
import numpy as np

D_MODEL = 1024
BATCH = 1
SEQ = 512
DEPTH = 1

HEAD_DIM = 64
RWKV_WIDTH = D_MODEL // 2
RWKV_HEADS = RWKV_WIDTH // HEAD_DIM
ATTN_WIDTH = D_MODEL - RWKV_WIDTH
ATTN_HEADS = ATTN_WIDTH // HEAD_DIM
MIX_WIDTH = RWKV_WIDTH + ATTN_WIDTH
DECAY_RANK = 64
ICLR_RANK = 64
GATE_RANK = 128
RWKV_SPLITS = (RWKV_WIDTH, 2 * RWKV_WIDTH, 3 * RWKV_WIDTH, 3 * RWKV_WIDTH + DECAY_RANK, 3 * RWKV_WIDTH + DECAY_RANK + ICLR_RANK)
RWKV_COLS = 3 * RWKV_WIDTH + DECAY_RANK + ICLR_RANK + GATE_RANK
IN_COLS = RWKV_COLS + 3 * ATTN_WIDTH
DILATED_PATTERNS = ((128, 1), (512, 4), (2048, 16))
ROPE_THETA = 10000.0
PEER_HEADS = 8
PEER_N_KEYS = 128
PEER_N_EXPERTS = PEER_N_KEYS * PEER_N_KEYS
PEER_QUERY_DIM = 256
PEER_SUBKEY_DIM = PEER_QUERY_DIM // 2
PEER_TOPK = 16
PEER_TOKEN_BLOCK = 128
RMS_EPS = 1e-6
GN_EPS = 64e-5

kernel_name = 'hybrid_rwkv7_dilated_attn_peer'

def rms_norm(x, g):
    xf = x.astype(jnp.float32)
    y = xf * lax.rsqrt(jnp.mean(xf * xf, axis=-1, keepdims=True) + RMS_EPS)
    return (y * g.astype(jnp.float32)).astype(x.dtype)

def rope(x):
    s, dh = x.shape[1], x.shape[-1]
    inv_freq = ROPE_THETA ** (-jnp.arange(0, dh, 2, dtype=jnp.float32) / dh)
    ang = jnp.arange(s, dtype=jnp.float32)[:, None] * inv_freq[None, :]
    cos = jnp.cos(ang)[None, :, None, :]
    sin = jnp.sin(ang)[None, :, None, :]
    xf = x.astype(jnp.float32)
    x1, x2 = xf[..., : dh // 2], xf[..., dh // 2:]
    return jnp.concatenate([x1 * cos - x2 * sin, x1 * sin + x2 * cos], axis=-1).astype(x.dtype)

def rwkv7_time_mix(z, mu, w0, w_up, a0, a_up, g_up, k_k, k_a, r_k, gn_w, gn_b):
    f32 = jnp.float32
    b, s, _ = z.shape
    zf = z.astype(f32)
    z_prev = jnp.pad(zf, ((0, 0), (1, 0), (0, 0)))[:, :-1]
    zm = zf + (z_prev - zf) * mu.astype(f32)
    r, k, v, wd, ad, gd = jnp.split(zm, RWKV_SPLITS, axis=-1)
    w_log = -jax.nn.softplus(-(w0.astype(f32) + jnp.tanh(wd) @ w_up.astype(f32))) - 0.5
    decay = jnp.exp(-jnp.exp(w_log))
    a = jax.nn.sigmoid(a0.astype(f32) + ad @ a_up.astype(f32))
    g = jax.nn.sigmoid(gd) @ g_up.astype(f32)

    def heads(t):
        return t.reshape(b, s, RWKV_HEADS, HEAD_DIM)

    kk = heads(k * k_k.astype(f32))
    kk = kk / jnp.maximum(jnp.sqrt(jnp.sum(kk * kk, axis=-1, keepdims=True)), 1e-12)
    k = k * (1.0 + (a - 1.0) * k_a.astype(f32))
    r_h, k_h, v_h, w_h, a_h = heads(r), heads(k), heads(v), heads(decay), heads(a)

    def step(state, inp):
        r_t, w_t, k_t, v_t, a_t, b_t = inp
        sa = jnp.einsum('bhij,bhj->bhi', state, a_t)
        state = (state * w_t[:, :, None, :] + sa[..., None] * b_t[:, :, None, :]
                 + v_t[..., None] * k_t[:, :, None, :])
        return state, jnp.einsum('bhij,bhj->bhi', state, r_t)

    xs = tuple(jnp.moveaxis(t, 1, 0) for t in (r_h, w_h, k_h, v_h, -kk, kk * a_h))
    state0 = jnp.zeros((b, RWKV_HEADS, HEAD_DIM, HEAD_DIM), f32)
    _, y = lax.scan(step, state0, xs)
    y = jnp.moveaxis(y, 0, 1)
    mean = jnp.mean(y, axis=-1, keepdims=True)
    var = jnp.mean(jnp.square(y - mean), axis=-1, keepdims=True)
    y = ((y - mean) * lax.rsqrt(var + GN_EPS)).reshape(b, s, RWKV_WIDTH) * gn_w.astype(f32) + gn_b.astype(f32)
    bonus = jnp.sum(r_h * k_h * r_k.astype(f32), axis=-1, keepdims=True) * v_h
    return ((y + bonus.reshape(b, s, RWKV_WIDTH)) * g).astype(z.dtype)

def dilated_window_partial(q, k, v, window, dilation):
    f32 = jnp.float32
    b, s, h, dh = q.shape
    n = window // dilation
    span = dilation * n
    sp = -(-s // span) * span
    nb = sp // span

    def to_blocks(t):
        t = jnp.pad(t.astype(f32), ((0, 0), (0, sp - s), (0, 0), (0, 0)))
        t = jnp.moveaxis(t.reshape(b, sp // dilation, dilation, h, dh), 2, 1)
        return t.reshape(b, dilation, nb, n, h, dh)

    def with_prev(t):
        prev = jnp.pad(t, ((0, 0), (0, 0), (1, 0), (0, 0), (0, 0), (0, 0)))[:, :, :-1]
        return jnp.concatenate([prev, t], axis=3)

    qb = to_blocks(q)
    kw = with_prev(to_blocks(k))
    vw = with_prev(to_blocks(v))
    scores = jnp.einsum('brnqhd,brnkhd->brnhqk', qb, kw) * (dh ** -0.5)
    qi = jnp.arange(n)[:, None]
    ki = jnp.arange(2 * n)[None, :]
    dist = n + qi - ki
    band = (dist >= 0) & (dist <= n)
    valid = band[None] & ((jnp.arange(nb)[:, None, None] > 0) | (ki[None] >= n))
    scores = jnp.where(valid[None, None, :, None], scores, -jnp.inf)
    m = jnp.max(scores, axis=-1)
    p = jnp.exp(scores - m[..., None])
    l = jnp.sum(p, axis=-1)
    num = jnp.einsum('brnhqk,brnkhd->brnqhd', p, vw)

    def from_blocks(t):
        rest = t.shape[4:]
        t = jnp.moveaxis(t.reshape(b, dilation, sp // dilation, *rest), 1, 2)
        return t.reshape(b, sp, *rest)[:, :s]

    return from_blocks(num), from_blocks(jnp.moveaxis(m, 3, 4)), from_blocks(jnp.moveaxis(l, 3, 4))

def dilated_mixture_attention(z):
    b, s, _ = z.shape
    q, k, v = jnp.split(z, 3, axis=-1)
    q = rope(q.reshape(b, s, ATTN_HEADS, HEAD_DIM))
    k = rope(k.reshape(b, s, ATTN_HEADS, HEAD_DIM))
    v = v.reshape(b, s, ATTN_HEADS, HEAD_DIM)
    parts = [dilated_window_partial(q, k, v, w, d) for (w, d) in DILATED_PATTERNS]
    m_all = jnp.stack([p[1] for p in parts])
    wts = jnp.exp(m_all - jnp.max(m_all, axis=0))
    num = sum(p[0] * wts[i][..., None] for i, p in enumerate(parts))
    den = sum(p[2] * wts[i] for i, p in enumerate(parts))
    return (num / den[..., None]).reshape(b, s, ATTN_WIDTH).astype(z.dtype)

def peer_ffn(x, w_q, sub_keys, u_tab, v_tab):
    f32 = jnp.float32
    b, s, d = x.shape
    q = jnp.einsum('bsd,dq->bsq', x, w_q).reshape(b, s, PEER_HEADS, 2, PEER_SUBKEY_DIM)
    scores = jnp.einsum('bshcq,ckq->bshck', q.astype(f32), sub_keys.astype(f32))
    top_s, top_i = lax.top_k(scores, PEER_TOPK)
    cand_s = (top_s[..., 0, :, None] + top_s[..., 1, None, :]).reshape(b, s, PEER_HEADS, PEER_TOPK * PEER_TOPK)
    cand_i = (top_i[..., 0, :, None] * PEER_N_KEYS + top_i[..., 1, None, :]).reshape(b, s, PEER_HEADS, PEER_TOPK * PEER_TOPK)
    best_s, pos = lax.top_k(cand_s, PEER_TOPK)
    expert = jnp.take_along_axis(cand_i, pos, axis=-1)
    gate = jax.nn.softmax(best_s, axis=-1).astype(x.dtype)
    t = b * s
    nblk = t // PEER_TOKEN_BLOCK
    xb = x.reshape(nblk, PEER_TOKEN_BLOCK, d)
    eb = expert.reshape(nblk, PEER_TOKEN_BLOCK, PEER_HEADS, PEER_TOPK)
    gb = gate.reshape(nblk, PEER_TOKEN_BLOCK, PEER_HEADS, PEER_TOPK)

    def eval_block(args):
        xc, ec, gc = args
        u = u_tab[ec]
        act = jax.nn.gelu(jnp.einsum('cd,chkd->chk', xc, u), approximate=False)
        return jnp.einsum('chk,chkd->cd', act * gc, v_tab[ec])

    y = lax.map(eval_block, (xb, eb, gb))
    return y.reshape(b, s, d)

def setup_inputs(seed: int = 0) -> dict:
    key = jax.random.key(seed)
    ks = jax.random.split(key, 22)
    L, D = DEPTH, D_MODEL
    f32 = jnp.float32

    def nrm(k, shape, scale):
        return jax.random.normal(k, shape, f32) * scale

    return {
        'x': nrm(ks[0], (BATCH, SEQ, D), 1.0),
        'norm_mix': 1.0 + nrm(ks[1], (L, D), 0.02),
        'w_in': nrm(ks[2], (L, D, IN_COLS), D ** -0.5),
        'rwkv_mu': jax.random.uniform(ks[3], (L, RWKV_COLS), f32),
        'rwkv_w0': jax.random.uniform(ks[4], (L, RWKV_WIDTH), f32, -6.0, -1.0),
        'rwkv_w_up': nrm(ks[5], (L, DECAY_RANK, RWKV_WIDTH), 0.1),
        'rwkv_a0': nrm(ks[6], (L, RWKV_WIDTH), 0.1),
        'rwkv_a_up': nrm(ks[7], (L, ICLR_RANK, RWKV_WIDTH), 0.5 * ICLR_RANK ** -0.5),
        'rwkv_g_up': nrm(ks[8], (L, GATE_RANK, RWKV_WIDTH), GATE_RANK ** -0.5),
        'rwkv_k_k': 0.85 + nrm(ks[9], (L, RWKV_WIDTH), 0.02),
        'rwkv_k_a': 1.0 + nrm(ks[10], (L, RWKV_WIDTH), 0.02),
        'rwkv_r_k': nrm(ks[11], (L, RWKV_HEADS, HEAD_DIM), 0.1),
        'rwkv_gn_w': 1.0 + nrm(ks[12], (L, RWKV_WIDTH), 0.02),
        'rwkv_gn_b': nrm(ks[13], (L, RWKV_WIDTH), 0.02),
        'w_out': nrm(ks[14], (L, MIX_WIDTH, D), MIX_WIDTH ** -0.5),
        'norm_ffn': 1.0 + nrm(ks[15], (L, D), 0.02),
        'peer_w_q': nrm(ks[16], (L, D, PEER_HEADS * PEER_QUERY_DIM), D ** -0.5),
        'peer_sub_keys': nrm(ks[17], (L, 2, PEER_N_KEYS, PEER_SUBKEY_DIM), PEER_SUBKEY_DIM ** -0.5),
        'peer_u': nrm(ks[18], (L, PEER_N_EXPERTS, D), D ** -0.5),
        'peer_v': nrm(ks[19], (L, PEER_N_EXPERTS, D), 0.5),
        'norm_final': 1.0 + nrm(ks[20], (D,), 0.02),
    }

def reference(x, norm_mix, w_in, rwkv_mu, rwkv_w0, rwkv_w_up, rwkv_a0, rwkv_a_up, rwkv_g_up,
              rwkv_k_k, rwkv_k_a, rwkv_r_k, rwkv_gn_w, rwkv_gn_b, w_out, norm_ffn,
              peer_w_q, peer_sub_keys, peer_u, peer_v, norm_final):
    h = x
    for layer in range(DEPTH):
        xn = rms_norm(h, norm_mix[layer])
        z = jnp.einsum('bsd,dc->bsc', xn, w_in[layer])
        y_rwkv = rwkv7_time_mix(z[..., :RWKV_COLS], rwkv_mu[layer], rwkv_w0[layer], rwkv_w_up[layer],
                                rwkv_a0[layer], rwkv_a_up[layer], rwkv_g_up[layer], rwkv_k_k[layer],
                                rwkv_k_a[layer], rwkv_r_k[layer], rwkv_gn_w[layer], rwkv_gn_b[layer])
        y_attn = dilated_mixture_attention(z[..., RWKV_COLS:])
        mixed = jnp.concatenate([y_rwkv, y_attn], axis=-1)
        h = h + jnp.einsum('bsm,md->bsd', mixed, w_out[layer])
        h = h + peer_ffn(rms_norm(h, norm_ffn[layer]), peer_w_q[layer], peer_sub_keys[layer],
                         peer_u[layer], peer_v[layer])
    return rms_norm(h, norm_final)


_drawn_inputs = setup_inputs


def setup_inputs(seed=0):
    import zlib

    import numpy as np

    out = dict(_drawn_inputs(seed))
    spreads = {}
    factors = {}
    for name, (base, spread) in spreads.items():
        noise = np.random.default_rng([zlib.crc32(name.encode()), seed]).standard_normal(out[name].shape)
        drawn = base * np.exp(spread * noise) if base else spread * noise
        out[name] = jnp.asarray(drawn.astype(out[name].dtype))
    for name, factor in factors.items():
        out[name] = (out[name] * factor).astype(out[name].dtype)
    return out
```

```python
from contextlib import ExitStack

import concourse.bass as bass
import concourse.mybir as mybir
import numpy as np

F32 = mybir.dt.float32
F32R = mybir.dt.float32r
U32 = mybir.dt.uint32
ALU = mybir.AluOpType
ACT = mybir.ActivationFunctionType
AX = mybir.AxisListType.X

P = 128
D = 1024
T = 512
KT = D // P
TT = T // P
HD = 64
HP = 4
C = 64
NCH = T // C
NRW = 14
NQK = 8
NV = 4
NWIN = NRW + NQK + NV
PH = 8
TOPK = 16
NKEY = 128
NCAND = 64
RAW = 6
SPL = 3
KAPPA = float(np.exp(-0.5))
RMS_EPS = 1e-6
GN_EPS = 64e-5
LOWEST = -3.0e38
SW = 64
NSW = T // SW
EG = 2
NG = NKEY // EG

CONST_COLS = {}


def build_constants():
    parts = []
    at = 0

    def put(name, a):
        nonlocal at
        a = np.asarray(a, np.float32)
        CONST_COLS[name] = (at, at + a.shape[1])
        at += a.shape[1]
        parts.append(a)

    r = np.arange(P)
    put("ident", np.eye(P))
    swap = (r // HD) * HD + (r % HD + HD // 2) % HD
    perm = np.zeros((P, P))
    perm[swap, r] = 1.0
    put("perm", perm)
    put("block_ones", (r[:, None] // HD == r[None, :] // HD))
    put("ones", np.ones((P, P)))
    put("iota", np.tile(np.arange(P), (P, 1)))
    inv_freq = np.float32(10000.0) ** (-np.arange(0, HD, 2, dtype=np.float32) / np.float32(HD))
    ang = np.arange(T, dtype=np.float32)[None, :] * inv_freq[r % (HD // 2)][:, None]
    put("cos", np.cos(ang))
    put("sin", np.sin(ang) * np.where(r % HD < HD // 2, -1.0, 1.0)[:, None])
    cols = []
    for delta in range(TT - 1, -1, -1):
        dist = delta * P + r[:, None] - r[None, :]
        n = ((dist >= 0) & (dist <= 128)).astype(int)
        n += (dist >= 0) & (dist % 4 == 0)
        n += (dist >= 0) & (dist % 16 == 0)
        cols.append(np.where(n > 0, np.log(np.maximum(n, 1)), -1e30))
    put("attn_bias", np.concatenate(cols, axis=1))
    put("keep", np.tile((np.arange(T) % C != 0), (P, 1)))
    s, t = r[:, None] % C, np.arange(C)[None, :]
    put("strict", s < t)
    put("inclusive", s <= t)
    put("eye_compact", s == t)
    for level in range(6):
        m = 1 << level
        put(f"level{level}", (s // (2 * m) == t // (2 * m)) & (s // m < t // m))
    starts = [16, 24, 32, 40, 44, 48, 52] + list(range(56, 64))
    put("row_starts", np.tile(starts, (P, 1)))
    return np.concatenate(parts, axis=1)


build_constants()
NCONST = max(b for _, b in CONST_COLS.values())
PARAM_COLS = {}
_at = 0
for _name, _n in (("g_mix", KT), ("mu", NRW), ("w0", HP), ("a0", HP), ("k_k", HP), ("k_a", HP), ("r_k", HP),
                  ("gn_w", HP), ("gn_b", HP), ("g_ffn", KT)):
    PARAM_COLS[_name] = (_at, _at + _n)
    _at += _n
NPARAM = _at


class Steps:

    def __init__(self, eng, own, counts):
        self.eng, self.own, self.counts, self.last = eng, own, counts, None

    def do(self, ins, signal=None):
        sem = self.own if signal is None else signal
        ins.then_inc(sem, 1)
        self.counts[sem.name] = self.counts.get(sem.name, 0) + 1
        self.last = (sem, self.counts[sem.name])

    def settle(self):
        self.eng.wait_ge(*self.last)


class Shared:
    pass


def bc(ap, axis, n):
    ap = ap.unsqueeze(axis)
    shape = list(ap.shape)
    shape[axis] = n
    return ap.to_broadcast(shape)


def three_pass(nc, out, w_hi, w_lo, m_hi, m_lo, first, last):
    nc.tensor.matmul(out, w_hi, m_hi, start=first, stop=False)
    nc.tensor.matmul(out, w_hi, m_lo, start=False, stop=False)
    return nc.tensor.matmul(out, w_lo, m_hi, start=False, stop=last)


def project(nc, S, dram):
    sem = S.sem
    with ExitStack() as ctx:
        def sb(name, shape, dt=F32):
            return ctx.enter_context(nc.sbuf_tensor(name, shape, dt))

        xt = sb("x_t", [P, KT, T])
        sq = S.zm[:, 0:KT, :]
        rstd = sb("x_rstd", [P, T])
        xn_hi = sb("xn_hi", [P, KT, T], F32R)
        xn_lo = sb("xn_lo", [P, KT, T], F32R)
        raw = sb("win_raw", [P, RAW, D])
        w_hi = sb("win_hi", [P, SPL, D], F32R)
        w_lo = sb("win_lo", [P, SPL, D], F32R)
        zb = sb("z_shift", [P, 2, T + 1])
        zd = sb("z_delta", [P, 2, T])

        s_const = sem("p_const")
        s_x = [sem(f"p_x{q}") for q in range(4)]
        s_raw = [sem(f"p_raw{i}") for i in range(RAW)]
        s_sq, s_ms, s_mean, s_rstd = sem("p_sq"), sem("p_ms"), sem("p_mean"), sem("p_rstd")
        s_xn, s_xhi, s_xlo = sem("p_xn"), sem("p_xhi"), sem("p_xlo")
        s_hi, s_lo, s_mm, s_out, s_zero, s_shift = (sem("p_hi"), sem("p_lo"), sem("p_mm"), sem("p_out"),
                                                    sem("p_zero"), sem("p_shift"))
        block = ctx.enter_context(nc.Block())

        @block.sync
        def _(sp):
            for q in range(4):
                sp.dma_start(xt[:, 2 * q:2 * q + 2, :], dram["x_t"][:, 2 * q:2 * q + 2, :]).then_inc(s_x[q], 16)
            for n in range(NWIN):
                if n >= RAW:
                    sp.wait_ge(s_lo, n - RAW + 1)
                sp.dma_start(raw[:, n % RAW, :], dram["win_t"][n]).then_inc(s_raw[n % RAW], 16)

        @block.gpsimd
        def _(pool):
            st = Steps(pool, S.own_pool, S.counts)
            st.do(pool.memset(zb[:, :, 0:1], 0.0), s_zero)

        @block.scalar
        def _(act):
            st = Steps(act, S.own_act, S.counts)
            act.dma_start(S.consts[:, :], dram["consts"]).then_inc(s_const, 16)
            act.dma_start(S.params[:, :], dram["params"]).then_inc(s_const, 16)
            act.dma_start(S.up[:, :, :], dram["up"]).then_inc(s_const, 16)
            act.dma_start(S.g_final[:, :], dram["g_final"]).then_inc(s_const, 16)
            for k in range(KT):
                if k % 2 == 0:
                    act.wait_ge(s_x[k // 2], 16)
                st.do(act.activation(sq[:, k, :], xt[:, k, :], ACT.Square), s_sq)
            act.wait_ge(s_mean, 2)
            st.do(act.activation(rstd[:, :], rstd[:, :], ACT.Sqrt), s_rstd)
            for k in range(KT):
                act.wait_ge(s_xn, k + 1)
                st.do(act.activation(xn_hi[:, k, :], xt[:, k, :], ACT.Copy), s_xhi)

            def take(n):
                act.wait_ge(s_mm, n + 1)
                if n < NRW:
                    if n == 0:
                        act.wait_ge(s_zero, 1)
                    if n >= 2:
                        act.wait_ge(s_shift, n - 1)
                    st.do(act.activation(zb[:, n % 2, 1:T + 1], S.ps[:, n % 3, :], ACT.Copy), s_out)
                else:
                    st.do(act.activation(S.qk[:, n - NRW, :], S.ps[:, n % 3, :], ACT.Copy), s_out)

            for n in range(NWIN):
                act.wait_ge(s_raw[n % RAW], 16 * (n // RAW + 1))
                if n >= SPL:
                    act.wait_ge(s_mm, n - SPL + 1)
                st.do(act.activation(w_hi[:, n % SPL, :], raw[:, n % RAW, :], ACT.Copy), s_hi)
                if 1 <= n <= NRW + NQK:
                    take(n - 1)
            act.wait_ge(s_mm, NWIN)
            for t in range(TT):
                st.do(act.activation(S.v_tok[:, t, :], S.ps[:, 4 + t, :], ACT.Copy), s_out)

        @block.vector
        def _(dve):
            st = Steps(dve, S.own_dve, S.counts)
            v = nc.vector
            dve.wait_ge(s_ms, 1)
            st.do(v.tensor_scalar(rstd[:, :], S.ps[:, 3, :], 1.0 / D, RMS_EPS, ALU.mult, ALU.add), s_mean)
            st.settle()
            st.do(v.reciprocal(rstd[:, :], rstd[:, :]), s_mean)
            dve.wait_ge(s_const, 64)
            dve.wait_ge(s_rstd, 1)
            for k in range(KT):
                st.do(v.scalar_tensor_tensor(xt[:, k, :], xt[:, k, :], S.param("g_mix", k), rstd[:, :],
                                             ALU.mult, ALU.mult), s_xn)
            for k in range(KT):
                dve.wait_ge(s_xhi, k + 1)
                st.do(v.tensor_tensor(xn_lo[:, k, :], xt[:, k, :], xn_hi[:, k, :].bitcast(F32), ALU.subtract), s_xlo)

            def shift(n):
                dve.wait_ge(s_out, n + 1)
                st.do(v.tensor_tensor(zd[:, n % 2, :], zb[:, n % 2, 0:T], zb[:, n % 2, 1:T + 1], ALU.subtract))
                st.settle()
                st.do(v.scalar_tensor_tensor(S.zm[:, n, :], zd[:, n % 2, :], S.param("mu", n), zb[:, n % 2, 1:T + 1],
                                             ALU.mult, ALU.add), s_shift)

            for n in range(NWIN):
                dve.wait_ge(s_hi, n + 1)
                st.do(v.tensor_tensor(w_lo[:, n % SPL, :], raw[:, n % RAW, :], w_hi[:, n % SPL, :].bitcast(F32),
                                      ALU.subtract), s_lo)
                if 1 <= n <= NRW:
                    shift(n - 1)

        @block.tensor
        def _(pe):
            pe.wait_ge(s_const, 64)
            for k in range(KT):
                pe.wait_ge(s_sq, k + 1)
                last = nc.tensor.matmul(S.ps[:, 3, :], S.const("ones"), sq[:, k, :], start=k == 0, stop=k == KT - 1)
            last.then_inc(s_ms, 1)
            pe.wait_ge(s_xlo, KT)
            for n in range(NWIN):
                pe.wait_ge(s_lo, n + 1)
                if n < NRW + NQK:
                    if n >= 3:
                        pe.wait_ge(s_out, n - 2)
                    for k in range(KT):
                        w = slice(k * P, (k + 1) * P)
                        last = three_pass(nc, S.ps[:, n % 3, :], w_hi[:, n % SPL, w], w_lo[:, n % SPL, w],
                                          xn_hi[:, k, :], xn_lo[:, k, :], k == 0, k == KT - 1)
                else:
                    kk = n - NRW - NQK
                    for t in range(TT):
                        x = slice(t * P, (t + 1) * P)
                        for j in range(2):
                            k, w = 2 * kk + j, slice(j * T, (j + 1) * T)
                            last = three_pass(nc, S.ps[:, 4 + t, :], xn_hi[:, k, x], xn_lo[:, k, x],
                                              w_hi[:, n % SPL, w], w_lo[:, n % SPL, w], k == 0, k == KT - 1)
                last.then_inc(s_mm, 1)


def attend(nc, S, dram):
    sem = S.sem
    with ExitStack() as ctx:
        def sb(name, shape, dt=F32):
            return ctx.enter_context(nc.sbuf_tensor(name, shape, dt))

        tmp = sb("rope_tmp", [P, 2, T])
        sm = sb("scores", [P, 2, T])
        pt = sb("probs_t", [P, 2, TT, T])
        mx = sb("row_max", [P, 32])
        nmx = sb("neg_max", [P, 32])
        den = sb("row_sum", [P, 32])
        rden = sb("row_inv", [P, 32])
        s_perm, s_sin, s_rope = sem("a_perm"), sem("a_sin"), sem("a_rope")
        s_sc, s_bias, s_neg, s_exp, s_prob = sem("a_sc"), sem("a_bias"), sem("a_neg"), sem("a_exp"), sem("a_prob")
        s_tr, s_pt, s_pv, s_mix = sem("a_tr"), sem("a_pt"), sem("a_pv"), sem("a_mix")
        NU = 8 * TT
        block = ctx.enter_context(nc.Block())

        @block.tensor
        def _(pe):
            for n in range(NQK):
                if n >= 2:
                    pe.wait_ge(s_sin, n - 1)
                nc.tensor.matmul(S.ps[:, n % 2, :], S.const("perm"), S.qk[:, n, :], start=True,
                                 stop=True).then_inc(s_perm, 1)
            pe.wait_ge(s_rope, NQK)

            def scores(u):
                h, t = divmod(u, TT)
                rows = slice(HD * (h % 2), HD * (h % 2) + HD)
                if u >= 2:
                    pe.wait_ge(s_bias, u - 1)
                nc.tensor.matmul(S.ps[:, u % 2, 0:(t + 1) * P], S.qk[rows, h // 2, t * P:(t + 1) * P],
                                 S.qk[rows, 4 + h // 2, 0:(t + 1) * P], start=True, stop=True).then_inc(s_sc, 1)

            def turn(u):
                t = u % TT
                pe.wait_ge(s_prob, u + 1)
                if u >= 2:
                    pe.wait_ge(s_pt, u - 1)
                for j in range(t + 1):
                    last = nc.tensor.transpose(S.ps[:, 2 + u % 2, j * P:(j + 1) * P], sm[:, u % 2, j * P:(j + 1) * P],
                                               S.const("ident"))
                last.then_inc(s_tr, 1)

            def values(h):
                pe.wait_ge(s_pt, TT * (h + 1))
                if h >= 4 and h % 2 == 0:
                    pe.wait_ge(s_mix, h // 2 - 1)
                for j in range(TT):
                    last = nc.tensor.matmul(S.ps[HD * (h % 2):HD * (h % 2) + HD, 4 + (h // 2) % 2, j * P:T],
                                            S.v_tok[:, j, h * HD:(h + 1) * HD], pt[:, h % 2, j, j * P:T],
                                            start=j == 0, stop=j == TT - 1)
                last.then_inc(s_pv, 1)

            scores(0)
            for u in range(NU):
                if u + 1 < NU:
                    scores(u + 1)
                turn(u)
                if u % TT == 1 and u > TT:
                    values(u // TT - 1)
            values(7)

        @block.scalar
        def _(act):
            st = Steps(act, S.own_act, S.counts)

            def take(u):
                h, t = divmod(u, TT)
                act.wait_ge(s_tr, u + 1)
                if h >= 2:
                    act.wait_ge(s_pv, h - 1)
                st.do(act.activation(pt[:, h % 2, 0:t + 1, t * P:(t + 1) * P],
                                     S.ps[:, 2 + u % 2, 0:(t + 1) * P].rearrange("p (j q) -> p j q", q=P), ACT.Copy),
                      s_pt)

            def pair(p):
                act.wait_ge(s_pv, 2 * p + 2)
                st.do(act.activation(S.mixed[:, HP + p, :], S.ps[:, 4 + p % 2, :], ACT.Copy), s_mix)

            for u in range(NU):
                t = u % TT
                act.wait_ge(s_neg, u + 1)
                st.do(act.activation(sm[:, u % 2, 0:(t + 1) * P], sm[:, u % 2, 0:(t + 1) * P], ACT.Exp,
                                     bias=nmx[:, u:u + 1], accum_out=den[:, u:u + 1]), s_exp)
                if u >= 1:
                    take(u - 1)
                if u > 2 * TT and u % (2 * TT) == 2:
                    pair(u // (2 * TT) - 1)
            take(NU - 1)
            pair(HP - 1)

        @block.vector
        def _(dve):
            st = Steps(dve, S.own_dve, S.counts)
            v = nc.vector
            for n in range(NQK):
                dve.wait_ge(s_perm, n + 1)
                st.do(v.tensor_tensor(tmp[:, n % 2, :], S.ps[:, n % 2, :], S.const("sin"), ALU.mult), s_sin)
                st.do(v.tensor_tensor(S.qk[:, n, :], S.qk[:, n, :], S.const("cos"), ALU.mult))
                st.settle()
                st.do(v.tensor_tensor(S.qk[:, n, :], S.qk[:, n, :], tmp[:, n % 2, :], ALU.add), s_rope)

            def bias(u):
                t = u % TT
                dve.wait_ge(s_sc, u + 1)
                if u >= 2:
                    dve.wait_ge(s_tr, u - 1)
                st.do(v.scalar_tensor_tensor(sm[:, u % 2, 0:(t + 1) * P], S.ps[:, u % 2, 0:(t + 1) * P], HD ** -0.5,
                                             S.const("attn_bias")[:, (TT - 1 - t) * P:], ALU.mult, ALU.add), s_bias)
                st.settle()
                st.do(v.tensor_reduce(mx[:, u:u + 1], sm[:, u % 2, 0:(t + 1) * P], AX, ALU.max))
                st.settle()
                st.do(v.tensor_scalar(nmx[:, u:u + 1], mx[:, u:u + 1], -1.0, None, ALU.mult), s_neg)

            def normalise(u):
                t = u % TT
                dve.wait_ge(s_exp, u + 1)
                st.do(v.reciprocal(rden[:, u:u + 1], den[:, u:u + 1]))
                st.settle()
                st.do(v.tensor_scalar(sm[:, u % 2, 0:(t + 1) * P], sm[:, u % 2, 0:(t + 1) * P], rden[:, u:u + 1],
                                      None, ALU.mult), s_prob)

            bias(0)
            for u in range(NU):
                if u + 1 < NU:
                    bias(u + 1)
                normalise(u)


def prepare(nc, S, dram):
    sem = S.sem
    with ExitStack() as ctx:
        def sb(name, shape, dt=F32):
            return ctx.enter_context(nc.sbuf_tensor(name, shape, dt))

        kk = sb("kk", [P, HP, T])
        nrm = sb("kk_norm", [P, HP, T])
        sw = sb("decay_rate", [P, HP, T])
        icl = sb("iclr", [P, HP, T])
        cum = sb("decay_sum", [P, HP, T])
        prev = sb("decay_prev", [P, HP, T])
        omka = sb("one_minus_k_a", [P, HP])
        R, K, V, WA, G = S.zm[:, 0:4, :], S.zm[:, 4:8, :], S.zm[:, 8:12, :], S.zm[:, 12, :], S.zm[:, 13, :]
        s_tanh, s_gsig, s_up, s_act, s_gate = sem("r_tanh"), sem("r_gsig"), sem("r_up"), sem("r_act"), sem("r_gate")
        s_ksq, s_ssum, s_nrm, s_cum, s_prev = sem("r_ksq"), sem("r_ssum"), sem("r_nrm"), sem("r_cum"), sem("r_prev")
        s_exp, s_rk, s_rsum, s_vtr, s_vt = sem("r_exp"), sem("r_rk"), sem("r_rsum"), sem("r_vtr"), sem("r_vt")
        s_pd = sem("r_pd")
        block = ctx.enter_context(nc.Block())

        @block.tensor
        def _(pe):
            for j in range(HP):
                for q in range(TT):
                    last = nc.tensor.transpose(S.ps[:, 4 + j, q * P:(q + 1) * P], V[:, j, q * P:(q + 1) * P],
                                               S.const("ident"))
                last.then_inc(s_vtr, 1)
            pe.wait_ge(s_tanh, 1)
            pe.wait_ge(s_gsig, 1)
            for j in range(HP):
                c = slice(j * P, (j + 1) * P)
                if j >= 1:
                    pe.wait_ge(s_act, 3 * j)
                nc.tensor.matmul(S.ps[:, 0, :], S.up[0:HD, 0, c], WA[0:HD, :], start=True, stop=True).then_inc(s_up, 1)
                nc.tensor.matmul(S.ps[:, 1, :], S.up[HD:P, 0, c], WA[HD:P, :], start=True, stop=True).then_inc(s_up, 1)
                nc.tensor.matmul(S.ps[:, 2, :], S.up[:, 1, c], G, start=True, stop=True).then_inc(s_up, 1)
            pe.wait_ge(s_ksq, 1)
            pe.wait_ge(s_vt, 4 * HP)
            for j in range(HP):
                nc.tensor.matmul(S.ps[:, 4 + j, :], S.const("block_ones"), nrm[:, j, :], start=True,
                                 stop=True).then_inc(s_ssum, 1)
            for j in range(HP):
                pe.wait_ge(s_rk, j + 1)
                pe.wait_ge(s_nrm, j + 1)
                nc.tensor.matmul(S.ps[:, 4 + j, :], S.const("block_ones"), cum[:, j, :], start=True,
                                 stop=True).then_inc(s_rsum, 1)

        @block.scalar
        def _(act):
            st = Steps(act, S.own_act, S.counts)
            st.do(act.activation(WA[0:HD, :], WA[0:HD, :], ACT.Tanh), s_tanh)
            st.do(act.activation(G, G, ACT.Sigmoid), s_gsig)
            for j in range(HP):
                act.wait_ge(s_up, 3 * j + 1)
                st.do(act.activation(sw[:, j, :], S.ps[:, 0, :], ACT.Sigmoid, bias=S.param("w0", j)), s_act)
                act.wait_ge(s_up, 3 * j + 2)
                st.do(act.activation(icl[:, j, :], S.ps[:, 1, :], ACT.Sigmoid, bias=S.param("a0", j)), s_act)
                act.wait_ge(s_up, 3 * j + 3)
                st.do(act.activation(S.gate[:, j, :], S.ps[:, 2, :], ACT.Copy), s_act)
            for j in range(HP):
                act.wait_ge(s_ssum, j + 1)
                if j == 0:
                    act.wait_ge(s_ssum, HP)
                st.do(act.activation(nrm[:, j, :], S.ps[:, 4 + j, :], ACT.Sqrt), s_nrm)
            act.wait_ge(s_cum, HP)
            act.wait_ge(s_prev, 1)
            st.do(act.activation(sw[:, :, :], cum[:, :, :], ACT.Exp, scale=-KAPPA), s_exp)
            st.do(act.activation(prev[:, :, :], prev[:, :, :], ACT.Exp, scale=-KAPPA), s_exp)
            st.do(act.activation(cum[:, :, :], cum[:, :, :], ACT.Exp, scale=KAPPA), s_exp)

        @block.gpsimd
        def _(pool):
            st = Steps(pool, S.own_pool, S.counts)
            st.do(pool.tensor_scalar(omka[:, :], S.param_all("k_a"), -1.0, 1.0, ALU.mult, ALU.add), s_pd)

        @block.vector
        def _(dve):
            st = Steps(dve, S.own_dve, S.counts)
            v = nc.vector
            for j in range(HP):
                st.do(v.tensor_scalar(kk[:, j, :], K[:, j, :], S.param("k_k", j), None, ALU.mult))
            st.settle()
            st.do(v.tensor_tensor(nrm[:, :, :], kk[:, :, :], kk[:, :, :], ALU.mult), s_ksq)
            for j in range(HP):
                dve.wait_ge(s_vtr, j + 1)
                turned = S.ps[:, 4 + j, :].rearrange("p (q c) -> p q c", c=P)
                for cp in range(2):
                    for hd in range(2):
                        st.do(v.tensor_copy(S.v_chunk[hd * C:(hd + 1) * C, :, j, :].rearrange(
                            "p (q e) i -> p q e i", e=2)[:, :, cp, :],
                            turned[cp * C:(cp + 1) * C, :, hd * HD:(hd + 1) * HD]), s_vt)
            dve.wait_ge(s_act, 3 * HP)
            for j in range(HP):
                st.do(v.tensor_tensor_scan(cum[:, j, :], S.const("keep"), sw[:, j, :], 0.0, ALU.mult, ALU.add), s_cum)
            st.settle()
            st.do(v.tensor_tensor(prev[:, :, :], cum[:, :, :], sw[:, :, :], ALU.subtract), s_prev)
            dve.wait_ge(s_nrm, HP)
            st.do(v.tensor_scalar(nrm[:, :, :], nrm[:, :, :], 1e-12, None, ALU.max))
            st.settle()
            st.do(v.reciprocal(nrm[:, :, :], nrm[:, :, :]))
            st.settle()
            st.do(v.tensor_tensor(kk[:, :, :], kk[:, :, :], nrm[:, :, :], ALU.mult))
            st.settle()
            dve.wait_ge(s_pd, 1)
            for j in range(HP):
                st.do(v.tensor_scalar(nrm[:, j, :], icl[:, j, :], S.param("k_a", j), omka[:, j:j + 1],
                                      ALU.mult, ALU.add))
            st.settle()
            st.do(v.tensor_tensor(K, K, nrm[:, :, :], ALU.mult))
            st.do(v.tensor_tensor(icl[:, :, :], icl[:, :, :], kk[:, :, :], ALU.mult))
            st.settle()
            dve.wait_ge(s_exp, 3)
            ra = S.ra[:, :, :, :, :]
            st.do(v.scalar_tensor_tensor(ra[:, :, :, 0, :].rearrange("p j n t -> p (j n) t"),
                                         kk[:, :, :].rearrange("p j (n t) -> p (j n) t", t=C), -1.0,
                                         prev[:, :, :].rearrange("p j (n t) -> p (j n) t", t=C), ALU.mult, ALU.mult))
            st.do(v.tensor_tensor(ra[:, :, :, 1, :].rearrange("p j n t -> p (j n) t"),
                                  R.rearrange("p j (n t) -> p (j n) t", t=C),
                                  sw[:, :, :].rearrange("p j (n t) -> p (j n) t", t=C), ALU.mult))
            st.do(v.tensor_tensor(S.bs[:, :, :], icl[:, :, :], cum[:, :, :], ALU.mult))
            st.do(v.tensor_tensor(S.ks[:, :, :], K, cum[:, :, :], ALU.mult))
            st.do(v.tensor_copy(S.pc[:, :, :], sw[:, :, :].rearrange("p j (n t) -> p j n t", t=C)[:, :, :, C - 1]))
            st.settle()
            for j in range(HP):
                st.do(v.scalar_tensor_tensor(cum[:, j, :], R[:, j, :], S.param("r_k", j), K[:, j, :],
                                             ALU.mult, ALU.mult), s_rk)
            for j in range(HP):
                dve.wait_ge(s_rsum, j + 1)
                st.do(v.tensor_tensor(R[:, j, :], S.ps[:, 4 + j, :], V[:, j, :], ALU.mult), s_gate)


def scan(nc, S, dram):
    sem = S.sem
    with ExitStack() as ctx:
        def sb(name, shape, dt=F32):
            return ctx.enter_context(nc.sbuf_tensor(name, shape, dt))

        HC = NCH // 2
        NB = HC // 2
        bbd = sb("b_bd", [P, HC, HP, P])
        kbd = sb("k_bd", [P, HC, HP, P])
        abd = sb("a_bd", [P, HC, HP, P])
        rbd = sb("r_bd", [P, HC, HP, P])
        aktbd = sb("akt_bd", [P, HC, HP, P])
        rbtbd = sb("rbt_bd", [P, HC, HP, P])
        rktbd = sb("rkt_bd", [P, HC, HP, P])
        btbd = sb("bt_bd", [P, HC, HP, P])
        ktbd = sb("kt_bd", [P, HC, HP, P])
        lt = sb("l_t", [P, HC, HP, C])
        lbd = sb("l_bd", [P, HC, HP, P])
        tc = sb("t_c", [P, HC, HP, C])
        ttc = sb("tt_c", [P, HC, HP, C])
        xc = S.zm[:, 8:10, :].rearrange("p a (c j t) -> p (a c) j t", c=2, j=HP)
        st_s = S.zm[:, 10, :].rearrange("p (w j i) -> p w j i", w=2, j=HP)
        o1 = S.zm[:, 11, 0:HP * HD].rearrange("p (j i) -> p j i", j=HP)
        us = S.zm[:, 11, HP * HD:].rearrange("p (j i) -> p j i", j=HP)
        s_zero, s_bd, s_g, s_gev, s_tr, s_trev = (sem("s_zero"), sem("s_bd"), sem("s_g"), sem("s_gev"),
                                                  sem("s_tr"), sem("s_trev"))
        s_lbd, s_x, s_xbd, s_xc, s_y, s_tup, s_ttbd = (sem("s_lbd"), sem("s_x"), sem("s_xbd"), sem("s_xc"),
                                                       sem("s_y"), sem("s_tup"), sem("s_ttbd"))
        s_o1, s_o1c, s_u, s_uc, s_s, s_snew, s_yo, s_yc = (sem("s_o1"), sem("s_o1c"), sem("s_u"), sem("s_uc"),
                                                           sem("s_s"), sem("s_snew"), sem("s_yo"), sem("s_yc"))
        NL = 6
        par = [slice(0, C), slice(C, P)]
        block = ctx.enter_context(nc.Block())
        yb = S.y_chunk

        def compact(bank, n):
            return S.ps[:, bank, 0:n * HP * C].rearrange("p (c j t) -> p c j t", c=n, j=HP)

        @block.gpsimd
        def _(pool):
            st = Steps(pool, S.own_pool, S.counts)
            for buf in (bbd, kbd, abd, rbd, aktbd, rbtbd, rktbd, lbd):
                st.do(pool.memset(buf[:, :, :, :], 0.0), s_zero)
            st.do(pool.memset(st_s[:, 0, :, :], 0.0), s_zero)
            st.settle()
            for half in range(2):
                chunks = slice(half * HC, (half + 1) * HC)
                if half:
                    pool.wait_ge(s_yo, HC)
                for dst, src in ((bbd, S.bs), (kbd, S.ks)):
                    for e in range(2):
                        st.do(pool.tensor_copy(dst[par[e], :, :, par[e]],
                                               src[par[e], :, half * HC * C:(half + 1) * HC * C].rearrange(
                                                   "p j (c t) -> p c j t", t=C)), s_bd)
                for w, dst in ((0, abd), (1, rbd)):
                    for e in range(2):
                        st.do(pool.tensor_copy(dst[par[e], :, :, par[e]],
                                               S.ra[par[e], :, chunks, w, :].rearrange("p j c t -> p c j t")), s_bd)
                for level in range(NL):
                    n = half * NL + level
                    if level == 0:
                        pool.wait_ge(s_gev, 14 * (half * NB + NB))
                    else:
                        pool.wait_ge(s_x, NB * n)
                    for e in range(2):
                        st.do(pool.tensor_tensor(
                            lbd[par[e], :, :, par[e]].rearrange("p c j t -> p (c j) t"),
                            lt[par[e], :, :, :].rearrange("p c j t -> p (c j) t"),
                            bc(S.const(f"level{level}")[par[e], :], 1, HC * HP), ALU.mult), s_lbd)
                    for b in range(NB):
                        cs = slice(2 * b, 2 * b + 2)
                        pool.wait_ge(s_tup, NB * n + b + 1)
                        for e in range(2):
                            st.do(pool.tensor_copy(kbd[par[e], cs, :, par[e]], ttc[par[e], cs, :, :]), s_ttbd)

        @block.tensor
        def _(pe):
            for half in range(2):
                pe.wait_ge(s_bd, 8 * (half + 1))
                if half:
                    pe.wait_ge(s_yc, HC)
                    pe.wait_ge(s_snew, 2 * HC)
                for c in range(HC):
                    ch = half * HC + c
                    if ch >= 2:
                        pe.wait_ge(s_gev, 7 * (ch - 1))
                    for j in range(HP):
                        nc.tensor.matmul(S.ps[:, c % 2, j * P:(j + 1) * P], bbd[:, c, j, :],
                                         S.ra[:, j, ch, :, :].rearrange("p w t -> p (w t)"), start=True, stop=True)
                    for j in range(HP):
                        last = nc.tensor.matmul(S.ps[:, 2 + c % 2, j * P:(j + 1) * P], kbd[:, c, j, :],
                                                S.ra[:, j, ch, :, :].rearrange("p w t -> p (w t)"),
                                                start=True, stop=True)
                    last.then_inc(s_g, 1)
                    if ch >= 1:
                        pe.wait_ge(s_trev, 2 * ch)
                    for j in range(HP):
                        nc.tensor.transpose(S.ps[:, 4, j * P:(j + 1) * P], bbd[:, c, j, :], S.const("ident"))
                    for j in range(HP):
                        last = nc.tensor.transpose(S.ps[:, 5, j * P:(j + 1) * P], kbd[:, c, j, :], S.const("ident"))
                    last.then_inc(s_tr, 1)
                pe.wait_ge(s_gev, 7 * HC * (half + 1))
                pe.wait_ge(s_trev, 2 * HC * (half + 1))
                for level in range(NL):
                    n = half * NL + level
                    pe.wait_ge(s_lbd, 2 * (n + 1))
                    for b in range(NB):
                        if level:
                            pe.wait_ge(s_tup, NB * (n - 1) + b + 1)
                        for c in (2 * b, 2 * b + 1):
                            for j in range(HP):
                                rhs = tc[:, c, j, :] if level else S.const("eye_compact")
                                last = nc.tensor.matmul(compact(b, 2)[:, c % 2, j, :], lbd[:, c, j, :], rhs,
                                                        start=True, stop=True)
                        last.then_inc(s_x, 1)
                    if level == 0:
                        continue
                    for b in range(NB):
                        pe.wait_ge(s_xbd, 2 * (NB * (half * (NL - 1) + level - 1) + b + 1))
                        pe.wait_ge(s_xc, NB * n + b + 1)
                        pe.wait_ge(s_ttbd, 2 * (NB * (n - 1) + b + 1))
                        for c in (2 * b, 2 * b + 1):
                            for j in range(HP):
                                if level < NL - 1:
                                    nc.tensor.matmul(compact(2 + b, 2)[:, c % 2, j, :], kbd[:, c, j, :],
                                                     xc[:, c, j, :], start=True, stop=True)
                                last = nc.tensor.matmul(compact(4 + b, 2)[:, c % 2, j, :], bbd[:, c, j, :],
                                                        ttc[:, c, j, :], start=True, stop=True)
                        last.then_inc(s_y, 1)
                pe.wait_ge(s_ttbd, 2 * NB * NL * (half + 1))
                for c in range(HC):
                    ch = half * HC + c
                    for j in range(HP):
                        o = S.ps[:, 0, j * HD:(j + 1) * HD]
                        nc.tensor.matmul(o, aktbd[:, c, j, :], S.v_chunk[:, ch, j, :], start=True, stop=False)
                        if j == 0 and ch:
                            pe.wait_ge(s_snew, 2 * ch)
                        last = nc.tensor.matmul(o, abd[:, c, j, :], st_s[:, ch % 2, j, :], start=False, stop=True)
                    last.then_inc(s_o1, 1)
                    pe.wait_ge(s_o1c, ch + 1)
                    for j in range(HP):
                        last = nc.tensor.matmul(S.ps[:, 1, j * HD:(j + 1) * HD], kbd[:, c, j, :], o1[:, j, :],
                                                start=True, stop=True)
                    last.then_inc(s_u, 1)
                    pe.wait_ge(s_uc, ch + 1)
                    for j in range(HP):
                        o = S.ps[:, 4, j * HD:(j + 1) * HD]
                        nc.tensor.matmul(o, ktbd[:, c, j, :], S.v_chunk[:, ch, j, :], start=True, stop=False)
                        last = nc.tensor.matmul(o, btbd[:, c, j, :], us[:, j, :], start=False, stop=True)
                    last.then_inc(s_s, 1)
                    if ch >= 2:
                        pe.wait_ge(s_yc, ch - 1)
                    for j in range(HP):
                        o = S.ps[:, 2 + ch % 2, j * HD:(j + 1) * HD]
                        nc.tensor.matmul(o, rbd[:, c, j, :], st_s[:, ch % 2, j, :], start=True, stop=False)
                        nc.tensor.matmul(o, rktbd[:, c, j, :], S.v_chunk[:, ch, j, :], start=False, stop=False)
                        last = nc.tensor.matmul(o, rbtbd[:, c, j, :], us[:, j, :], start=False, stop=True)
                    last.then_inc(s_yo, 1)

        @block.scalar
        def _(act):
            st = Steps(act, S.own_act, S.counts)
            for half in range(2):
                for c in range(HC):
                    ch = half * HC + c
                    act.wait_ge(s_tr, ch + 1)
                    for dst, bank in ((btbd, 4), (ktbd, 5)):
                        st.do(act.activation(dst[:, c, :, :].rearrange("p j t -> p (j t)"), S.ps[:, bank, :],
                                             ACT.Copy), s_trev)
                for level in range(1, NL):
                    n = half * NL + level
                    for b in range(NB):
                        cs = slice(2 * b, 2 * b + 2)
                        act.wait_ge(s_xc, NB * n + b + 1)
                        for e in range(2):
                            st.do(act.activation(bbd[par[e], cs, :, par[e]], xc[par[e], cs, :, :], ACT.Copy), s_xbd)
                for c in range(HC):
                    ch = half * HC + c
                    act.wait_ge(s_yo, ch + 1)
                    st.do(act.activation(yb[:, ch, :, :].rearrange("p j t -> p (j t)"),
                                         S.ps[:, 2 + ch % 2, 0:HP * HD], ACT.Copy), s_yc)

        @block.vector
        def _(dve):
            st = Steps(dve, S.own_dve, S.counts)
            v = nc.vector
            dve.wait_ge(s_zero, 9)
            for half in range(2):
                for c in range(HC):
                    ch = half * HC + c
                    dve.wait_ge(s_g, ch + 1)
                    g1 = S.ps[:, c % 2, :].rearrange("p (j w t) -> p j w t", j=HP, w=2)
                    g2 = S.ps[:, 2 + c % 2, :].rearrange("p (j w t) -> p j w t", j=HP, w=2)
                    st.do(v.tensor_tensor(lt[:, c, :, :], g1[:, :, 0, :], bc(S.const("strict"), 1, HP), ALU.mult),
                          s_gev)
                    for dst, src, w, m in ((rbtbd, g1, 1, "inclusive"), (aktbd, g2, 0, "strict"),
                                           (rktbd, g2, 1, "inclusive")):
                        for e in range(2):
                            st.do(v.tensor_tensor(dst[par[e], c, :, par[e]], src[par[e], :, w, :],
                                                  bc(S.const(m)[par[e], :], 1, HP), ALU.mult), s_gev)
                eye = bc(S.const("eye_compact"), 1, 2 * HP)
                for level in range(NL):
                    n = half * NL + level
                    ny = half * (NL - 1) + level
                    for b in range(NB):
                        cs = slice(2 * b, 2 * b + 2)
                        flat = "p c j t -> p (c j) t"
                        dve.wait_ge(s_x, NB * n + b + 1)
                        if level == 0:
                            st.do(v.tensor_tensor(tc[:, cs, :, :].rearrange(flat), compact(b, 2).rearrange(flat), eye,
                                                  ALU.add), s_xc)
                            st.do(v.tensor_tensor(ttc[:, cs, :, :].rearrange(flat), lt[:, cs, :, :].rearrange(flat),
                                                  bc(S.const("level0"), 1, 2 * HP), ALU.mult))
                            st.settle()
                            st.do(v.tensor_tensor(ttc[:, cs, :, :].rearrange(flat), ttc[:, cs, :, :].rearrange(flat),
                                                  eye, ALU.add), s_tup)
                        else:
                            st.do(v.tensor_copy(xc[:, cs, :, :], compact(b, 2)), s_xc)
                    if level == 0:
                        continue
                    for b in range(NB):
                        cs = slice(2 * b, 2 * b + 2)
                        dve.wait_ge(s_y, NB * (ny - 1) + b + 1)
                        if level < NL - 1:
                            st.do(v.tensor_tensor(tc[:, cs, :, :], tc[:, cs, :, :], compact(2 + b, 2), ALU.add))
                        dve.wait_ge(s_ttbd, 2 * (NB * (n - 1) + b + 1))
                        st.do(v.tensor_tensor(ttc[:, cs, :, :], ttc[:, cs, :, :], compact(4 + b, 2), ALU.add), s_tup)
                for c in range(HC):
                    ch = half * HC + c
                    dve.wait_ge(s_o1, ch + 1)
                    st.do(v.tensor_copy(o1[:, :, :].rearrange("p j t -> p (j t)"), S.ps[:, 0, 0:HP * HD]), s_o1c)
                    dve.wait_ge(s_u, ch + 1)
                    st.do(v.tensor_copy(us[:, :, :].rearrange("p j t -> p (j t)"), S.ps[:, 1, 0:HP * HD]), s_uc)
                    dve.wait_ge(s_s, ch + 1)
                    if ch:
                        dve.wait_ge(s_yo, ch)
                    new = st_s[:, (ch + 1) % 2, :, :]
                    st.do(v.tensor_tensor(new.rearrange("p j t -> p (j t)"),
                                          st_s[:, ch % 2, :, :].rearrange("p j t -> p (j t)"),
                                          S.ps[:, 4, 0:HP * HD], ALU.add), s_snew)
                    st.settle()
                    st.do(v.tensor_tensor(new, new, bc(S.pc[:, :, ch], 2, HD), ALU.mult), s_snew)


def normalise_heads(nc, S, dram):
    sem = S.sem
    with ExitStack() as ctx:
        def sb(name, shape, dt=F32):
            return ctx.enter_context(nc.sbuf_tensor(name, shape, dt))

        sq = sb("y_sq", [P, NCH * HP, HD])
        mean = sb("y_mean", [P, NCH * HP])
        var = sb("y_var", [P, NCH * HP])
        s_var, s_std, s_y, s_tr, s_cp = sem("n_var"), sem("n_std"), sem("n_y"), sem("n_tr"), sem("n_cp")
        block = ctx.enter_context(nc.Block())
        y = S.y_chunk[:, :, :, :].rearrange("p c j i -> p (c j) i")
        M = S.mixed

        @block.vector
        def _(dve):
            st = Steps(dve, S.own_dve, S.counts)
            v = nc.vector
            st.do(v.tensor_reduce(mean[:, :], y, AX, ALU.add))
            st.settle()
            st.do(v.tensor_scalar(mean[:, :], mean[:, :], 1.0 / HD, None, ALU.mult))
            st.settle()
            st.do(v.tensor_tensor(y, y, bc(mean[:, :], 2, HD), ALU.subtract))
            st.settle()
            st.do(v.tensor_tensor(sq[:, :, :], y, y, ALU.mult))
            st.settle()
            st.do(v.tensor_reduce(var[:, :], sq[:, :, :], AX, ALU.add))
            st.settle()
            st.do(v.tensor_scalar(var[:, :], var[:, :], 1.0 / HD, GN_EPS, ALU.mult, ALU.add))
            st.settle()
            st.do(v.reciprocal(var[:, :], var[:, :]), s_var)
            dve.wait_ge(s_std, 1)
            st.do(v.tensor_tensor(y, y, bc(var[:, :], 2, HD), ALU.mult), s_y)
            for a in range(2):
                for q in range(2):
                    dve.wait_ge(s_tr, 2 * a + q + 1)
                    src = S.ps[:, 2 * a + q, :].rearrange("p (c h t) -> p c h t", c=4, h=2)
                    for pp in range(2):
                        for h in range(2):
                            st.do(v.tensor_copy(
                                M[h * HD:(h + 1) * HD, 2 * a + pp, q * 256:(q + 1) * 256].rearrange(
                                    "p (c t) -> p c t", t=C), src[pp * HD:(pp + 1) * HD, :, h, :]))
            st.settle()
            for j in range(HP):
                st.do(v.tensor_scalar(M[:, j, :], M[:, j, :], S.param("gn_w", j), S.param("gn_b", j),
                                      ALU.mult, ALU.add))
            st.settle()
            st.do(v.tensor_tensor(M[:, 0:HP, :], M[:, 0:HP, :], S.zm[:, 0:HP, :], ALU.add))
            st.settle()
            st.do(v.tensor_tensor(M[:, 0:HP, :], M[:, 0:HP, :], S.gate[:, :, :], ALU.mult))

        @block.scalar
        def _(act):
            st = Steps(act, S.own_act, S.counts)
            act.wait_ge(s_var, 1)
            st.do(act.activation(var[:, :], var[:, :], ACT.Sqrt), s_std)

        @block.tensor
        def _(pe):
            pe.wait_ge(s_y, 1)
            for a in range(2):
                for q in range(2):
                    for c in range(4):
                        last = nc.tensor.transpose(
                            S.ps[:, 2 * a + q, c * P:(c + 1) * P],
                            S.y_chunk[:, 4 * q + c, 2 * a:2 * a + 2, :].rearrange("p j i -> p (j i)"),
                            S.const("ident"))
                    last.then_inc(s_tr, 1)


def mix(nc, S, dram):
    sem = S.sem
    with ExitStack() as ctx:
        def sb(name, shape, dt=F32):
            return ctx.enter_context(nc.sbuf_tensor(name, shape, dt))

        mx_hi = sb("mixed_hi", [P, KT, T], F32R)
        mx_lo = sb("mixed_lo", [P, KT, T], F32R)
        raw = sb("wout_raw", [P, 4, D])
        w_hi = sb("wout_hi", [P, SPL, D], F32R)
        w_lo = sb("wout_lo", [P, SPL, D], F32R)
        xs = sb("h_scaled", [P, TT, D])
        sq = sb("h_sq", [P, D])
        ss = sb("h_ss", [P, TT])
        s_x = sem("m_x")
        s_raw = [sem(f"m_raw{i}") for i in range(4)]
        s_mhi, s_mlo, s_hi, s_lo, s_mm, s_res = (sem("m_mhi"), sem("m_mlo"), sem("m_hi"), sem("m_lo"),
                                                 sem("m_mm"), sem("m_res"))
        s_ss, s_var, s_std, s_sc, s_tr, s_thi, s_tlo = (sem("m_ss"), sem("m_var"), sem("m_std"), sem("m_sc"),
                                                        sem("m_tr"), sem("m_thi"), sem("m_tlo"))
        block = ctx.enter_context(nc.Block())

        @block.sync
        def _(sp):
            sp.dma_start(S.h[:, :, :], dram["x"]).then_inc(s_x, 16)
            for k in range(KT):
                if k >= 4:
                    sp.wait_ge(s_lo, k - 3)
                sp.dma_start(raw[:, k % 4, :], dram["wout"][k]).then_inc(s_raw[k % 4], 16)

        @block.scalar
        def _(act):
            st = Steps(act, S.own_act, S.counts)
            for k in range(KT):
                st.do(act.activation(mx_hi[:, k, :], S.mixed[:, k, :], ACT.Copy), s_mhi)
                act.wait_ge(s_raw[k % 4], 16 * (k // 4 + 1))
                if k >= SPL:
                    act.wait_ge(s_mm, k - SPL + 1)
                st.do(act.activation(w_hi[:, k % SPL, :], raw[:, k % 4, :], ACT.Copy), s_hi)
            for t in range(TT):
                act.wait_ge(s_res, 2 * t + 2)
                if t:
                    st.settle()
                st.do(act.activation(sq[:, :], S.h[:, t, :], ACT.Square, accum_out=ss[:, t:t + 1]), s_ss)
            act.wait_ge(s_var, 1)
            st.do(act.activation(ss[:, :], ss[:, :], ACT.Sqrt), s_std)
            for k in range(KT):
                act.wait_ge(s_tr, k + 1)
                st.do(act.activation(S.xn_hi[:, k, :], S.ps[:, k, :], ACT.Copy, scale=S.param("g_ffn", k)), s_thi)

        @block.vector
        def _(dve):
            st = Steps(dve, S.own_dve, S.counts)
            v = nc.vector
            for k in range(KT):
                dve.wait_ge(s_mhi, k + 1)
                st.do(v.tensor_tensor(mx_lo[:, k, :], S.mixed[:, k, :], mx_hi[:, k, :].bitcast(F32), ALU.subtract),
                      s_mlo)
                dve.wait_ge(s_hi, k + 1)
                st.do(v.tensor_tensor(w_lo[:, k % SPL, :], raw[:, k % 4, :], w_hi[:, k % SPL, :].bitcast(F32),
                                      ALU.subtract), s_lo)
            dve.wait_ge(s_x, 16)
            dve.wait_ge(s_mm, KT)
            for o in range(8):
                t, d = divmod(o, 2)
                st.do(v.tensor_tensor(S.h[:, t, d * T:(d + 1) * T], S.h[:, t, d * T:(d + 1) * T], S.ps[:, o, :],
                                      ALU.add), s_res)
            dve.wait_ge(s_ss, TT)
            st.do(v.tensor_scalar(ss[:, :], ss[:, :], 1.0 / D, RMS_EPS, ALU.mult, ALU.add))
            st.settle()
            st.do(v.reciprocal(ss[:, :], ss[:, :]), s_var)
            dve.wait_ge(s_std, 1)
            for t in range(TT):
                st.do(v.tensor_scalar(xs[:, t, :], S.h[:, t, :], ss[:, t:t + 1], None, ALU.mult), s_sc)
            for k in range(KT):
                dve.wait_ge(s_thi, k + 1)
                st.do(v.scalar_tensor_tensor(S.xn_lo[:, k, :], S.ps[:, k, :], S.param("g_ffn", k),
                                             S.xn_hi[:, k, :].bitcast(F32), ALU.mult, ALU.subtract), s_tlo)

        @block.tensor
        def _(pe):
            for k in range(KT):
                pe.wait_ge(s_mlo, k + 1)
                pe.wait_ge(s_lo, k + 1)
                for o in range(8):
                    t, d = divmod(o, 2)
                    x, w = slice(t * P, (t + 1) * P), slice(d * T, (d + 1) * T)
                    last = three_pass(nc, S.ps[:, o, :], mx_hi[:, k, x], mx_lo[:, k, x], w_hi[:, k % SPL, w],
                                      w_lo[:, k % SPL, w], k == 0, k == KT - 1)
                last.then_inc(s_mm, 1)
            pe.wait_ge(s_res, 8)
            pe.wait_ge(s_sc, TT)
            for k in range(KT):
                for t in range(TT):
                    last = nc.tensor.transpose(S.ps[:, k, t * P:(t + 1) * P], xs[:, t, k * P:(k + 1) * P],
                                               S.const("ident"))
                last.then_inc(s_tr, 1)


def route(nc, S, dram):
    sem = S.sem
    NQ = 2 * PH
    with ExitStack() as ctx:
        def sb(name, shape, dt=F32):
            return ctx.enter_context(nc.sbuf_tensor(name, shape, dt))

        raw = sb("wq_raw", [P, RAW, D])
        w_hi = sb("wq_hi", [P, SPL, D], F32R)
        w_lo = sb("wq_lo", [P, SPL, D], F32R)
        keys = sb("sub_keys", [P, 2, NKEY])
        qt = sb("q_t", [P, 4, T])
        sc = sb("key_scores", [P, 2, TT, 2, NKEY])
        sc2 = sb("key_scores_left", [P, TT, 2, NKEY])
        top = sb("top_scores", [P, TT, PH, 2, TOPK])
        topi = sb("top_index", [P, TT, PH, 2, TOPK], U32)
        topf = sb("top_index_f", [P, TT, PH, 2, TOPK])
        cand = sb("cand", [P, TT, NCAND])
        cand2 = sb("cand_left", [P, TT, NCAND])
        best = sb("best", [P, TT, PH, TOPK])
        pos = sb("pos", [P, TT, PH, TOPK], U32)
        bits = sb("pos_bits", [P, 2, TT * PH * TOPK], U32)
        posf = sb("pos_f", [P, 3, TT * PH * TOPK])
        small = sb("small", [P, TT * PH])
        delta = sb("delta", [P, TT, PH, TOPK])
        wide = sb("wide", [P, PH * TOPK, TOPK])
        widej = sb("wide_j", [P, PH * TOPK, TOPK])
        tab = S.mixed[:, 0:3, :].rearrange("p w (t k) -> p w t k", k=PH * TOPK)
        s_k = sem("q_k")
        s_raw = [sem(f"q_raw{i}") for i in range(RAW)]
        s_hi, s_lo, s_mm, s_q, s_s, s_sev, s_top = (sem("q_hi"), sem("q_lo"), sem("q_mm"), sem("q_q"), sem("q_s"),
                                                    sem("q_sev"), sem("q_top"))
        s_sub, s_e, s_b, s_j, s_jr, s_tab, s_tr, s_out = (sem("q_sub"), sem("q_e"), sem("q_b"), sem("q_j"),
                                                          sem("q_jr"), sem("q_tab"), sem("q_tr"), sem("q_out"))
        block = ctx.enter_context(nc.Block())

        @block.sync
        def _(sp):
            sp.dma_start(keys[:, :, :], dram["keys_t"]).then_inc(s_k, 16)
            for n in range(NQ):
                if n >= RAW:
                    sp.wait_ge(s_lo, n - RAW + 1)
                sp.dma_start(raw[:, n % RAW, :], dram["wq_t"][n]).then_inc(s_raw[n % RAW], 16)

        @block.gpsimd
        def _(pool):
            st = Steps(pool, S.own_pool, S.counts)
            for n in range(NQ):
                pool.wait_ge(s_hi, n + 1)
                st.do(pool.tensor_tensor(w_lo[:, n % SPL, :], raw[:, n % RAW, :], w_hi[:, n % SPL, :].bitcast(F32),
                                         ALU.subtract), s_lo)
            pool.wait_ge(s_b, 1)
            for t in range(TT):
                b = posf[:, 0, t * P:(t + 1) * P]
                if t:
                    pool.wait_ge(s_jr, t)
                st.do(pool.tensor_tensor(widej[:, :, :], bc(S.const("iota")[:, 0:TOPK], 1, P), bc(b, 2, TOPK),
                                         ALU.subtract))
                st.settle()
                st.do(pool.tensor_scalar(widej[:, :, :], widej[:, :, :], 0.0, None, ALU.is_equal))
                st.settle()
                wj = widej[:, :, :].rearrange("p (h k) b -> p h k b", h=PH)
                st.do(pool.tensor_tensor(wj, wj, bc(topf[:, t, :, 1, :], 2, TOPK), ALU.mult), s_j)

        @block.scalar
        def _(act):
            st = Steps(act, S.own_act, S.counts)

            def take_q(n):
                act.wait_ge(s_mm, n + 1)
                if n >= 4:
                    act.wait_ge(s_s, n // 2 - 1)
                st.do(act.activation(qt[:, n % 4, :], S.ps[:, n % 3, :], ACT.Copy), s_q)

            def take_scores(h):
                act.wait_ge(s_s, h + 1)
                if h >= 2:
                    act.wait_ge(s_top, h - 1)
                for c in range(2):
                    st.do(act.activation(sc[:, h % 2, :, c, :],
                                         S.ps[:, 3 + c, :].rearrange("p (t k) -> p t k", k=NKEY), ACT.Copy), s_sev)

            for n in range(NQ):
                act.wait_ge(s_raw[n % RAW], 16 * (n // RAW + 1))
                if n >= SPL:
                    act.wait_ge(s_mm, n - SPL + 1)
                st.do(act.activation(w_hi[:, n % SPL, :], raw[:, n % RAW, :], ACT.Copy), s_hi)
                if n >= 1:
                    take_q(n - 1)
                if n >= 4 and n % 2 == 0:
                    take_scores(n // 2 - 2)
            take_q(NQ - 1)
            take_scores(PH - 2)
            take_scores(PH - 1)
            act.wait_ge(s_sub, 1)
            st.do(act.activation(best[:, :, :, :], best[:, :, :, :], ACT.Exp), s_e)
            for w in range(3):
                act.wait_ge(s_tr, w + 1)
                st.do(act.activation(S.tab[:, w, :], S.ps[:, w, :], ACT.Copy), s_out)

        @block.tensor
        def _(pe):
            pe.wait_ge(s_k, 16)

            def scores(h):
                pe.wait_ge(s_q, 2 * h + 2)
                if h >= 1:
                    pe.wait_ge(s_sev, 2 * h)
                for c in range(2):
                    for t in range(TT):
                        last = nc.tensor.matmul(S.ps[:, 3 + c, t * P:(t + 1) * P],
                                                qt[:, (2 * h + c) % 4, t * P:(t + 1) * P], keys[:, c, :],
                                                start=True, stop=True)
                last.then_inc(s_s, 1)

            for n in range(NQ):
                pe.wait_ge(s_lo, n + 1)
                if n >= 3:
                    pe.wait_ge(s_q, n - 2)
                for k in range(KT):
                    w = slice(k * P, (k + 1) * P)
                    last = three_pass(nc, S.ps[:, n % 3, :], w_hi[:, n % SPL, w], w_lo[:, n % SPL, w],
                                      S.xn_hi[:, k, :], S.xn_lo[:, k, :], k == 0, k == KT - 1)
                last.then_inc(s_mm, 1)
                if n >= 2 and n % 2 == 0:
                    scores(n // 2 - 1)
            scores(PH - 1)
            pe.wait_ge(s_q, NQ)
            for w in range(3):
                pe.wait_ge(*((s_tab, 1), (s_jr, TT), (s_tab, 2))[w])
                for t in range(TT):
                    last = nc.tensor.transpose(S.ps[:, w, t * P:(t + 1) * P], tab[:, w, t, :], S.const("ident"))
                last.then_inc(s_tr, 1)

        @block.vector
        def _(dve):
            st = Steps(dve, S.own_dve, S.counts)
            v = nc.vector
            both = [(t, c) for t in range(TT) for c in range(2)]
            for h in range(PH):
                dve.wait_ge(s_sev, 2 * h + 2)
                for t, c in both:
                    st.do(v.max(top[:, t, h, c, 0:8], sc[:, h % 2, t, c, :]))
                st.settle()
                for t, c in both:
                    st.do(v.max_index(topi[:, t, h, c, 0:8], top[:, t, h, c, 0:8], sc[:, h % 2, t, c, :]))
                    st.do(v.match_replace(sc2[:, t, c, :], top[:, t, h, c, 0:8], sc[:, h % 2, t, c, :], LOWEST))
                st.settle()
                for t, c in both:
                    st.do(v.max(top[:, t, h, c, 8:16], sc2[:, t, c, :]))
                st.settle()
                for t, c in both:
                    st.do(v.max_index(topi[:, t, h, c, 8:16], top[:, t, h, c, 8:16], sc2[:, t, c, :]))
                s0, s1 = top[:, :, h, 0, :], top[:, :, h, 1, :]
                for lo, a0, na, nb in ((0, 0, 1, 16), (16, 1, 3, 8), (40, 4, 4, 4), (56, 8, 8, 1)):
                    out = cand[:, :, lo:lo + na * nb].rearrange("p t (a b) -> p t a b", b=nb)
                    st.do(v.tensor_tensor(out, bc(s0[:, :, a0:a0 + na], 3, nb), bc(s1[:, :, 0:nb], 2, na), ALU.add))
                st.settle()
                for t in range(TT):
                    st.do(v.max(best[:, t, h, 0:8], cand[:, t, :]))
                st.settle()
                for t in range(TT):
                    st.do(v.max_index(pos[:, t, h, 0:8], best[:, t, h, 0:8], cand[:, t, :]))
                    st.do(v.match_replace(cand2[:, t, :], best[:, t, h, 0:8], cand[:, t, :], LOWEST))
                st.settle()
                for t in range(TT):
                    st.do(v.max(best[:, t, h, 8:16], cand2[:, t, :]))
                st.settle()
                for t in range(TT):
                    last = v.max_index(pos[:, t, h, 8:16], best[:, t, h, 8:16], cand2[:, t, :])
                    st.do(last, s_top if t == TT - 1 else None)
                st.settle()
            st.do(v.tensor_copy(small[:, :].rearrange("p (t h) -> p t h", h=PH), best[:, :, :, 0]))
            st.do(v.tensor_copy(topf[:, :, :, :, :], topi[:, :, :, :, :]))
            p32 = pos[:, :, :, :].rearrange("p t h k -> p (t h k)")
            st.do(v.tensor_scalar(bits[:, 0, :], p32, 7, None, ALU.bitwise_and))
            st.do(v.tensor_scalar(bits[:, 1, :], p32, 3, None, ALU.bitwise_and))
            st.do(v.tensor_copy(posf[:, 0, :], p32))
            st.settle()
            bst = best[:, :, :, :].rearrange("p t h k -> p (t h) k")
            st.do(v.tensor_tensor(bst, bst, bc(small[:, :], 2, TOPK), ALU.subtract), s_sub)
            st.do(v.tensor_copy(posf[:, 1, :], bits[:, 0, :]))
            st.do(v.tensor_copy(posf[:, 2, :], bits[:, 1, :]))
            st.do(v.tensor_tensor(delta[:, :, :, 1:TOPK], topf[:, :, :, 0, 1:TOPK], topf[:, :, :, 0, 0:TOPK - 1],
                                  ALU.subtract))
            st.settle()
            for t in range(TT):
                p_t = posf[:, 0, t * P:(t + 1) * P]
                w15 = wide[:, :, 0:TOPK - 1]
                st.do(v.tensor_tensor(w15, bc(p_t, 2, TOPK - 1), bc(S.const("row_starts"), 1, P), ALU.is_ge))
                st.settle()
                w4 = w15.rearrange("p (h k) b -> p h k b", h=PH)
                st.do(v.tensor_tensor(w4, w4, bc(delta[:, t, :, 1:TOPK], 2, TOPK), ALU.mult))
                st.settle()
                st.do(v.tensor_reduce(tab[:, 0, t, :], w15, AX, ALU.add))
                st.settle()
            row0 = topf[:, :, :, 0, 0]
            t0 = tab[:, 0, :, :].rearrange("p t (h k) -> p t h k", h=PH)
            st.do(v.tensor_tensor(t0, t0, bc(row0, 3, TOPK), ALU.add), s_tab)
            st.do(v.tensor_tensor(posf[:, 2, :], posf[:, 2, :], posf[:, 1, :], ALU.subtract))
            st.do(v.tensor_scalar(bits[:, 0, :].bitcast(F32), posf[:, 0, :], 16.0, None, ALU.is_lt))
            st.settle()
            lt16 = bits[:, 0, :].bitcast(F32)
            acc = bits[:, 1, :].bitcast(F32)
            st.do(v.scalar_tensor_tensor(acc, posf[:, 0, :], 40.0, posf[:, 2, :], ALU.is_ge, ALU.mult))
            st.settle()
            st.do(v.tensor_tensor(acc, acc, posf[:, 1, :], ALU.add))
            st.settle()
            st.do(v.scalar_tensor_tensor(acc, posf[:, 0, :], 56.0, acc, ALU.is_lt, ALU.mult))
            st.settle()
            st.do(v.tensor_tensor(posf[:, 1, :], posf[:, 0, :], acc, ALU.subtract))
            st.settle()
            st.do(v.tensor_tensor(posf[:, 1, :], posf[:, 1, :], lt16, ALU.mult))
            st.settle()
            st.do(v.tensor_tensor(posf[:, 0, :], posf[:, 1, :], acc, ALU.add), s_b)
            for t in range(TT):
                dve.wait_ge(s_j, t + 1)
                st.do(v.tensor_reduce(tab[:, 1, t, :], widej[:, :, :], AX, ALU.add), s_jr)
            dve.wait_ge(s_e, 1)
            st.do(v.tensor_reduce(small[:, :], bst, AX, ALU.add))
            st.settle()
            st.do(v.reciprocal(small[:, :], small[:, :]))
            st.settle()
            st.do(v.tensor_tensor(tab[:, 2, :, :].rearrange("p t (h k) -> p (t h) k", h=PH), bst,
                                  bc(small[:, :], 2, TOPK), ALU.mult), s_tab)


def spread(nc, S, dram):
    sem = S.sem
    Q = 4
    NQB = SW // Q
    with ExitStack() as ctx:
        def sb(name, shape, dt=F32):
            return ctx.enter_context(nc.sbuf_tensor(name, shape, dt))

        rows = [sb(f"onehot_rows{i}", [P, Q, NKEY]) for i in range(2)]
        cols = [sb(f"gated_cols{i}", [P, Q, NKEY]) for i in range(2)]
        stage = [sb(f"gate_stage{i}", [P, NKEY, SW]) for i in range(2)]
        s_rows, s_cols, s_w, s_st, s_out0, s_out1 = (sem("w_rows"), sem("w_cols"), sem("w_w"), sem("w_st"),
                                                     sem("w_out0"), sem("w_out1"))
        s_diff = sem("w_diff")
        s_out = [s_out0, s_out1]
        block = ctx.enter_context(nc.Block())
        tab = S.tab

        @block.gpsimd
        def _(pool):
            for s in range(NSW):
                with pool.Fori(0, NQB // 2) as i:
                    for e in range(2):
                        n = s * NQB + 2 * i + e
                        tok = s * SW + (2 * i + e) * Q
                        pool.wait_ge(S.w_free, n + 1)
                        pool.tensor_tensor(rows[e][:, :, :], bc(S.const("iota"), 1, Q),
                                           bc(tab[:, 0, bass.ds(tok, Q)], 2, NKEY), ALU.subtract).then_inc(s_diff, 1)
                        pool.wait_ge(S.w_free, 1)
                        pool.wait_ge(s_diff, n + 1)
                        pool.nop()
                        pool.tensor_scalar(rows[e][:, :, :], rows[e][:, :, :], 0.0, None,
                                           ALU.is_equal).then_inc(s_rows, 1)

        @block.vector
        def _(dve):
            for s in range(NSW):
                with dve.Fori(0, NQB // 2) as i:
                    for e in range(2):
                        n = s * NQB + 2 * i + e
                        tok = s * SW + (2 * i + e) * Q
                        dve.wait_ge(S.w_free, n + 1)
                        for q in range(Q):
                            nc.vector.tensor_scalar(cols[e][:, q, :], S.const("iota"), tab[:, 1, bass.ds(tok + q, 1)],
                                                    tab[:, 2, bass.ds(tok + q, 1)], ALU.is_equal,
                                                    ALU.mult).then_inc(s_cols, 1)

        @block.tensor
        def _(pe):
            pe.nop().then_inc(S.w_free, 1)
            pe.nop().then_inc(S.w_free, 1)
            for s in range(NSW):
                with pe.Fori(0, NQB // 2) as i:
                    for e in range(2):
                        n = s * NQB + 2 * i + e
                        pe.wait_ge(s_rows, n + 1)
                        pe.wait_ge(s_cols, Q * (n + 1))
                        pe.wait_ge(S.w_bank, n + 1)
                        for q in range(Q):
                            last = nc.tensor.matmul(S.ps[:, e, q * P:(q + 1) * P], rows[e][:, q, :], cols[e][:, q, :],
                                                    start=True, stop=True)
                        last.then_inc(S.w_free, 1)

        @block.scalar
        def _(act):
            act.nop().then_inc(S.w_bank, 1)
            act.nop().then_inc(S.w_bank, 1)
            for s in range(NSW):
                if s >= 2:
                    act.wait_ge(s_out[s % 2], 16 * (s // 2))
                with act.Fori(0, NQB // 2) as i:
                    for e in range(2):
                        n = s * NQB + 2 * i + e
                        tok = (2 * i + e) * Q
                        act.wait_ge(S.w_free, n + 3)
                        act.activation(stage[s % 2][:, :, bass.ds(tok, Q)].rearrange("p j t -> p t j"),
                                       S.ps[:, e, :].rearrange("p (t j) -> p t j", j=NKEY),
                                       ACT.Copy).then_inc(S.w_bank, 1)

        @block.sync
        def _(sp):
            for s in range(NSW):
                sp.wait_ge(S.w_bank, 2 + NQB * (s + 1))
                sp.dma_start(dram["gates"][s], stage[s % 2][:, :, :]).then_inc(s_out[s % 2], 16)
            for e in range(2):
                sp.wait_ge(s_out[e], 16 * (NSW // 2))


def experts(nc, S, dram):
    sem = S.sem
    with ExitStack() as ctx:
        def sb(name, shape, dt=F32):
            return ctx.enter_context(nc.sbuf_tensor(name, shape, dt))

        u_raw = sb("u_raw", [P, 2, EG, D])
        v_raw = sb("v_raw", [P, 2, EG, D])
        u_hi = sb("u_hi", [P, 2, D], F32R)
        u_lo = sb("u_lo", [P, 2, D], F32R)
        v_hi = sb("v_hi", [P, 2, EG, D], F32R)
        v_lo = sb("v_lo", [P, 2, EG, D], F32R)
        gates = sb("gates", [P, 2, NSW, EG, SW])
        act_g = sb("act_g", [P, 2, T])
        a_hi = sb("a_hi", [P, 2, EG, T], F32R)
        a_lo = sb("a_lo", [P, 2, EG, T], F32R)
        ss = sb("o_ss", [P, TT])
        s_u = [sem(f"e_u{i}") for i in range(2)]
        s_v = [sem(f"e_v{i}") for i in range(2)]
        s_g = [sem(f"e_g{i}") for i in range(2)]
        s_uhi, s_ulo, s_h, s_gelu, s_gated, s_ahi, s_alo = (sem("e_uhi"), sem("e_ulo"), sem("e_h"), sem("e_gelu"),
                                                            sem("e_gated"), sem("e_ahi"), sem("e_alo"))
        s_vhi, s_vlo, s_o, s_acc = sem("e_vhi"), sem("e_vlo"), sem("e_o"), sem("e_acc")
        s_ss, s_var, s_std, s_sc, s_out = sem("e_ss"), sem("e_var"), sem("e_std"), sem("e_sc"), sem("e_out")
        block = ctx.enter_context(nc.Block())

        def groups(eng, step):
            step(0, 0, True, False, 1, 1)
            with eng.Fori(0, (NG - 2) // 2) as i:
                step(2 * i + 1, 1, False, False, i + 1, i + 2)
                step(2 * i + 2, 0, False, False, i + 2, i + 2)
            step(NG - 1, (NG - 1) % 2, False, True, NG // 2, None)

        def loads(sp, g, p, fresh):
            if not fresh:
                sp.wait_ge(s_ulo, EG * (g - 1))
            sp.dma_start(u_raw[:, p, :, :], dram["u_t"][:, bass.ds(g * EG, EG), :]).then_inc(s_u[p], 16)
            if not fresh:
                sp.wait_ge(s_gated, EG * (g - 1))
            sp.dma_start(gates[:, p, :, :, :], dram["gates_in"][:, :, bass.ds(g * EG, EG), :]).then_inc(s_g[p], 16)
            if not fresh:
                sp.wait_ge(s_vlo, EG * (g - 1))
            sp.dma_start(v_raw[:, p, :, :], dram["v"][:, bass.ds(g * EG, EG), :]).then_inc(s_v[p], 16)

        @block.sync
        def _(sp):
            loads(sp, 0, 0, True)
            loads(sp, 1, 1, True)
            with sp.Fori(0, (NG - 2) // 2) as i:
                loads(sp, 2 * i + 2, 0, False)
                loads(sp, 2 * i + 3, 1, False)
            for t in range(TT):
                sp.wait_ge(s_sc, t + 1)
                sp.dma_start(dram["out"][t * P:(t + 1) * P, :], S.h[:, t, :]).then_inc(s_out, 16)
            sp.wait_ge(s_out, 16 * TT)

        @block.scalar
        def _(act):
            def split_u(n, e, p, landed, fresh):
                act.wait_ge(s_u[p], landed)
                if not fresh:
                    act.wait_ge(s_h, n - 1)
                act.activation(u_hi[:, e, :], u_raw[:, p, e, :], ACT.Copy).then_inc(s_uhi, 1)

            def step(g, p, first, last, loaded, loaded_next):
                for e in range(EG):
                    n = EG * g + e
                    if e == 0:
                        split_u(n + 1, 1, p, 16 * loaded, first)
                    elif not last:
                        split_u(n + 1, 0, 1 - p, 16 * loaded_next, False)
                    act.wait_ge(s_h, n + 1)
                    if not first:
                        act.wait_ge(s_gated, n - 1)
                        act.wait_ge(s_alo, n - 1)
                    act.activation(act_g[:, e, :], S.ps[:, e, :], ACT.Gelu).then_inc(s_gelu, 1)
                    act.wait_ge(s_v[p], 16 * loaded)
                    if not first and not (isinstance(g, int) and g < 2):
                        act.wait_ge(s_o, 8 * (g - 1))
                    act.activation(v_hi[:, p, e, :], v_raw[:, p, e, :], ACT.Copy).then_inc(s_vhi, 1)
                    act.wait_ge(s_gated, n + 1)
                    act.activation(a_hi[:, p, e, :], act_g[:, e, :], ACT.Copy).then_inc(s_ahi, 1)

            split_u(0, 0, 0, 16, True)
            groups(act, step)
            for t in range(TT):
                act.wait_ge(s_acc, 8 * NG + 8)
                act.activation(act_g[:, :, :], S.h[:, t, :].rearrange("p (a b) -> p a b", a=2), ACT.Square,
                               accum_out=ss[:, t:t + 1]).then_inc(s_ss, 1)
                act.wait_ge(s_ss, t + 1)
            act.wait_ge(s_var, 1)
            act.activation(ss[:, :], ss[:, :], ACT.Sqrt).then_inc(s_std, 1)

        @block.vector
        def _(dve):
            v = nc.vector

            def split_u(n, e, p):
                dve.wait_ge(s_uhi, n + 1)
                v.tensor_tensor(u_lo[:, e, :], u_raw[:, p, e, :], u_hi[:, e, :].bitcast(F32),
                                ALU.subtract).then_inc(s_ulo, 1)

            def accumulate(g, e):
                for o in range(4 * e, 4 * e + 4):
                    t, d = divmod(o, 2)
                    dve.wait_ge(s_o, 8 * g + o + 1)
                    dve.wait_ge(s_acc, 8 * g + o + 1)
                    v.tensor_tensor(S.h[:, t, d * T:(d + 1) * T], S.h[:, t, d * T:(d + 1) * T], S.ps[:, 4 + o % 4, :],
                                    ALU.add).then_inc(s_acc, 1)

            def step(g, p, first, last, loaded, loaded_next):
                for e in range(EG):
                    n = EG * g + e
                    if e == 0:
                        split_u(n + 1, 1, p)
                    elif not last:
                        split_u(n + 1, 0, 1 - p)
                    dve.wait_ge(s_gelu, n + 1)
                    dve.wait_ge(s_g[p], 16 * loaded)
                    v.tensor_tensor(act_g[:, e, :].rearrange("p (s t) -> p s t", t=SW),
                                    act_g[:, e, :].rearrange("p (s t) -> p s t", t=SW), gates[:, p, :, e, :],
                                    ALU.mult).then_inc(s_gated, 1)
                    if not first:
                        accumulate(g - 1, e)
                    dve.wait_ge(s_vhi, n + 1)
                    v.tensor_tensor(v_lo[:, p, e, :], v_raw[:, p, e, :], v_hi[:, p, e, :].bitcast(F32),
                                    ALU.subtract).then_inc(s_vlo, 1)
                    dve.wait_ge(s_ahi, n + 1)
                    v.tensor_tensor(a_lo[:, p, e, :], act_g[:, e, :], a_hi[:, p, e, :].bitcast(F32),
                                    ALU.subtract).then_inc(s_alo, 1)

            dve.nop().then_inc(s_acc, 8)
            split_u(0, 0, 0)
            groups(dve, step)
            accumulate(NG - 1, 0)
            accumulate(NG - 1, 1)
            dve.wait_ge(s_ss, TT)
            st = Steps(dve, S.own_dve, S.counts)
            st.do(v.tensor_scalar(ss[:, :], ss[:, :], 1.0 / D, RMS_EPS, ALU.mult, ALU.add))
            st.settle()
            st.do(v.reciprocal(ss[:, :], ss[:, :]), s_var)
            dve.wait_ge(s_std, 1)
            for t in range(TT):
                st.do(v.scalar_tensor_tensor(S.h[:, t, :], S.h[:, t, :], ss[:, t:t + 1], S.g_final[:, :],
                                             ALU.mult, ALU.mult), s_sc)

        @block.tensor
        def _(pe):
            def hidden(n, e, fresh):
                pe.wait_ge(s_ulo, n + 1)
                if not fresh:
                    pe.wait_ge(s_gelu, n - 1)
                for k in range(KT):
                    w = slice(k * P, (k + 1) * P)
                    last = three_pass(nc, S.ps[:, e, :], u_hi[:, e, w], u_lo[:, e, w], S.xn_hi[:, k, :],
                                      S.xn_lo[:, k, :], k == 0, k == KT - 1)
                last.then_inc(s_h, 1)

            def outputs(g, e, p):
                if e == 0:
                    pe.wait_ge(s_alo, EG * (g + 1))
                    pe.wait_ge(s_vlo, EG * (g + 1))
                for o in range(4 * e, 4 * e + 4):
                    t, d = divmod(o, 2)
                    x, w = slice(t * P, (t + 1) * P), slice(d * T, (d + 1) * T)
                    pe.wait_ge(s_acc, 8 * g + o + 5)
                    for k in range(EG):
                        last = three_pass(nc, S.ps[:, 4 + o % 4, :], a_hi[:, p, k, x], a_lo[:, p, k, x],
                                          v_hi[:, p, k, w], v_lo[:, p, k, w], k == 0, k == EG - 1)
                    last.then_inc(s_o, 1)

            def step(g, p, first, last, loaded, loaded_next):
                for e in range(EG):
                    hidden(EG * g + e, e, first)
                    if not first:
                        outputs(g - 1, e, 1 - p)

            groups(pe, step)
            outputs(NG - 1, 0, (NG - 1) % 2)
            outputs(NG - 1, 1, (NG - 1) % 2)


def build(nc, dram):
    with ExitStack() as ctx:
        def sb(name, shape, dt=F32):
            return ctx.enter_context(nc.sbuf_tensor(name, shape, dt))

        S = Shared()
        S.counts = {}
        S.sem = lambda name: ctx.enter_context(nc.semaphore(name))
        S.own_dve, S.own_act, S.own_pool = S.sem("own_dve"), S.sem("own_act"), S.sem("own_pool")
        S.w_free, S.w_bank = S.sem("w_free"), S.sem("w_bank")
        S.ps = ctx.enter_context(nc.psum_tensor("ps", [P, 8, 512], F32))
        S.consts = sb("consts", [P, NCONST])
        S.params = sb("params", [P, NPARAM])
        S.g_final = sb("g_final", [P, D])
        S.const = lambda name: S.consts[:, CONST_COLS[name][0]:CONST_COLS[name][1]]
        S.param = lambda name, j: S.params[:, PARAM_COLS[name][0] + j:PARAM_COLS[name][0] + j + 1]
        S.param_all = lambda name: S.params[:, PARAM_COLS[name][0]:PARAM_COLS[name][1]]
        with ExitStack() as front:
            def sf(name, shape, dt=F32):
                return front.enter_context(nc.sbuf_tensor(name, shape, dt))

            S.up = sf("up_weights", [P, 2, T])
            S.mixed = sf("mixed", [P, KT, T])
            with ExitStack() as rwkv:
                def sr(name, shape, dt=F32):
                    return rwkv.enter_context(nc.sbuf_tensor(name, shape, dt))

                S.zm = sr("z_mixed", [P, NRW, T])
                with ExitStack() as attn:
                    S.qk = attn.enter_context(nc.sbuf_tensor("qk", [P, NQK, T], F32))
                    S.v_tok = attn.enter_context(nc.sbuf_tensor("v_tok", [P, TT, T], F32))
                    project(nc, S, dram)
                    attend(nc, S, dram)
                S.gate = sr("gate", [P, HP, T])
                S.v_chunk = sr("v_chunk", [P, NCH, HP, HD])
                S.pc = sr("chunk_decay", [P, HP, NCH])
                S.ra = sr("r_and_a", [P, HP, NCH, 2, C])
                S.bs = sr("b_scaled", [P, HP, T])
                S.ks = sr("k_scaled", [P, HP, T])
                prepare(nc, S, dram)
                S.y_chunk = S.zm[:, 4:8, :].rearrange("p a (b j i) -> p (a b) j i", b=2, i=HD)
                scan(nc, S, dram)
                normalise_heads(nc, S, dram)
            S.h = sf("h", [P, TT, D])
            S.xn_hi = sf("xn2_hi", [P, KT, T], F32R)
            S.xn_lo = sf("xn2_lo", [P, KT, T], F32R)
            S.tab = sf("tables", [P, 3, T])
            mix(nc, S, dram)
            route(nc, S, dram)
            spread(nc, S, dram)
            experts(nc, S, dram)


def kernel(**inputs):
    import concourse.bacc as bacc
    from concourse.bass_utils import run_bass_kernel_spmd

    a = {k: np.ascontiguousarray(v) for k, v in inputs.items()}
    f = np.ascontiguousarray
    x = a["x"][0]
    w_in = a["w_in"][0]
    cols = (NRW + NQK) * P
    win_cols = w_in[:, :cols].reshape(KT, P, NRW + NQK, P).transpose(2, 1, 0, 3).reshape(NRW + NQK, P, D)
    win_v = w_in[:, cols:].reshape(NV, 2, P, T).transpose(0, 2, 1, 3).reshape(NV, P, D)

    def tiles(vec):
        return vec.reshape(-1, P).T

    par = np.concatenate([tiles(a["norm_mix"][0]), tiles(a["rwkv_mu"][0]), tiles(a["rwkv_w0"][0]),
                          tiles(a["rwkv_a0"][0]), tiles(a["rwkv_k_k"][0]), tiles(a["rwkv_k_a"][0]),
                          tiles(a["rwkv_r_k"][0].reshape(-1)), tiles(a["rwkv_gn_w"][0]), tiles(a["rwkv_gn_b"][0]),
                          tiles(a["norm_ffn"][0])], axis=1)
    up = np.stack([np.concatenate([a["rwkv_w_up"][0], a["rwkv_a_up"][0]], axis=0), a["rwkv_g_up"][0]], axis=1)
    arrays = {
        "x_t": f(x.T.reshape(KT, P, T).transpose(1, 0, 2)),
        "x": f(x.reshape(TT, P, D).transpose(1, 0, 2)),
        "win_t": f(np.concatenate([win_cols, win_v], axis=0)),
        "consts": build_constants(),
        "params": f(par),
        "up": f(up),
        "g_final": f(np.broadcast_to(a["norm_final"][None, :], (P, D))),
        "wout": f(a["w_out"][0].reshape(KT, P, D)),
        "wq_t": f(a["peer_w_q"][0].reshape(KT, P, 2 * PH, P).transpose(2, 1, 0, 3).reshape(2 * PH, P, D)),
        "keys_t": f(a["peer_sub_keys"][0].transpose(2, 0, 1)),
        "u_t": f(a["peer_u"][0].reshape(NKEY, NKEY, KT, P).transpose(3, 1, 2, 0).reshape(P, NKEY, D)),
        "v": f(a["peer_v"][0].reshape(NKEY, NKEY, D)),
    }
    nc = bacc.Bacc("TRN2", target_bir_lowering=False, num_devices=1)
    dram = {k: nc.dram_tensor(f"in_{k}", v.shape, mybir.dt.from_np(v.dtype), kind="ExternalInput").ap()
            for k, v in arrays.items()}
    dram["out"] = nc.dram_tensor("out_h", (T, D), F32, kind="ExternalOutput").ap()
    gates = nc.dram_tensor("gate_matrix", (NSW, P, NKEY, SW), F32, kind="Internal").ap()
    dram["gates"] = gates
    dram["gates_in"] = gates.rearrange("s p j t -> p s j t")
    build(nc, dram)
    r = run_bass_kernel_spmd(nc, [{f"in_{k}": v for k, v in arrays.items()}], core_ids=[0])
    return r.results[0]["out_h"].reshape(1, T, D)
```

```python
from contextlib import ExitStack

import concourse.bass as bass
import concourse.mybir as mybir
import numpy as np

F32 = mybir.dt.float32
F32R = mybir.dt.float32r
U32 = mybir.dt.uint32
ALU = mybir.AluOpType
ACT = mybir.ActivationFunctionType
AX = mybir.AxisListType.X

P = 128
D = 1024
T = 512
KT = D // P
TT = T // P
HD = 64
HP = 4
C = 64
NCH = T // C
NRW = 14
NQK = 8
NV = 4
NWIN = NRW + NQK + NV
PH = 8
TOPK = 16
NKEY = 128
NCAND = 64
RAW = 6
SPL = 3
KAPPA = float(np.exp(-0.5))
RMS_EPS = 1e-6
GN_EPS = 64e-5
LOWEST = -3.0e38
SW = 64
NSW = T // SW
EG = 2
NG = NKEY // EG

CONST_COLS = {}


def build_constants():
    parts = []
    at = 0

    def put(name, a):
        nonlocal at
        a = np.asarray(a, np.float32)
        CONST_COLS[name] = (at, at + a.shape[1])
        at += a.shape[1]
        parts.append(a)

    r = np.arange(P)
    put("ident", np.eye(P))
    swap = (r // HD) * HD + (r % HD + HD // 2) % HD
    perm = np.zeros((P, P))
    perm[swap, r] = 1.0
    put("perm", perm)
    put("block_ones", (r[:, None] // HD == r[None, :] // HD))
    put("ones", np.ones((P, P)))
    put("iota", np.tile(np.arange(P), (P, 1)))
    inv_freq = np.float32(10000.0) ** (-np.arange(0, HD, 2, dtype=np.float32) / np.float32(HD))
    ang = np.arange(T, dtype=np.float32)[None, :] * inv_freq[r % (HD // 2)][:, None]
    put("cos", np.cos(ang))
    put("sin", np.sin(ang) * np.where(r % HD < HD // 2, -1.0, 1.0)[:, None])
    cols = []
    for delta in range(TT - 1, -1, -1):
        dist = delta * P + r[:, None] - r[None, :]
        n = ((dist >= 0) & (dist <= 128)).astype(int)
        n += (dist >= 0) & (dist % 4 == 0)
        n += (dist >= 0) & (dist % 16 == 0)
        cols.append(np.where(n > 0, np.log(np.maximum(n, 1)), -1e30))
    put("attn_bias", np.concatenate(cols, axis=1))
    put("keep", np.tile((np.arange(T) % C != 0), (P, 1)))
    s, t = r[:, None] % C, np.arange(C)[None, :]
    put("strict", s < t)
    put("inclusive", s <= t)
    put("eye_compact", s == t)
    for level in range(6):
        m = 1 << level
        put(f"level{level}", (s // (2 * m) == t // (2 * m)) & (t // m < s // m))
    put("level0_t", (s // 2 == t // 2) & (s < t))
    starts = [16, 24, 32, 40, 44, 48, 52] + list(range(56, 64))
    put("row_starts", np.tile(starts, (P, 1)))
    return np.concatenate(parts, axis=1)


build_constants()
NCONST = max(b for _, b in CONST_COLS.values())
PARAM_COLS = {}
_at = 0
for _name, _n in (("g_mix", KT), ("mu", NRW), ("w0", HP), ("a0", HP), ("k_k", HP), ("k_a", HP), ("r_k", HP),
                  ("gn_w", HP), ("gn_b", HP), ("g_ffn", KT)):
    PARAM_COLS[_name] = (_at, _at + _n)
    _at += _n
NPARAM = _at


class Steps:

    def __init__(self, eng, own, counts):
        self.eng, self.own, self.counts, self.last = eng, own, counts, None

    def do(self, ins, signal=None):
        sem = self.own if signal is None else signal
        ins.then_inc(sem, 1)
        self.counts[sem.name] = self.counts.get(sem.name, 0) + 1
        self.last = (sem, self.counts[sem.name])

    def settle(self):
        self.eng.wait_ge(*self.last)


class Shared:
    pass


def bc(ap, axis, n):
    ap = ap.unsqueeze(axis)
    shape = list(ap.shape)
    shape[axis] = n
    return ap.to_broadcast(shape)


def three_pass(nc, out, w_hi, w_lo, m_hi, m_lo, first, last):
    nc.tensor.matmul(out, w_hi, m_hi, start=first, stop=False)
    nc.tensor.matmul(out, w_hi, m_lo, start=False, stop=False)
    return nc.tensor.matmul(out, w_lo, m_hi, start=False, stop=last)


def two_heads(nc, out, blocks, rhs, start=True, stop=True):
    for e in range(2):
        h = slice(e * HD, (e + 1) * HD)
        last = nc.tensor.matmul(out[h], blocks[:, h], rhs, start=start, stop=stop)
    return last


def project(nc, S, dram):
    sem = S.sem
    with ExitStack() as ctx:
        def sb(name, shape, dt=F32):
            return ctx.enter_context(nc.sbuf_tensor(name, shape, dt))

        xt = sb("x_t", [P, KT, T])
        sq = S.zm[:, 0:KT, :]
        rstd = sb("x_rstd", [P, T])
        xn_hi = sb("xn_hi", [P, KT, T], F32R)
        xn_lo = sb("xn_lo", [P, KT, T], F32R)
        raw = sb("win_raw", [P, RAW, D])
        w_hi = sb("win_hi", [P, SPL, D], F32R)
        w_lo = sb("win_lo", [P, SPL, D], F32R)
        zb = sb("z_shift", [P, 2, T + 1])
        zd = sb("z_delta", [P, 2, T])
        tmp = sb("rope_tmp", [P, 2, T])

        s_const = sem("p_const")
        s_perm, s_sin, s_rope = sem("p_perm"), sem("p_sin"), sem("p_rope")
        s_x = [sem(f"p_x{q}") for q in range(4)]
        s_raw = [sem(f"p_raw{i}") for i in range(RAW)]
        s_sq, s_ms, s_mean, s_rstd = sem("p_sq"), sem("p_ms"), sem("p_mean"), sem("p_rstd")
        s_xn, s_xhi, s_xlo = sem("p_xn"), sem("p_xhi"), sem("p_xlo")
        s_hi, s_lo, s_mm, s_out, s_zero, s_shift = (sem("p_hi"), sem("p_lo"), sem("p_mm"), sem("p_out"),
                                                    sem("p_zero"), sem("p_shift"))
        block = ctx.enter_context(nc.Block())

        @block.sync
        def _(sp):
            for q in range(4):
                sp.dma_start(xt[:, 2 * q:2 * q + 2, :], dram["x_t"][:, 2 * q:2 * q + 2, :]).then_inc(s_x[q], 16)
            for n in range(NWIN):
                if n >= RAW:
                    sp.wait_ge(s_lo, n - RAW + 1)
                sp.dma_start(raw[:, n % RAW, :], dram["win_t"][n]).then_inc(s_raw[n % RAW], 16)

        @block.gpsimd
        def _(pool):
            st = Steps(pool, S.own_pool, S.counts)
            st.do(pool.memset(zb[:, :, 0:1], 0.0), s_zero)

        @block.scalar
        def _(act):
            st = Steps(act, S.own_act, S.counts)
            act.dma_start(S.consts[:, :], dram["consts"]).then_inc(s_const, 16)
            act.dma_start(S.params[:, :], dram["params"]).then_inc(s_const, 16)
            act.dma_start(S.up[:, :, :], dram["up"]).then_inc(s_const, 16)
            act.dma_start(S.g_final[:, :], dram["g_final"]).then_inc(s_const, 16)
            for k in range(KT):
                if k % 2 == 0:
                    act.wait_ge(s_x[k // 2], 16)
                st.do(act.activation(sq[:, k, :], xt[:, k, :], ACT.Square), s_sq)
            act.wait_ge(s_mean, 2)
            st.do(act.activation(rstd[:, :], rstd[:, :], ACT.Sqrt), s_rstd)
            for k in range(KT):
                act.wait_ge(s_xn, k + 1)
                st.do(act.activation(xn_hi[:, k, :], xt[:, k, :], ACT.Copy), s_xhi)

            def take(n):
                act.wait_ge(s_mm, n + 1)
                if n < NRW:
                    if n == 0:
                        act.wait_ge(s_zero, 1)
                    if n >= 2:
                        act.wait_ge(s_shift, n - 1)
                    st.do(act.activation(zb[:, n % 2, 1:T + 1], S.ps[:, n % 3, :], ACT.Copy), s_out)
                else:
                    st.do(act.activation(S.qk[:, n - NRW, :], S.ps[:, n % 3, :], ACT.Copy), s_out)

            for n in range(NWIN):
                act.wait_ge(s_raw[n % RAW], 16 * (n // RAW + 1))
                if n >= SPL:
                    act.wait_ge(s_mm, n - SPL + 1)
                st.do(act.activation(w_hi[:, n % SPL, :], raw[:, n % RAW, :], ACT.Copy), s_hi)
                if 1 <= n <= NRW + NQK:
                    take(n - 1)
            act.wait_ge(s_mm, NWIN)
            for t in range(TT):
                st.do(act.activation(S.v_tok[:, t, :], S.ps[:, 4 + t, :], ACT.Copy), s_out)

        @block.vector
        def _(dve):
            st = Steps(dve, S.own_dve, S.counts)
            v = nc.vector
            dve.wait_ge(s_ms, 1)
            st.do(v.tensor_scalar(rstd[:, :], S.ps[:, 3, :], 1.0 / D, RMS_EPS, ALU.mult, ALU.add), s_mean)
            st.settle()
            st.do(v.reciprocal(rstd[:, :], rstd[:, :]), s_mean)
            dve.wait_ge(s_const, 64)
            dve.wait_ge(s_rstd, 1)
            for k in range(KT):
                st.do(v.scalar_tensor_tensor(xt[:, k, :], xt[:, k, :], S.param("g_mix", k), rstd[:, :],
                                             ALU.mult, ALU.mult), s_xn)
            for k in range(KT):
                dve.wait_ge(s_xhi, k + 1)
                st.do(v.tensor_tensor(xn_lo[:, k, :], xt[:, k, :], xn_hi[:, k, :].bitcast(F32), ALU.subtract), s_xlo)

            def shift(n):
                dve.wait_ge(s_out, n + 1)
                st.do(v.tensor_tensor(zd[:, n % 2, :], zb[:, n % 2, 0:T], zb[:, n % 2, 1:T + 1], ALU.subtract))
                st.settle()
                st.do(v.scalar_tensor_tensor(S.zm[:, n, :], zd[:, n % 2, :], S.param("mu", n), zb[:, n % 2, 1:T + 1],
                                             ALU.mult, ALU.add), s_shift)

            def rope(m):
                dve.wait_ge(s_perm, m + 1)
                st.do(v.tensor_tensor(tmp[:, m % 2, :], S.ps[:, 3, :], S.const("sin"), ALU.mult), s_sin)
                st.do(v.tensor_tensor(S.qk[:, m, :], S.qk[:, m, :], S.const("cos"), ALU.mult))
                st.settle()
                st.do(v.tensor_tensor(S.qk[:, m, :], S.qk[:, m, :], tmp[:, m % 2, :], ALU.add), s_rope)

            for n in range(NWIN):
                dve.wait_ge(s_hi, n + 1)
                st.do(v.tensor_tensor(w_lo[:, n % SPL, :], raw[:, n % RAW, :], w_hi[:, n % SPL, :].bitcast(F32),
                                      ALU.subtract), s_lo)
                if 1 <= n <= NRW:
                    shift(n - 1)
                if NRW < n - 1 < NRW + NQK + 1:
                    rope(n - 2 - NRW)

        @block.tensor
        def _(pe):
            pe.wait_ge(s_const, 64)
            for k in range(KT):
                pe.wait_ge(s_sq, k + 1)
                last = nc.tensor.matmul(S.ps[:, 3, :], S.const("ones"), sq[:, k, :], start=k == 0, stop=k == KT - 1)
            last.then_inc(s_ms, 1)
            def swap(m):
                pe.wait_ge(s_out, NRW + m + 1)
                if m:
                    pe.wait_ge(s_sin, m)
                nc.tensor.matmul(S.ps[:, 3, :], S.const("perm"), S.qk[:, m, :], start=True,
                                 stop=True).then_inc(s_perm, 1)

            pe.wait_ge(s_xlo, KT)
            for n in range(NWIN):
                pe.wait_ge(s_lo, n + 1)
                if n < NRW + NQK:
                    if n >= 3:
                        pe.wait_ge(s_out, n - 2)
                    for k in range(KT):
                        w = slice(k * P, (k + 1) * P)
                        last = three_pass(nc, S.ps[:, n % 3, :], w_hi[:, n % SPL, w], w_lo[:, n % SPL, w],
                                          xn_hi[:, k, :], xn_lo[:, k, :], k == 0, k == KT - 1)
                else:
                    kk = n - NRW - NQK
                    for t in range(TT):
                        x = slice(t * P, (t + 1) * P)
                        for j in range(2):
                            k, w = 2 * kk + j, slice(j * T, (j + 1) * T)
                            last = three_pass(nc, S.ps[:, 4 + t, :], xn_hi[:, k, x], xn_lo[:, k, x],
                                              w_hi[:, n % SPL, w], w_lo[:, n % SPL, w], k == 0, k == KT - 1)
                last.then_inc(s_mm, 1)
                if NRW < n < NRW + NQK + 1:
                    swap(n - 1 - NRW)


def attend(nc, S, dram):
    sem = S.sem
    with ExitStack() as ctx:
        def sb(name, shape, dt=F32):
            return ctx.enter_context(nc.sbuf_tensor(name, shape, dt))

        R4 = 4
        sm = sb("scores", [P, R4, T])
        pt = sb("probs_t", [P, 2, TT, T])
        mx = sb("row_max", [P, 32])
        nmx = sb("neg_max", [P, 32])
        den = sb("row_sum", [P, 32])
        rden = sb("row_inv", [P, 32])
        s_sc, s_bias, s_neg, s_exp, s_prob = sem("a_sc"), sem("a_bias"), sem("a_neg"), sem("a_exp"), sem("a_prob")
        s_tr, s_pt, s_pv, s_mix = sem("a_tr"), sem("a_pt"), sem("a_pv"), sem("a_mix")
        NU = 8 * TT
        block = ctx.enter_context(nc.Block())

        @block.tensor
        def _(pe):
            def scores(u):
                h, t = divmod(u, TT)
                rows = slice(HD * (h % 2), HD * (h % 2) + HD)
                if u >= 3:
                    pe.wait_ge(s_bias, u - 2)
                nc.tensor.matmul(S.ps[:, u % 3, 0:(t + 1) * P], S.qk[rows, h // 2, t * P:(t + 1) * P],
                                 S.qk[rows, 4 + h // 2, 0:(t + 1) * P], start=True, stop=True).then_inc(s_sc, 1)

            def turn(u):
                t = u % TT
                pe.wait_ge(s_prob, u + 1)
                if u >= 2:
                    pe.wait_ge(s_pt, u - 1)
                for j in range(t + 1):
                    last = nc.tensor.transpose(S.ps[:, 3 + u % 2, j * P:(j + 1) * P],
                                               sm[:, u % R4, j * P:(j + 1) * P], S.const("ident"))
                last.then_inc(s_tr, 1)

            def values(h):
                pe.wait_ge(s_pt, TT * (h + 1))
                if h >= 4 and h % 2 == 0:
                    pe.wait_ge(s_mix, h // 2 - 1)
                for j in range(TT):
                    last = nc.tensor.matmul(S.ps[HD * (h % 2):HD * (h % 2) + HD, 5 + (h // 2) % 2, j * P:T],
                                            S.v_tok[:, j, h * HD:(h + 1) * HD], pt[:, h % 2, j, j * P:T],
                                            start=j == 0, stop=j == TT - 1)
                last.then_inc(s_pv, 1)

            for i in range(NU + 3):
                if i < NU:
                    scores(i)
                if i >= 3:
                    turn(i - 3)
                    if (i - 3) % TT == 1 and i - 3 > TT:
                        values((i - 3) // TT - 1)
            values(7)

        @block.scalar
        def _(act):
            st = Steps(act, S.own_act, S.counts)

            def exps(u):
                t = u % TT
                act.wait_ge(s_neg, u + 1)
                st.do(act.activation(sm[:, u % R4, 0:(t + 1) * P], sm[:, u % R4, 0:(t + 1) * P], ACT.Exp,
                                     bias=nmx[:, u:u + 1], accum_out=den[:, u:u + 1]), s_exp)

            def take(u):
                h, t = divmod(u, TT)
                act.wait_ge(s_tr, u + 1)
                if h >= 2:
                    act.wait_ge(s_pv, h - 1)
                st.do(act.activation(pt[:, h % 2, 0:t + 1, t * P:(t + 1) * P],
                                     S.ps[:, 3 + u % 2, 0:(t + 1) * P].rearrange("p (j q) -> p j q", q=P), ACT.Copy),
                      s_pt)

            def pair(p):
                act.wait_ge(s_pv, 2 * p + 2)
                st.do(act.activation(S.mixed[:, HP + p, :], S.ps[:, 5 + p % 2, :], ACT.Copy), s_mix)

            for i in range(1, NU + 4):
                if i <= NU:
                    exps(i - 1)
                if i >= 4:
                    u = i - 4
                    take(u)
                    if u > 2 * TT and u % (2 * TT) == 2:
                        pair(u // (2 * TT) - 1)
            pair(HP - 1)

        @block.vector
        def _(dve):
            st = Steps(dve, S.own_dve, S.counts)
            v = nc.vector
            for i in range(NU + 2):
                u, w = i, i - 2
                if u < NU:
                    t = u % TT
                    dve.wait_ge(s_sc, u + 1)
                    if u >= R4:
                        dve.wait_ge(s_tr, u - R4 + 1)
                    st.do(v.scalar_tensor_tensor(sm[:, u % R4, 0:(t + 1) * P], S.ps[:, u % 3, 0:(t + 1) * P],
                                                 HD ** -0.5, S.const("attn_bias")[:, (TT - 1 - t) * P:], ALU.mult,
                                                 ALU.add), s_bias)
                if w >= 0:
                    dve.wait_ge(s_exp, w + 1)
                    st.do(v.reciprocal(rden[:, w:w + 1], den[:, w:w + 1]))
                st.settle()
                if u < NU:
                    st.do(v.tensor_reduce(mx[:, u:u + 1], sm[:, u % R4, 0:(t + 1) * P], AX, ALU.max))
                if w >= 0:
                    n = (w % TT + 1) * P
                    st.do(v.tensor_scalar(sm[:, w % R4, 0:n], sm[:, w % R4, 0:n], rden[:, w:w + 1], None, ALU.mult),
                          s_prob)
                if u < NU:
                    st.settle()
                    st.do(v.tensor_scalar(nmx[:, u:u + 1], mx[:, u:u + 1], -1.0, None, ALU.mult), s_neg)


def prepare(nc, S, dram):
    sem = S.sem
    with ExitStack() as ctx:
        def sb(name, shape, dt=F32):
            return ctx.enter_context(nc.sbuf_tensor(name, shape, dt))

        kk = sb("kk", [P, HP, T])
        nrm = sb("kk_norm", [P, HP, T])
        sw = sb("decay_rate", [P, HP, T])
        icl = sb("iclr", [P, HP, T])
        cum = sb("decay_sum", [P, HP, T])
        prev = sb("decay_prev", [P, HP, T])
        omka = sb("one_minus_k_a", [P, HP])
        R, K, V, WA, G = S.zm[:, 0:4, :], S.zm[:, 4:8, :], S.zm[:, 8:12, :], S.zm[:, 12, :], S.zm[:, 13, :]
        s_tanh, s_gsig, s_up, s_act, s_gate = sem("r_tanh"), sem("r_gsig"), sem("r_up"), sem("r_act"), sem("r_gate")
        s_ksq, s_ssum, s_nrm, s_cum, s_prev = sem("r_ksq"), sem("r_ssum"), sem("r_nrm"), sem("r_cum"), sem("r_prev")
        s_exp, s_rk, s_rsum, s_vtr, s_vt = sem("r_exp"), sem("r_rk"), sem("r_rsum"), sem("r_vtr"), sem("r_vt")
        s_pd = sem("r_pd")
        block = ctx.enter_context(nc.Block())

        @block.tensor
        def _(pe):
            for j in range(HP):
                for q in range(TT):
                    last = nc.tensor.transpose(S.ps[:, 4 + j, q * P:(q + 1) * P], V[:, j, q * P:(q + 1) * P],
                                               S.const("ident"))
                last.then_inc(s_vtr, 1)
            pe.wait_ge(s_tanh, 1)
            pe.wait_ge(s_gsig, 1)
            for j in range(HP):
                c = slice(j * P, (j + 1) * P)
                if j >= 1:
                    pe.wait_ge(s_act, 3 * j)
                nc.tensor.matmul(S.ps[:, 0, :], S.up[0:HD, 0, c], WA[0:HD, :], start=True, stop=True).then_inc(s_up, 1)
                nc.tensor.matmul(S.ps[:, 1, :], S.up[HD:P, 0, c], WA[HD:P, :], start=True, stop=True).then_inc(s_up, 1)
                nc.tensor.matmul(S.ps[:, 2, :], S.up[:, 1, c], G, start=True, stop=True).then_inc(s_up, 1)
            pe.wait_ge(s_ksq, 1)
            pe.wait_ge(s_vt, 4 * HP)
            for j in range(HP):
                nc.tensor.matmul(S.ps[:, 4 + j, :], S.const("block_ones"), nrm[:, j, :], start=True,
                                 stop=True).then_inc(s_ssum, 1)
            for j in range(HP):
                pe.wait_ge(s_rk, j + 1)
                pe.wait_ge(s_nrm, j + 1)
                nc.tensor.matmul(S.ps[:, 4 + j, :], S.const("block_ones"), cum[:, j, :], start=True,
                                 stop=True).then_inc(s_rsum, 1)

        @block.scalar
        def _(act):
            st = Steps(act, S.own_act, S.counts)
            st.do(act.activation(WA[0:HD, :], WA[0:HD, :], ACT.Tanh), s_tanh)
            st.do(act.activation(G, G, ACT.Sigmoid), s_gsig)
            for j in range(HP):
                act.wait_ge(s_up, 3 * j + 1)
                st.do(act.activation(sw[:, j, :], S.ps[:, 0, :], ACT.Sigmoid, bias=S.param("w0", j)), s_act)
                act.wait_ge(s_up, 3 * j + 2)
                st.do(act.activation(icl[:, j, :], S.ps[:, 1, :], ACT.Sigmoid, bias=S.param("a0", j)), s_act)
                act.wait_ge(s_up, 3 * j + 3)
                st.do(act.activation(S.gate[:, j, :], S.ps[:, 2, :], ACT.Copy), s_act)
            for j in range(HP):
                act.wait_ge(s_ssum, j + 1)
                if j == 0:
                    act.wait_ge(s_ssum, HP)
                st.do(act.activation(nrm[:, j, :], S.ps[:, 4 + j, :], ACT.Sqrt), s_nrm)
            act.wait_ge(s_cum, HP)
            act.wait_ge(s_prev, 1)
            st.do(act.activation(sw[:, :, :], cum[:, :, :], ACT.Exp, scale=-KAPPA), s_exp)
            st.do(act.activation(prev[:, :, :], prev[:, :, :], ACT.Exp, scale=-KAPPA), s_exp)
            st.do(act.activation(cum[:, :, :], cum[:, :, :], ACT.Exp, scale=KAPPA), s_exp)

        @block.gpsimd
        def _(pool):
            st = Steps(pool, S.own_pool, S.counts)
            st.do(pool.tensor_scalar(omka[:, :], S.param_all("k_a"), -1.0, 1.0, ALU.mult, ALU.add), s_pd)

        @block.vector
        def _(dve):
            st = Steps(dve, S.own_dve, S.counts)
            v = nc.vector
            for j in range(HP):
                st.do(v.tensor_scalar(kk[:, j, :], K[:, j, :], S.param("k_k", j), None, ALU.mult))
            st.settle()
            st.do(v.tensor_tensor(nrm[:, :, :], kk[:, :, :], kk[:, :, :], ALU.mult), s_ksq)
            for j in range(HP):
                dve.wait_ge(s_vtr, j + 1)
                turned = S.ps[:, 4 + j, :].rearrange("p (q c) -> p q c", c=P)
                for cp in range(2):
                    for hd in range(2):
                        st.do(v.tensor_copy(S.v_chunk[hd * C:(hd + 1) * C, :, j, :].rearrange(
                            "p (q e) i -> p q e i", e=2)[:, :, cp, :],
                            turned[cp * C:(cp + 1) * C, :, hd * HD:(hd + 1) * HD]), s_vt)
            dve.wait_ge(s_act, 3 * HP)
            for j in range(HP):
                st.do(v.tensor_tensor_scan(cum[:, j, :], S.const("keep"), sw[:, j, :], 0.0, ALU.mult, ALU.add), s_cum)
            st.settle()
            st.do(v.tensor_tensor(prev[:, :, :], cum[:, :, :], sw[:, :, :], ALU.subtract), s_prev)
            dve.wait_ge(s_nrm, HP)
            st.do(v.tensor_scalar(nrm[:, :, :], nrm[:, :, :], 1e-12, None, ALU.max))
            st.settle()
            st.do(v.reciprocal(nrm[:, :, :], nrm[:, :, :]))
            st.settle()
            st.do(v.tensor_tensor(kk[:, :, :], kk[:, :, :], nrm[:, :, :], ALU.mult))
            st.settle()
            dve.wait_ge(s_pd, 1)
            for j in range(HP):
                st.do(v.tensor_scalar(nrm[:, j, :], icl[:, j, :], S.param("k_a", j), omka[:, j:j + 1],
                                      ALU.mult, ALU.add))
            st.settle()
            st.do(v.tensor_tensor(K, K, nrm[:, :, :], ALU.mult))
            st.do(v.tensor_tensor(icl[:, :, :], icl[:, :, :], kk[:, :, :], ALU.mult))
            st.settle()
            dve.wait_ge(s_exp, 3)
            ra = S.ra[:, :, :, :, :]
            st.do(v.scalar_tensor_tensor(ra[:, :, :, 0, :].rearrange("p j n t -> p (j n) t"),
                                         kk[:, :, :].rearrange("p j (n t) -> p (j n) t", t=C), -1.0,
                                         prev[:, :, :].rearrange("p j (n t) -> p (j n) t", t=C), ALU.mult, ALU.mult))
            st.do(v.tensor_tensor(ra[:, :, :, 1, :].rearrange("p j n t -> p (j n) t"),
                                  R.rearrange("p j (n t) -> p (j n) t", t=C),
                                  sw[:, :, :].rearrange("p j (n t) -> p (j n) t", t=C), ALU.mult))
            st.do(v.tensor_tensor(S.bs[:, :, :], icl[:, :, :], cum[:, :, :], ALU.mult))
            st.do(v.tensor_tensor(S.ks[:, :, :], K, cum[:, :, :], ALU.mult))
            st.do(v.tensor_copy(S.pc[:, :, :], sw[:, :, :].rearrange("p j (n t) -> p j n t", t=C)[:, :, :, C - 1]))
            st.settle()
            for j in range(HP):
                st.do(v.scalar_tensor_tensor(cum[:, j, :], R[:, j, :], S.param("r_k", j), K[:, j, :],
                                             ALU.mult, ALU.mult), s_rk)
            for j in range(HP):
                dve.wait_ge(s_rsum, j + 1)
                st.do(v.tensor_tensor(R[:, j, :], S.ps[:, 4 + j, :], V[:, j, :], ALU.mult), s_gate)


def scan(nc, S, dram):
    sem = S.sem
    with ExitStack() as ctx:
        def sb(name, shape, dt=F32):
            return ctx.enter_context(nc.sbuf_tensor(name, shape, dt))

        HC = NCH // 2
        NB = HC // 2
        bbd = sb("b_bd", [P, HC, HP, P])
        kbd = sb("k_bd", [P, HC, HP, P])
        abd = sb("a_bd", [P, HC, HP, P])
        rbd = sb("r_bd", [P, HC, HP, P])
        aktbd = sb("akt_bd", [P, HC, HP, P])
        rbtbd = sb("rbt_bd", [P, HC, HP, P])
        rktbd = sb("rkt_bd", [P, HC, HP, P])
        btbd = sb("bt_bd", [P, HC, HP, P])
        ktbd = sb("kt_bd", [P, 2, HP, P])
        lbd = sb("l_bd", [P, HC, HP, P])
        tc = S.mixed[:, 0:2, :].rearrange("p a (c j t) -> p (a c) j t", c=2, j=HP)
        ttc = S.mixed[:, 2:4, :].rearrange("p a (c j t) -> p (a c) j t", c=2, j=HP)
        prod = sb("v_products", [P, HC, 3, HP, HD])
        xc = S.zm[:, 8:10, :].rearrange("p a (c j t) -> p (a c) j t", c=2, j=HP)
        st_s = S.zm[:, 10, :].rearrange("p (w j i) -> p w j i", w=2, j=HP)
        o1 = S.zm[:, 11, 0:HP * HD].rearrange("p (j i) -> p j i", j=HP)
        us = S.zm[:, 11, HP * HD:].rearrange("p (j i) -> p j i", j=HP)
        pre = S.zm[:, 12, 0:HP * HD].rearrange("p (j i) -> p j i", j=HP)
        s_zero, s_bd, s_bda, s_g, s_gev, s_tr, s_trev = (sem("s_zero"), sem("s_bd"), sem("s_bda"), sem("s_g"),
                                                         sem("s_gev"), sem("s_tr"), sem("s_trev"))
        s_pr, s_prev = sem("s_pr"), sem("s_prev")
        s_x, s_xbd, s_xc, s_y, s_tup, s_ttbd = (sem("s_x"), sem("s_xbd"), sem("s_xc"), sem("s_y"), sem("s_tup"),
                                                sem("s_ttbd"))
        s_o1, s_o1c, s_u, s_uc, s_s, s_snew, s_yo, s_yc = (sem("s_o1"), sem("s_o1c"), sem("s_u"), sem("s_uc"),
                                                           sem("s_s"), sem("s_snew"), sem("s_yo"), sem("s_yc"))
        NL = 6
        par = [slice(0, C), slice(C, P)]
        block = ctx.enter_context(nc.Block())
        yb = S.y_chunk
        flat = "p c j t -> p (c j) t"
        row = "p j t -> p (j t)"

        def compact(bank, n):
            return S.ps[:, bank, 0:n * HP * C].rearrange("p (c j t) -> p c j t", c=n, j=HP)

        @block.gpsimd
        def _(pool):
            st = Steps(pool, S.own_pool, S.counts)
            for buf in (bbd, kbd, lbd, rbtbd, aktbd, rktbd, abd, rbd):
                st.do(pool.memset(buf[:, :, :, :], 0.0), s_zero)
            st.do(pool.memset(st_s[:, 0, :, :], 0.0), s_zero)

        @block.tensor
        def _(pe):
            def products(ch):
                c = ch % HC
                pe.wait_ge(s_gev, 9 * (ch + 1))
                pe.wait_ge(s_trev, 2 * (ch + 1))
                if ch >= 1:
                    pe.wait_ge(s_prev, 3 * ch)
                for o, lhs in enumerate((aktbd[:, c], rktbd[:, c], ktbd[:, c % 2])):
                    for j in range(HP):
                        at = (o % 2) * HP * HD + j * HD
                        last = two_heads(nc, S.ps[:, 6 + o // 2, at:at + HD], lhs[:, j, :], S.v_chunk[:, ch, j, :])
                last.then_inc(s_pr, 1)

            for half in range(2):
                pe.wait_ge(s_bd, 4 * (half + 1))
                if half:
                    pe.wait_ge(s_yc, HC)
                    pe.wait_ge(s_snew, 2 * HC)
                for c in range(HC):
                    ch = half * HC + c
                    if ch >= 2:
                        pe.wait_ge(s_gev, 9 * (ch - 1))
                    for j in range(HP):
                        nc.tensor.matmul(S.ps[:, c % 2, j * P:(j + 1) * P], bbd[:, c, j, :],
                                         S.ra[:, j, ch, :, :].rearrange("p w t -> p (w t)"), start=True, stop=True)
                    for j in range(HP):
                        last = nc.tensor.matmul(S.ps[:, 2 + c % 2, j * P:(j + 1) * P], kbd[:, c, j, :],
                                                S.ra[:, j, ch, :, :].rearrange("p w t -> p (w t)"),
                                                start=True, stop=True)
                    last.then_inc(s_g, 1)
                    if ch >= 1:
                        pe.wait_ge(s_trev, 2 * ch)
                    for j in range(HP):
                        nc.tensor.transpose(S.ps[:, 4, j * P:(j + 1) * P], bbd[:, c, j, :], S.const("ident"))
                    for j in range(HP):
                        last = nc.tensor.transpose(S.ps[:, 5, j * P:(j + 1) * P], kbd[:, c, j, :], S.const("ident"))
                    last.then_inc(s_tr, 1)
                    if c:
                        products(ch - 1)
                products(half * HC + HC - 1)
                for level in range(NL):
                    n = half * NL + level
                    for b in range(NB):
                        if level:
                            pe.wait_ge(s_tup, NB * (n - 1) + b + 1)
                        for c in (2 * b, 2 * b + 1):
                            for j in range(HP):
                                rhs = tc[:, c, j, :] if level else S.const("eye_compact")
                                last = two_heads(nc, compact(b, 2)[:, c % 2, j, :], lbd[:, c, j, :], rhs)
                        last.then_inc(s_x, 1)
                    if level == 0:
                        continue
                    for b in range(NB):
                        pe.wait_ge(s_xbd, 2 * (NB * (half * (NL - 1) + level - 1) + b + 1))
                        pe.wait_ge(s_ttbd, 2 * (NB * (n - 1) + b + 1))
                        for c in (2 * b, 2 * b + 1):
                            for j in range(HP):
                                if level < NL - 1:
                                    two_heads(nc, compact(2 + b, 2)[:, c % 2, j, :], kbd[:, c, j, :], xc[:, c, j, :])
                                last = two_heads(nc, compact(4 + b, 2)[:, c % 2, j, :], bbd[:, c, j, :],
                                                 ttc[:, c, j, :])
                        last.then_inc(s_y, 1)
                pe.wait_ge(s_ttbd, 2 * NB * NL * (half + 1))
                pe.wait_ge(s_bda, 4 * (half + 1))
                for c in range(HC):
                    ch = half * HC + c
                    if ch:
                        pe.wait_ge(s_snew, 2 * ch)
                    for j in range(HP):
                        last = two_heads(nc, S.ps[:, 0, j * HD:(j + 1) * HD], abd[:, c, j, :], st_s[:, ch % 2, j, :])
                    last.then_inc(s_o1, 1)
                    pe.wait_ge(s_o1c, ch + 1)
                    for j in range(HP):
                        last = two_heads(nc, S.ps[:, 1, j * HD:(j + 1) * HD], kbd[:, c, j, :], o1[:, j, :])
                    last.then_inc(s_u, 1)
                    pe.wait_ge(s_uc, ch + 1)
                    for j in range(HP):
                        last = two_heads(nc, S.ps[:, 4, j * HD:(j + 1) * HD], btbd[:, c, j, :], us[:, j, :])
                    last.then_inc(s_s, 1)
                    if ch >= 2:
                        pe.wait_ge(s_yc, ch - 1)
                    for j in range(HP):
                        o = S.ps[:, 2 + ch % 2, j * HD:(j + 1) * HD]
                        for e in range(2):
                            h = slice(e * HD, (e + 1) * HD)
                            nc.tensor.matmul(o[h], rbd[:, c, j, h], st_s[:, ch % 2, j, :], start=True, stop=False)
                            last = nc.tensor.matmul(o[h], rbtbd[:, c, j, h], us[:, j, :], start=False, stop=True)
                    last.then_inc(s_yo, 1)

        @block.scalar
        def _(act):
            st = Steps(act, S.own_act, S.counts)
            for half in range(2):
                chunks = slice(half * HC, (half + 1) * HC)
                def take_products(ch):
                    act.wait_ge(s_pr, ch + 1)
                    c = ch % HC
                    for o in range(3):
                        at = (o % 2) * HP * HD
                        st.do(act.activation(prod[:, c, o, :, :].rearrange(row),
                                             S.ps[:, 6 + o // 2, at:at + HP * HD], ACT.Copy), s_prev)

                if half:
                    act.wait_ge(s_yo, HC)
                    act.wait_ge(s_yc, HC)
                    act.wait_ge(s_snew, 2 * HC)
                for c in range(HC):
                    ch = half * HC + c
                    act.wait_ge(s_tr, ch + 1)
                    if c >= 2:
                        act.wait_ge(s_pr, ch - 1)
                    for dst, bank in ((btbd[:, c], 4), (ktbd[:, c % 2], 5)):
                        st.do(act.activation(dst.rearrange(row), S.ps[:, bank, :], ACT.Copy), s_trev)
                    if c:
                        take_products(ch - 1)
                take_products(half * HC + HC - 1)
                act.wait_ge(s_zero, 9)
                for w, dst in ((0, abd), (1, rbd)):
                    for e in range(2):
                        st.do(act.activation(dst[par[e], :, :, par[e]],
                                             S.ra[par[e], :, chunks, w, :].rearrange("p j c t -> p c j t"),
                                             ACT.Copy), s_bda)
                for level in range(NL):
                    n = half * NL + level
                    for b in range(NB):
                        cs = slice(2 * b, 2 * b + 2)
                        if level:
                            act.wait_ge(s_xc, NB * n + b + 1)
                            for e in range(2):
                                st.do(act.activation(bbd[par[e], cs, :, par[e]], xc[par[e], cs, :, :], ACT.Copy), s_xbd)
                    for b in range(NB):
                        cs = slice(2 * b, 2 * b + 2)
                        act.wait_ge(s_tup, NB * n + b + 1)
                        for e in range(2):
                            st.do(act.activation(kbd[par[e], cs, :, par[e]], ttc[par[e], cs, :, :], ACT.Copy), s_ttbd)
                for c in range(HC):
                    ch = half * HC + c
                    act.wait_ge(s_u, ch + 1)
                    st.do(act.activation(us[:, :, :].rearrange(row), S.ps[:, 1, 0:HP * HD], ACT.Copy), s_uc)

        @block.vector
        def _(dve):
            st = Steps(dve, S.own_dve, S.counts)
            v = nc.vector
            for half in range(2):
                if half:
                    dve.wait_ge(s_yo, HC)
                for i, (dst, src) in enumerate(((bbd, S.bs), (kbd, S.ks))):
                    if not half:
                        dve.wait_ge(s_zero, i + 1)
                    for e in range(2):
                        st.do(v.tensor_copy(dst[par[e], :, :, par[e]],
                                            src[par[e], :, half * HC * C:(half + 1) * HC * C].rearrange(
                                                "p j (c t) -> p c j t", t=C)), s_bd)
                for c in range(HC):
                    ch = half * HC + c
                    dve.wait_ge(s_g, ch + 1)
                    g1 = S.ps[:, c % 2, :].rearrange("p (j w t) -> p j w t", j=HP, w=2)
                    g2 = S.ps[:, 2 + c % 2, :].rearrange("p (j w t) -> p j w t", j=HP, w=2)
                    st.do(v.tensor_tensor(ttc[:, c, :, :], g1[:, :, 0, :], bc(S.const("level0_t"), 1, HP), ALU.mult),
                          s_gev)
                    for i, (dst, src, w, m) in enumerate(((lbd, g1, 0, "strict"), (rbtbd, g1, 1, "inclusive"),
                                                          (aktbd, g2, 0, "strict"), (rktbd, g2, 1, "inclusive"))):
                        if not ch:
                            dve.wait_ge(s_zero, 3 + i)
                        for e in range(2):
                            st.do(v.tensor_tensor(dst[par[e], c, :, par[e]], src[par[e], :, w, :],
                                                  bc(S.const(m)[par[e], :], 1, HP), ALU.mult), s_gev)
                eye = bc(S.const("eye_compact"), 1, 2 * HP)
                for level in range(NL):
                    n = half * NL + level
                    ny = half * (NL - 1) + level
                    mask = bc(S.const(f"level{level}"), 1, 2 * HP)
                    for b in range(NB):
                        cs = slice(2 * b, 2 * b + 2)
                        dve.wait_ge(s_x, NB * n + b + 1)
                        to = xc if level else tc
                        st.do(v.tensor_tensor(to[:, cs, :, :].rearrange(flat), compact(b, 2).rearrange(flat), mask,
                                              ALU.mult), s_xc)
                    if level == 0:
                        st.settle()
                        for b in range(NB):
                            cs = slice(2 * b, 2 * b + 2)
                            for k, m in enumerate((tc, ttc)):
                                st.do(v.tensor_tensor(m[:, cs, :, :].rearrange(flat), m[:, cs, :, :].rearrange(flat),
                                                      eye, ALU.add), s_tup if k else None)
                        continue
                    for b in range(NB):
                        cs = slice(2 * b, 2 * b + 2)
                        dve.wait_ge(s_y, NB * (ny - 1) + b + 1)
                        if level < NL - 1:
                            st.do(v.tensor_tensor(tc[:, cs, :, :], tc[:, cs, :, :], compact(2 + b, 2), ALU.add))
                        st.do(v.tensor_tensor(ttc[:, cs, :, :], ttc[:, cs, :, :], compact(4 + b, 2), ALU.add), s_tup)
                if not half:
                    dve.wait_ge(s_zero, 9)
                dve.wait_ge(s_prev, 3 * HC * (half + 1))

                def take_y(ch):
                    dve.wait_ge(s_yo, ch + 1)
                    st.do(v.tensor_tensor(yb[:, ch, :, :].rearrange(row), S.ps[:, 2 + ch % 2, 0:HP * HD],
                                          prod[:, ch % HC, 1, :, :].rearrange(row), ALU.add), s_yc)

                for c in range(HC):
                    ch = half * HC + c
                    old, new = st_s[:, ch % 2, :, :], st_s[:, (ch + 1) % 2, :, :]
                    dve.wait_ge(s_o1, ch + 1)
                    st.do(v.tensor_tensor(o1[:, :, :].rearrange(row), S.ps[:, 0, 0:HP * HD],
                                          prod[:, c, 0, :, :].rearrange(row), ALU.add), s_o1c)
                    st.do(v.tensor_tensor(pre, old, prod[:, c, 2, :, :], ALU.add))
                    if c:
                        take_y(ch - 1)
                    st.settle()
                    dve.wait_ge(s_s, ch + 1)
                    st.do(v.tensor_tensor(new.rearrange(row), pre.rearrange(row), S.ps[:, 4, 0:HP * HD], ALU.add),
                          s_snew)
                    st.settle()
                    st.do(v.tensor_tensor(new, new, bc(S.pc[:, :, ch], 2, HD), ALU.mult), s_snew)
                    st.settle()
                take_y(half * HC + HC - 1)


def normalise_heads(nc, S, dram):
    sem = S.sem
    with ExitStack() as ctx:
        def sb(name, shape, dt=F32):
            return ctx.enter_context(nc.sbuf_tensor(name, shape, dt))

        sq = sb("y_sq", [P, NCH * HP, HD])
        mean = sb("y_mean", [P, NCH * HP])
        var = sb("y_var", [P, NCH * HP])
        s_var, s_std, s_y, s_tr, s_cp = sem("n_var"), sem("n_std"), sem("n_y"), sem("n_tr"), sem("n_cp")
        block = ctx.enter_context(nc.Block())
        y = S.y_chunk[:, :, :, :].rearrange("p c j i -> p (c j) i")
        M = S.mixed

        @block.vector
        def _(dve):
            st = Steps(dve, S.own_dve, S.counts)
            v = nc.vector
            st.do(v.tensor_reduce(mean[:, :], y, AX, ALU.add))
            st.settle()
            st.do(v.tensor_scalar(mean[:, :], mean[:, :], 1.0 / HD, None, ALU.mult))
            st.settle()
            st.do(v.tensor_tensor(y, y, bc(mean[:, :], 2, HD), ALU.subtract))
            st.settle()
            st.do(v.tensor_tensor(sq[:, :, :], y, y, ALU.mult))
            st.settle()
            st.do(v.tensor_reduce(var[:, :], sq[:, :, :], AX, ALU.add))
            st.settle()
            st.do(v.tensor_scalar(var[:, :], var[:, :], 1.0 / HD, GN_EPS, ALU.mult, ALU.add))
            st.settle()
            st.do(v.reciprocal(var[:, :], var[:, :]), s_var)
            dve.wait_ge(s_std, 1)
            st.do(v.tensor_tensor(y, y, bc(var[:, :], 2, HD), ALU.mult), s_y)
            for a in range(2):
                for q in range(2):
                    dve.wait_ge(s_tr, 2 * a + q + 1)
                    src = S.ps[:, 2 * a + q, :].rearrange("p (c h t) -> p c h t", c=4, h=2)
                    for pp in range(2):
                        for h in range(2):
                            st.do(v.tensor_copy(
                                M[h * HD:(h + 1) * HD, 2 * a + pp, q * 256:(q + 1) * 256].rearrange(
                                    "p (c t) -> p c t", t=C), src[pp * HD:(pp + 1) * HD, :, h, :]))
            st.settle()
            for j in range(HP):
                st.do(v.tensor_scalar(M[:, j, :], M[:, j, :], S.param("gn_w", j), S.param("gn_b", j),
                                      ALU.mult, ALU.add))
            st.settle()
            st.do(v.tensor_tensor(M[:, 0:HP, :], M[:, 0:HP, :], S.zm[:, 0:HP, :], ALU.add))
            st.settle()
            st.do(v.tensor_tensor(M[:, 0:HP, :], M[:, 0:HP, :], S.gate[:, :, :], ALU.mult))

        @block.scalar
        def _(act):
            st = Steps(act, S.own_act, S.counts)
            act.wait_ge(s_var, 1)
            st.do(act.activation(var[:, :], var[:, :], ACT.Sqrt), s_std)

        @block.tensor
        def _(pe):
            pe.wait_ge(s_y, 1)
            for a in range(2):
                for q in range(2):
                    for c in range(4):
                        last = nc.tensor.transpose(
                            S.ps[:, 2 * a + q, c * P:(c + 1) * P],
                            S.y_chunk[:, 4 * q + c, 2 * a:2 * a + 2, :].rearrange("p j i -> p (j i)"),
                            S.const("ident"))
                    last.then_inc(s_tr, 1)


def mix(nc, S, dram):
    sem = S.sem
    with ExitStack() as ctx:
        def sb(name, shape, dt=F32):
            return ctx.enter_context(nc.sbuf_tensor(name, shape, dt))

        mx_hi = sb("mixed_hi", [P, KT, T], F32R)
        mx_lo = sb("mixed_lo", [P, KT, T], F32R)
        raw = sb("wout_raw", [P, 4, D])
        w_hi = sb("wout_hi", [P, SPL, D], F32R)
        w_lo = sb("wout_lo", [P, SPL, D], F32R)
        xs = sb("h_scaled", [P, TT, D])
        sq = sb("h_sq", [P, D])
        ss = sb("h_ss", [P, TT])
        s_x = sem("m_x")
        s_raw = [sem(f"m_raw{i}") for i in range(4)]
        s_mhi, s_mlo, s_hi, s_lo, s_mm, s_res = (sem("m_mhi"), sem("m_mlo"), sem("m_hi"), sem("m_lo"),
                                                 sem("m_mm"), sem("m_res"))
        s_ss, s_var, s_std, s_sc, s_tr, s_thi, s_tlo = (sem("m_ss"), sem("m_var"), sem("m_std"), sem("m_sc"),
                                                        sem("m_tr"), sem("m_thi"), sem("m_tlo"))
        block = ctx.enter_context(nc.Block())

        @block.sync
        def _(sp):
            sp.dma_start(S.h[:, :, :], dram["x"]).then_inc(s_x, 16)
            for k in range(KT):
                if k >= 4:
                    sp.wait_ge(s_lo, k - 3)
                sp.dma_start(raw[:, k % 4, :], dram["wout"][k]).then_inc(s_raw[k % 4], 16)

        @block.scalar
        def _(act):
            st = Steps(act, S.own_act, S.counts)
            for k in range(KT):
                st.do(act.activation(mx_hi[:, k, :], S.mixed[:, k, :], ACT.Copy), s_mhi)
                act.wait_ge(s_raw[k % 4], 16 * (k // 4 + 1))
                if k >= SPL:
                    act.wait_ge(s_mm, k - SPL + 1)
                st.do(act.activation(w_hi[:, k % SPL, :], raw[:, k % 4, :], ACT.Copy), s_hi)
            for t in range(TT):
                act.wait_ge(s_res, 2 * t + 2)
                if t:
                    st.settle()
                st.do(act.activation(sq[:, :], S.h[:, t, :], ACT.Square, accum_out=ss[:, t:t + 1]), s_ss)
            act.wait_ge(s_var, 1)
            st.do(act.activation(ss[:, :], ss[:, :], ACT.Sqrt), s_std)
            for k in range(KT):
                act.wait_ge(s_tr, k + 1)
                st.do(act.activation(S.xn_hi[:, k, :], S.ps[:, k, :], ACT.Copy, scale=S.param("g_ffn", k)), s_thi)

        @block.vector
        def _(dve):
            st = Steps(dve, S.own_dve, S.counts)
            v = nc.vector
            for k in range(KT):
                dve.wait_ge(s_mhi, k + 1)
                st.do(v.tensor_tensor(mx_lo[:, k, :], S.mixed[:, k, :], mx_hi[:, k, :].bitcast(F32), ALU.subtract),
                      s_mlo)
                dve.wait_ge(s_hi, k + 1)
                st.do(v.tensor_tensor(w_lo[:, k % SPL, :], raw[:, k % 4, :], w_hi[:, k % SPL, :].bitcast(F32),
                                      ALU.subtract), s_lo)
            dve.wait_ge(s_x, 16)
            dve.wait_ge(s_mm, KT)
            for o in range(8):
                t, d = divmod(o, 2)
                st.do(v.tensor_tensor(S.h[:, t, d * T:(d + 1) * T], S.h[:, t, d * T:(d + 1) * T], S.ps[:, o, :],
                                      ALU.add), s_res)
            dve.wait_ge(s_ss, TT)
            st.do(v.tensor_scalar(ss[:, :], ss[:, :], 1.0 / D, RMS_EPS, ALU.mult, ALU.add))
            st.settle()
            st.do(v.reciprocal(ss[:, :], ss[:, :]), s_var)
            dve.wait_ge(s_std, 1)
            for t in range(TT):
                st.do(v.tensor_scalar(xs[:, t, :], S.h[:, t, :], ss[:, t:t + 1], None, ALU.mult), s_sc)
            for k in range(KT):
                dve.wait_ge(s_thi, k + 1)
                st.do(v.scalar_tensor_tensor(S.xn_lo[:, k, :], S.ps[:, k, :], S.param("g_ffn", k),
                                             S.xn_hi[:, k, :].bitcast(F32), ALU.mult, ALU.subtract), s_tlo)

        @block.tensor
        def _(pe):
            for k in range(KT):
                pe.wait_ge(s_mlo, k + 1)
                pe.wait_ge(s_lo, k + 1)
                for o in range(8):
                    t, d = divmod(o, 2)
                    x, w = slice(t * P, (t + 1) * P), slice(d * T, (d + 1) * T)
                    last = three_pass(nc, S.ps[:, o, :], mx_hi[:, k, x], mx_lo[:, k, x], w_hi[:, k % SPL, w],
                                      w_lo[:, k % SPL, w], k == 0, k == KT - 1)
                last.then_inc(s_mm, 1)
            pe.wait_ge(s_res, 8)
            pe.wait_ge(s_sc, TT)
            for k in range(KT):
                for t in range(TT):
                    last = nc.tensor.transpose(S.ps[:, k, t * P:(t + 1) * P], xs[:, t, k * P:(k + 1) * P],
                                               S.const("ident"))
                last.then_inc(s_tr, 1)


def route(nc, S, dram):
    sem = S.sem
    NQ = 2 * PH
    with ExitStack() as ctx:
        def sb(name, shape, dt=F32):
            return ctx.enter_context(nc.sbuf_tensor(name, shape, dt))

        raw = sb("wq_raw", [P, RAW, D])
        w_hi = sb("wq_hi", [P, SPL, D], F32R)
        w_lo = sb("wq_lo", [P, SPL, D], F32R)
        keys = sb("sub_keys", [P, 2, NKEY])
        qt = sb("q_t", [P, 4, T])
        sc = sb("key_scores", [P, 2, TT, 2, NKEY])
        sc2 = sb("key_scores_left", [P, TT, 2, NKEY])
        top = sb("top_scores", [P, TT, PH, 2, TOPK])
        topi = sb("top_index", [P, TT, PH, 2, TOPK], U32)
        topf = sb("top_index_f", [P, TT, PH, 2, TOPK])
        cand = sb("cand", [P, TT, NCAND])
        cand2 = sb("cand_left", [P, TT, NCAND])
        best = sb("best", [P, TT, PH, TOPK])
        pos = sb("pos", [P, TT, PH, TOPK], U32)
        bits = sb("pos_bits", [P, 2, TT * PH * TOPK], U32)
        posf = sb("pos_f", [P, 3, TT * PH * TOPK])
        small = sb("small", [P, TT * PH])
        delta = sb("delta", [P, TT, PH, TOPK])
        wide = sb("wide", [P, PH * TOPK, TOPK])
        widej = sb("wide_j", [P, PH * TOPK, TOPK])
        tab = S.mixed[:, 0:3, :].rearrange("p w (t k) -> p w t k", k=PH * TOPK)
        s_k = sem("q_k")
        s_raw = [sem(f"q_raw{i}") for i in range(RAW)]
        s_hi, s_lo, s_mm, s_q, s_s, s_sev, s_top = (sem("q_hi"), sem("q_lo"), sem("q_mm"), sem("q_q"), sem("q_s"),
                                                    sem("q_sev"), sem("q_top"))
        s_sub, s_e, s_b, s_j, s_jr, s_tab, s_tr, s_out = (sem("q_sub"), sem("q_e"), sem("q_b"), sem("q_j"),
                                                          sem("q_jr"), sem("q_tab"), sem("q_tr"), sem("q_out"))
        block = ctx.enter_context(nc.Block())

        @block.sync
        def _(sp):
            sp.dma_start(keys[:, :, :], dram["keys_t"]).then_inc(s_k, 16)
            for n in range(NQ):
                if n >= RAW:
                    sp.wait_ge(s_lo, n - RAW + 1)
                sp.dma_start(raw[:, n % RAW, :], dram["wq_t"][n]).then_inc(s_raw[n % RAW], 16)

        @block.gpsimd
        def _(pool):
            st = Steps(pool, S.own_pool, S.counts)
            for n in range(NQ):
                pool.wait_ge(s_hi, n + 1)
                st.do(pool.tensor_tensor(w_lo[:, n % SPL, :], raw[:, n % RAW, :], w_hi[:, n % SPL, :].bitcast(F32),
                                         ALU.subtract), s_lo)

        @block.scalar
        def _(act):
            st = Steps(act, S.own_act, S.counts)

            def take_q(n):
                act.wait_ge(s_mm, n + 1)
                if n >= 4:
                    act.wait_ge(s_s, n // 2 - 1)
                st.do(act.activation(qt[:, n % 4, :], S.ps[:, n % 3, :], ACT.Copy), s_q)

            def take_scores(h):
                act.wait_ge(s_s, h + 1)
                if h >= 2:
                    act.wait_ge(s_top, h - 1)
                for c in range(2):
                    st.do(act.activation(sc[:, h % 2, :, c, :],
                                         S.ps[:, 3 + c, :].rearrange("p (t k) -> p t k", k=NKEY), ACT.Copy), s_sev)

            for n in range(NQ):
                act.wait_ge(s_raw[n % RAW], 16 * (n // RAW + 1))
                if n >= SPL:
                    act.wait_ge(s_mm, n - SPL + 1)
                st.do(act.activation(w_hi[:, n % SPL, :], raw[:, n % RAW, :], ACT.Copy), s_hi)
                if n >= 1:
                    take_q(n - 1)
                if n >= 4 and n % 2 == 0:
                    take_scores(n // 2 - 2)
            take_q(NQ - 1)
            take_scores(PH - 2)
            take_scores(PH - 1)
            act.wait_ge(s_sub, 1)
            st.do(act.activation(best[:, :, :, :], best[:, :, :, :], ACT.Exp), s_e)
            for w in range(3):
                act.wait_ge(s_tr, w + 1)
                st.do(act.activation(S.tab[:, w, :], S.ps[:, w, :], ACT.Copy), s_out)

        @block.tensor
        def _(pe):
            pe.wait_ge(s_k, 16)

            def scores(h):
                pe.wait_ge(s_q, 2 * h + 2)
                if h >= 1:
                    pe.wait_ge(s_sev, 2 * h)
                for c in range(2):
                    for t in range(TT):
                        last = nc.tensor.matmul(S.ps[:, 3 + c, t * P:(t + 1) * P],
                                                qt[:, (2 * h + c) % 4, t * P:(t + 1) * P], keys[:, c, :],
                                                start=True, stop=True)
                last.then_inc(s_s, 1)

            for n in range(NQ):
                pe.wait_ge(s_lo, n + 1)
                if n >= 3:
                    pe.wait_ge(s_q, n - 2)
                for k in range(KT):
                    w = slice(k * P, (k + 1) * P)
                    last = three_pass(nc, S.ps[:, n % 3, :], w_hi[:, n % SPL, w], w_lo[:, n % SPL, w],
                                      S.xn_hi[:, k, :], S.xn_lo[:, k, :], k == 0, k == KT - 1)
                last.then_inc(s_mm, 1)
                if n >= 2 and n % 2 == 0:
                    scores(n // 2 - 1)
            scores(PH - 1)
            pe.wait_ge(s_q, NQ)
            for w in range(3):
                pe.wait_ge(*((s_tab, 1), (s_jr, TT), (s_tab, 2))[w])
                for t in range(TT):
                    last = nc.tensor.transpose(S.ps[:, w, t * P:(t + 1) * P], tab[:, w, t, :], S.const("ident"))
                last.then_inc(s_tr, 1)

        @block.vector
        def _(dve):
            st = Steps(dve, S.own_dve, S.counts)
            v = nc.vector
            both = [(t, c) for t in range(TT) for c in range(2)]
            for h in range(PH):
                dve.wait_ge(s_sev, 2 * h + 2)
                for t, c in both:
                    st.do(v.max(top[:, t, h, c, 0:8], sc[:, h % 2, t, c, :]))
                st.settle()
                for t, c in both:
                    st.do(v.max_index(topi[:, t, h, c, 0:8], top[:, t, h, c, 0:8], sc[:, h % 2, t, c, :]))
                    st.do(v.match_replace(sc2[:, t, c, :], top[:, t, h, c, 0:8], sc[:, h % 2, t, c, :], LOWEST))
                st.settle()
                for t, c in both:
                    st.do(v.max(top[:, t, h, c, 8:16], sc2[:, t, c, :]))
                st.settle()
                for t, c in both:
                    st.do(v.max_index(topi[:, t, h, c, 8:16], top[:, t, h, c, 8:16], sc2[:, t, c, :]))
                s0, s1 = top[:, :, h, 0, :], top[:, :, h, 1, :]
                for lo, a0, na, nb in ((0, 0, 1, 16), (16, 1, 3, 8), (40, 4, 4, 4), (56, 8, 8, 1)):
                    out = cand[:, :, lo:lo + na * nb].rearrange("p t (a b) -> p t a b", b=nb)
                    st.do(v.tensor_tensor(out, bc(s0[:, :, a0:a0 + na], 3, nb), bc(s1[:, :, 0:nb], 2, na), ALU.add))
                st.settle()
                for t in range(TT):
                    st.do(v.max(best[:, t, h, 0:8], cand[:, t, :]))
                st.settle()
                for t in range(TT):
                    st.do(v.max_index(pos[:, t, h, 0:8], best[:, t, h, 0:8], cand[:, t, :]))
                    st.do(v.match_replace(cand2[:, t, :], best[:, t, h, 0:8], cand[:, t, :], LOWEST))
                st.settle()
                for t in range(TT):
                    st.do(v.max(best[:, t, h, 8:16], cand2[:, t, :]))
                st.settle()
                for t in range(TT):
                    last = v.max_index(pos[:, t, h, 8:16], best[:, t, h, 8:16], cand2[:, t, :])
                    st.do(last, s_top if t == TT - 1 else None)
                st.settle()
            st.do(v.tensor_copy(small[:, :].rearrange("p (t h) -> p t h", h=PH), best[:, :, :, 0]))
            st.do(v.tensor_copy(topf[:, :, :, :, :], topi[:, :, :, :, :]))
            p32 = pos[:, :, :, :].rearrange("p t h k -> p (t h k)")
            st.do(v.tensor_scalar(bits[:, 0, :], p32, 7, None, ALU.bitwise_and))
            st.do(v.tensor_scalar(bits[:, 1, :], p32, 3, None, ALU.bitwise_and))
            st.do(v.tensor_copy(posf[:, 0, :], p32))
            st.settle()
            bst = best[:, :, :, :].rearrange("p t h k -> p (t h) k")
            st.do(v.tensor_tensor(bst, bst, bc(small[:, :], 2, TOPK), ALU.subtract), s_sub)
            st.do(v.tensor_copy(posf[:, 1, :], bits[:, 0, :]))
            st.do(v.tensor_copy(posf[:, 2, :], bits[:, 1, :]))
            st.do(v.tensor_tensor(delta[:, :, :, 1:TOPK], topf[:, :, :, 0, 1:TOPK], topf[:, :, :, 0, 0:TOPK - 1],
                                  ALU.subtract))
            st.settle()
            for t in range(TT):
                p_t = posf[:, 0, t * P:(t + 1) * P]
                w15 = wide[:, :, 0:TOPK - 1]
                st.do(v.tensor_tensor(w15, bc(p_t, 2, TOPK - 1), bc(S.const("row_starts"), 1, P), ALU.is_ge))
                st.settle()
                w4 = w15.rearrange("p (h k) b -> p h k b", h=PH)
                st.do(v.tensor_tensor(w4, w4, bc(delta[:, t, :, 1:TOPK], 2, TOPK), ALU.mult))
                st.settle()
                st.do(v.tensor_reduce(tab[:, 0, t, :], w15, AX, ALU.add))
                st.settle()
            row0 = topf[:, :, :, 0, 0]
            t0 = tab[:, 0, :, :].rearrange("p t (h k) -> p t h k", h=PH)
            st.do(v.tensor_tensor(t0, t0, bc(row0, 3, TOPK), ALU.add), s_tab)
            st.do(v.tensor_tensor(posf[:, 2, :], posf[:, 2, :], posf[:, 1, :], ALU.subtract))
            st.do(v.tensor_scalar(bits[:, 0, :].bitcast(F32), posf[:, 0, :], 16.0, None, ALU.is_lt))
            st.settle()
            lt16 = bits[:, 0, :].bitcast(F32)
            acc = bits[:, 1, :].bitcast(F32)
            st.do(v.scalar_tensor_tensor(acc, posf[:, 0, :], 40.0, posf[:, 2, :], ALU.is_ge, ALU.mult))
            st.settle()
            st.do(v.tensor_tensor(acc, acc, posf[:, 1, :], ALU.add))
            st.settle()
            st.do(v.scalar_tensor_tensor(acc, posf[:, 0, :], 56.0, acc, ALU.is_lt, ALU.mult))
            st.settle()
            st.do(v.tensor_tensor(posf[:, 1, :], posf[:, 0, :], acc, ALU.subtract))
            st.settle()
            st.do(v.tensor_tensor(posf[:, 1, :], posf[:, 1, :], lt16, ALU.mult))
            st.settle()
            st.do(v.tensor_tensor(posf[:, 0, :], posf[:, 1, :], acc, ALU.add), s_b)
            st.settle()
            for t in range(TT):
                wj = (wide, widej)[t % 2]
                st.do(v.tensor_tensor(wj[:, :, :], bc(S.const("iota")[:, 0:TOPK], 1, P),
                                      bc(posf[:, 0, t * P:(t + 1) * P], 2, TOPK), ALU.is_equal))
                st.settle()
                w4 = wj[:, :, :].rearrange("p (h k) b -> p h k b", h=PH)
                st.do(v.tensor_tensor(w4, w4, bc(topf[:, t, :, 1, :], 2, TOPK), ALU.mult))
                st.settle()
                st.do(v.tensor_reduce(tab[:, 1, t, :], wj[:, :, :], AX, ALU.add), s_jr)
            dve.wait_ge(s_e, 1)
            st.do(v.tensor_reduce(small[:, :], bst, AX, ALU.add))
            st.settle()
            st.do(v.reciprocal(small[:, :], small[:, :]))
            st.settle()
            st.do(v.tensor_tensor(tab[:, 2, :, :].rearrange("p t (h k) -> p (t h) k", h=PH), bst,
                                  bc(small[:, :], 2, TOPK), ALU.mult), s_tab)


def spread(nc, S, dram):
    sem = S.sem
    Q = 8
    R = 4
    NQ = SW // Q
    with ExitStack() as ctx:
        def sb(name, shape, dt=F32):
            return ctx.enter_context(nc.sbuf_tensor(name, shape, dt))

        rows = [sb(f"onehot_rows{i}", [P, Q, NKEY]) for i in range(R)]
        cols = [sb(f"gated_cols{i}", [P, Q, NKEY]) for i in range(R)]
        stage = [sb(f"gate_stage{i}", [P, NKEY, SW]) for i in range(2)]
        s_onehot, s_rows, s_cols = sem("w_onehot"), sem("w_rows"), sem("w_cols")
        s_used, s_taken = sem("w_used"), sem("w_taken")
        s_out = [sem(f"w_out{i}") for i in range(2)]
        block = ctx.enter_context(nc.Block())
        tab = S.tab
        iota = bc(S.const("iota"), 1, Q)

        def steps(eng, s, step):
            with eng.Fori(0, NQ // R) as i:
                for e in range(R):
                    step(s * NQ + R * i + e, e, (R * i + e) * Q)


        @block.vector
        def _(dve):
            for s in range(NSW):
                def step(n, e, tok):
                    dve.wait_ge(s_used, n + 1)
                    for w, to, done in ((1, cols[e], s_onehot), (0, rows[e], s_rows)):
                        nc.vector.tensor_tensor(to[:, :, :], iota, bc(tab[:, w, bass.ds(s * SW + tok, Q)], 2, NKEY),
                                                ALU.is_equal).then_inc(done, 1)

                steps(dve, s, step)

        @block.gpsimd
        def _(pool):
            for s in range(NSW):
                def step(n, e, tok):
                    pool.wait_ge(s_onehot, n + 1)
                    pool.tensor_tensor(cols[e][:, :, :], cols[e][:, :, :],
                                       bc(tab[:, 2, bass.ds(s * SW + tok, Q)], 2, NKEY), ALU.mult).then_inc(s_cols, 1)

                steps(pool, s, step)

        @block.tensor
        def _(pe):
            pe.nop().then_inc(s_used, R)
            for s in range(NSW):
                def step(n, e, tok):
                    pe.wait_ge(s_rows, n + 1)
                    pe.wait_ge(s_cols, n + 1)
                    pe.wait_ge(s_taken, n + 1)
                    for q in range(Q):
                        b, at = divmod(q * P, T)
                        last = nc.tensor.matmul(S.ps[:, 2 * e + b, at:at + P], rows[e][:, q, :], cols[e][:, q, :],
                                                start=True, stop=True)
                    last.then_inc(s_used, 1)

                steps(pe, s, step)

        @block.scalar
        def _(act):
            act.nop().then_inc(s_taken, R)
            for s in range(NSW):
                if s >= 2:
                    act.wait_ge(s_out[s % 2], 16 * (s // 2))

                def step(n, e, tok):
                    act.wait_ge(s_used, n + R + 1)
                    act.activation(stage[s % 2][:, :, bass.ds(tok, Q)].rearrange("p j t -> p t j"),
                                   S.ps[:, 2 * e:2 * e + 2, :].rearrange("p b (t j) -> p (b t) j", j=NKEY),
                                   ACT.Copy).then_inc(s_taken, 1)

                steps(act, s, step)

        @block.sync
        def _(sp):
            for s in range(NSW):
                sp.wait_ge(s_taken, R + NQ * (s + 1))
                sp.dma_start(dram["gates"][s], stage[s % 2][:, :, :]).then_inc(s_out[s % 2], 16)
            for e in range(2):
                sp.wait_ge(s_out[e], 16 * (NSW // 2))


def experts(nc, S, dram):
    sem = S.sem
    with ExitStack() as ctx:
        def sb(name, shape, dt=F32):
            return ctx.enter_context(nc.sbuf_tensor(name, shape, dt))

        u_raw = sb("u_raw", [P, 2, EG, D])
        v_raw = sb("v_raw", [P, 2, EG, D])
        u_hi = sb("u_hi", [P, 2, D], F32R)
        u_lo = sb("u_lo", [P, 2, D], F32R)
        v_hi = sb("v_hi", [P, 2, EG, D], F32R)
        v_lo = sb("v_lo", [P, 2, EG, D], F32R)
        gates = sb("gates", [P, 2, NSW, EG, SW])
        act_g = sb("act_g", [P, 2, T])
        a_hi = sb("a_hi", [P, 2, EG, T], F32R)
        a_lo = sb("a_lo", [P, 2, EG, T], F32R)
        ss = sb("o_ss", [P, TT])
        s_u = [sem(f"e_u{i}") for i in range(2)]
        s_v = [sem(f"e_v{i}") for i in range(2)]
        s_g = [sem(f"e_g{i}") for i in range(2)]
        s_uhi, s_ulo, s_h, s_gelu, s_gated, s_ahi, s_alo = (sem("e_uhi"), sem("e_ulo"), sem("e_h"), sem("e_gelu"),
                                                            sem("e_gated"), sem("e_ahi"), sem("e_alo"))
        s_vhi, s_vlo, s_o, s_acc = sem("e_vhi"), sem("e_vlo"), sem("e_o"), sem("e_acc")
        s_ss, s_var, s_std, s_sc, s_out = sem("e_ss"), sem("e_var"), sem("e_std"), sem("e_sc"), sem("e_out")
        block = ctx.enter_context(nc.Block())

        def groups(eng, step):
            step(0, 0, True, False, 1, 1)
            with eng.Fori(0, (NG - 2) // 2) as i:
                step(2 * i + 1, 1, False, False, i + 1, i + 2)
                step(2 * i + 2, 0, False, False, i + 2, i + 2)
            step(NG - 1, (NG - 1) % 2, False, True, NG // 2, None)

        def loads(sp, g, p, fresh):
            if not fresh:
                sp.wait_ge(s_ulo, EG * (g - 1))
            sp.dma_start(u_raw[:, p, :, :], dram["u_t"][:, bass.ds(g * EG, EG), :]).then_inc(s_u[p], 16)
            if not fresh:
                sp.wait_ge(s_gated, EG * (g - 1))
            sp.dma_start(gates[:, p, :, :, :], dram["gates_in"][:, :, bass.ds(g * EG, EG), :]).then_inc(s_g[p], 16)
            if not fresh:
                sp.wait_ge(s_vlo, EG * (g - 1))
            sp.dma_start(v_raw[:, p, :, :], dram["v"][:, bass.ds(g * EG, EG), :]).then_inc(s_v[p], 16)

        @block.sync
        def _(sp):
            loads(sp, 0, 0, True)
            loads(sp, 1, 1, True)
            with sp.Fori(0, (NG - 2) // 2) as i:
                loads(sp, 2 * i + 2, 0, False)
                loads(sp, 2 * i + 3, 1, False)
            for t in range(TT):
                sp.wait_ge(s_sc, t + 1)
                sp.dma_start(dram["out"][t * P:(t + 1) * P, :], S.h[:, t, :]).then_inc(s_out, 16)
            sp.wait_ge(s_out, 16 * TT)

        @block.scalar
        def _(act):
            def split_u(n, e, p, landed, fresh):
                act.wait_ge(s_u[p], landed)
                if not fresh:
                    act.wait_ge(s_h, n - 1)
                act.activation(u_hi[:, e, :], u_raw[:, p, e, :], ACT.Copy).then_inc(s_uhi, 1)

            def step(g, p, first, last, loaded, loaded_next):
                for e in range(EG):
                    n = EG * g + e
                    if e == 0:
                        split_u(n + 1, 1, p, 16 * loaded, first)
                    elif not last:
                        split_u(n + 1, 0, 1 - p, 16 * loaded_next, False)
                    act.wait_ge(s_h, n + 1)
                    if not first:
                        act.wait_ge(s_gated, n - 1)
                        act.wait_ge(s_alo, n - 1)
                    act.activation(act_g[:, e, :], S.ps[:, e, :], ACT.Gelu).then_inc(s_gelu, 1)
                    act.wait_ge(s_v[p], 16 * loaded)
                    if not first and not (isinstance(g, int) and g < 2):
                        act.wait_ge(s_o, 8 * (g - 1))
                    act.activation(v_hi[:, p, e, :], v_raw[:, p, e, :], ACT.Copy).then_inc(s_vhi, 1)
                    act.wait_ge(s_gated, n + 1)
                    act.activation(a_hi[:, p, e, :], act_g[:, e, :], ACT.Copy).then_inc(s_ahi, 1)

            split_u(0, 0, 0, 16, True)
            groups(act, step)
            for t in range(TT):
                act.wait_ge(s_acc, 8 * NG + 8)
                act.activation(act_g[:, :, :], S.h[:, t, :].rearrange("p (a b) -> p a b", a=2), ACT.Square,
                               accum_out=ss[:, t:t + 1]).then_inc(s_ss, 1)
                act.wait_ge(s_ss, t + 1)
            act.wait_ge(s_var, 1)
            act.activation(ss[:, :], ss[:, :], ACT.Sqrt).then_inc(s_std, 1)

        @block.vector
        def _(dve):
            v = nc.vector

            def split_u(n, e, p):
                dve.wait_ge(s_uhi, n + 1)
                v.tensor_tensor(u_lo[:, e, :], u_raw[:, p, e, :], u_hi[:, e, :].bitcast(F32),
                                ALU.subtract).then_inc(s_ulo, 1)

            def accumulate(g, e):
                for o in range(4 * e, 4 * e + 4):
                    t, d = divmod(o, 2)
                    dve.wait_ge(s_o, 8 * g + o + 1)
                    dve.wait_ge(s_acc, 8 * g + o + 1)
                    v.tensor_tensor(S.h[:, t, d * T:(d + 1) * T], S.h[:, t, d * T:(d + 1) * T], S.ps[:, 4 + o % 4, :],
                                    ALU.add).then_inc(s_acc, 1)

            def step(g, p, first, last, loaded, loaded_next):
                for e in range(EG):
                    n = EG * g + e
                    if e == 0:
                        split_u(n + 1, 1, p)
                    elif not last:
                        split_u(n + 1, 0, 1 - p)
                    dve.wait_ge(s_gelu, n + 1)
                    dve.wait_ge(s_g[p], 16 * loaded)
                    v.tensor_tensor(act_g[:, e, :].rearrange("p (s t) -> p s t", t=SW),
                                    act_g[:, e, :].rearrange("p (s t) -> p s t", t=SW), gates[:, p, :, e, :],
                                    ALU.mult).then_inc(s_gated, 1)
                    if not first:
                        accumulate(g - 1, e)
                    dve.wait_ge(s_vhi, n + 1)
                    v.tensor_tensor(v_lo[:, p, e, :], v_raw[:, p, e, :], v_hi[:, p, e, :].bitcast(F32),
                                    ALU.subtract).then_inc(s_vlo, 1)
                    dve.wait_ge(s_ahi, n + 1)
                    v.tensor_tensor(a_lo[:, p, e, :], act_g[:, e, :], a_hi[:, p, e, :].bitcast(F32),
                                    ALU.subtract).then_inc(s_alo, 1)

            dve.nop().then_inc(s_acc, 8)
            split_u(0, 0, 0)
            groups(dve, step)
            accumulate(NG - 1, 0)
            accumulate(NG - 1, 1)
            dve.wait_ge(s_ss, TT)
            st = Steps(dve, S.own_dve, S.counts)
            st.do(v.tensor_scalar(ss[:, :], ss[:, :], 1.0 / D, RMS_EPS, ALU.mult, ALU.add))
            st.settle()
            st.do(v.reciprocal(ss[:, :], ss[:, :]), s_var)
            dve.wait_ge(s_std, 1)
            for t in range(TT):
                st.do(v.scalar_tensor_tensor(S.h[:, t, :], S.h[:, t, :], ss[:, t:t + 1], S.g_final[:, :],
                                             ALU.mult, ALU.mult), s_sc)

        @block.tensor
        def _(pe):
            def hidden(n, e, fresh):
                pe.wait_ge(s_ulo, n + 1)
                if not fresh:
                    pe.wait_ge(s_gelu, n - 1)
                for k in range(KT):
                    w = slice(k * P, (k + 1) * P)
                    last = three_pass(nc, S.ps[:, e, :], u_hi[:, e, w], u_lo[:, e, w], S.xn_hi[:, k, :],
                                      S.xn_lo[:, k, :], k == 0, k == KT - 1)
                last.then_inc(s_h, 1)

            def outputs(g, e, p):
                if e == 0:
                    pe.wait_ge(s_alo, EG * (g + 1))
                    pe.wait_ge(s_vlo, EG * (g + 1))
                for o in range(4 * e, 4 * e + 4):
                    t, d = divmod(o, 2)
                    x, w = slice(t * P, (t + 1) * P), slice(d * T, (d + 1) * T)
                    pe.wait_ge(s_acc, 8 * g + o + 5)
                    for k in range(EG):
                        last = three_pass(nc, S.ps[:, 4 + o % 4, :], a_hi[:, p, k, x], a_lo[:, p, k, x],
                                          v_hi[:, p, k, w], v_lo[:, p, k, w], k == 0, k == EG - 1)
                    last.then_inc(s_o, 1)

            def step(g, p, first, last, loaded, loaded_next):
                for e in range(EG):
                    hidden(EG * g + e, e, first)
                    if not first:
                        outputs(g - 1, e, 1 - p)

            groups(pe, step)
            outputs(NG - 1, 0, (NG - 1) % 2)
            outputs(NG - 1, 1, (NG - 1) % 2)


def build(nc, dram):
    with ExitStack() as ctx:
        def sb(name, shape, dt=F32):
            return ctx.enter_context(nc.sbuf_tensor(name, shape, dt))

        S = Shared()
        S.counts = {}
        S.sem = lambda name: ctx.enter_context(nc.semaphore(name))
        S.own_dve, S.own_act, S.own_pool = S.sem("own_dve"), S.sem("own_act"), S.sem("own_pool")
        S.ps = ctx.enter_context(nc.psum_tensor("ps", [P, 8, 512], F32))
        S.consts = sb("consts", [P, NCONST])
        S.params = sb("params", [P, NPARAM])
        S.g_final = sb("g_final", [P, D])
        S.const = lambda name: S.consts[:, CONST_COLS[name][0]:CONST_COLS[name][1]]
        S.param = lambda name, j: S.params[:, PARAM_COLS[name][0] + j:PARAM_COLS[name][0] + j + 1]
        S.param_all = lambda name: S.params[:, PARAM_COLS[name][0]:PARAM_COLS[name][1]]
        with ExitStack() as front:
            def sf(name, shape, dt=F32):
                return front.enter_context(nc.sbuf_tensor(name, shape, dt))

            S.up = sf("up_weights", [P, 2, T])
            S.mixed = sf("mixed", [P, KT, T])
            with ExitStack() as rwkv:
                def sr(name, shape, dt=F32):
                    return rwkv.enter_context(nc.sbuf_tensor(name, shape, dt))

                S.zm = sr("z_mixed", [P, NRW, T])
                with ExitStack() as attn:
                    S.qk = attn.enter_context(nc.sbuf_tensor("qk", [P, NQK, T], F32))
                    S.v_tok = attn.enter_context(nc.sbuf_tensor("v_tok", [P, TT, T], F32))
                    project(nc, S, dram)
                    attend(nc, S, dram)
                S.gate = sr("gate", [P, HP, T])
                S.v_chunk = sr("v_chunk", [P, NCH, HP, HD])
                S.pc = sr("chunk_decay", [P, HP, NCH])
                S.ra = sr("r_and_a", [P, HP, NCH, 2, C])
                S.bs = sr("b_scaled", [P, HP, T])
                S.ks = sr("k_scaled", [P, HP, T])
                prepare(nc, S, dram)
                S.y_chunk = S.zm[:, 4:8, :].rearrange("p a (b j i) -> p (a b) j i", b=2, i=HD)
                scan(nc, S, dram)
                normalise_heads(nc, S, dram)
            S.h = sf("h", [P, TT, D])
            S.xn_hi = sf("xn2_hi", [P, KT, T], F32R)
            S.xn_lo = sf("xn2_lo", [P, KT, T], F32R)
            S.tab = sf("tables", [P, 3, T])
            mix(nc, S, dram)
            route(nc, S, dram)
            spread(nc, S, dram)
            experts(nc, S, dram)


def kernel(**inputs):
    import concourse.bacc as bacc
    from concourse.bass_utils import run_bass_kernel_spmd

    a = {k: np.ascontiguousarray(v) for k, v in inputs.items()}
    f = np.ascontiguousarray
    x = a["x"][0]
    w_in = a["w_in"][0]
    cols = (NRW + NQK) * P
    win_cols = w_in[:, :cols].reshape(KT, P, NRW + NQK, P).transpose(2, 1, 0, 3).reshape(NRW + NQK, P, D)
    win_v = w_in[:, cols:].reshape(NV, 2, P, T).transpose(0, 2, 1, 3).reshape(NV, P, D)

    def tiles(vec):
        return vec.reshape(-1, P).T

    par = np.concatenate([tiles(a["norm_mix"][0]), tiles(a["rwkv_mu"][0]), tiles(a["rwkv_w0"][0]),
                          tiles(a["rwkv_a0"][0]), tiles(a["rwkv_k_k"][0]), tiles(a["rwkv_k_a"][0]),
                          tiles(a["rwkv_r_k"][0].reshape(-1)), tiles(a["rwkv_gn_w"][0]), tiles(a["rwkv_gn_b"][0]),
                          tiles(a["norm_ffn"][0])], axis=1)
    up = np.stack([np.concatenate([a["rwkv_w_up"][0], a["rwkv_a_up"][0]], axis=0), a["rwkv_g_up"][0]], axis=1)
    arrays = {
        "x_t": f(x.T.reshape(KT, P, T).transpose(1, 0, 2)),
        "x": f(x.reshape(TT, P, D).transpose(1, 0, 2)),
        "win_t": f(np.concatenate([win_cols, win_v], axis=0)),
        "consts": build_constants(),
        "params": f(par),
        "up": f(up),
        "g_final": f(np.broadcast_to(a["norm_final"][None, :], (P, D))),
        "wout": f(a["w_out"][0].reshape(KT, P, D)),
        "wq_t": f(a["peer_w_q"][0].reshape(KT, P, 2 * PH, P).transpose(2, 1, 0, 3).reshape(2 * PH, P, D)),
        "keys_t": f(a["peer_sub_keys"][0].transpose(2, 0, 1)),
        "u_t": f(a["peer_u"][0].reshape(NKEY, NKEY, KT, P).transpose(3, 1, 2, 0).reshape(P, NKEY, D)),
        "v": f(a["peer_v"][0].reshape(NKEY, NKEY, D)),
    }
    nc = bacc.Bacc("TRN2", target_bir_lowering=False, num_devices=1)
    dram = {k: nc.dram_tensor(f"in_{k}", v.shape, mybir.dt.from_np(v.dtype), kind="ExternalInput").ap()
            for k, v in arrays.items()}
    dram["out"] = nc.dram_tensor("out_h", (T, D), F32, kind="ExternalOutput").ap()
    gates = nc.dram_tensor("gate_matrix", (NSW, P, NKEY, SW), F32, kind="Internal").ap()
    dram["gates"] = gates
    dram["gates_in"] = gates.rearrange("s p j t -> p s j t")
    build(nc, dram)
    r = run_bass_kernel_spmd(nc, [{f"in_{k}": v for k, v in arrays.items()}], core_ids=[0])
    return r.results[0]["out_h"].reshape(1, T, D)
```

```python
from contextlib import ExitStack

import concourse.bass as bass
import concourse.mybir as mybir
import numpy as np

F32 = mybir.dt.float32
F32R = mybir.dt.float32r
U32 = mybir.dt.uint32
ALU = mybir.AluOpType
ACT = mybir.ActivationFunctionType
AX = mybir.AxisListType.X

P = 128
D = 1024
T = 512
KT = D // P
TT = T // P
HD = 64
HP = 4
C = 64
NCH = T // C
NRW = 14
NQK = 8
NV = 4
NWIN = NRW + NQK + NV
PH = 8
TOPK = 16
NKEY = 128
NCAND = 64
RAW = 6
RQ = 4
SPL = 3
KAPPA = float(np.exp(-0.5))
RMS_EPS = 1e-6
GN_EPS = 64e-5
LOWEST = -3.0e38
SW = 64
NSW = T // SW
EG = 2
NG = NKEY // EG
NST = 12
NGN = NG - NST // EG

CONST_COLS = {}


def build_constants():
    parts = []
    at = 0

    def put(name, a):
        nonlocal at
        a = np.asarray(a, np.float32)
        CONST_COLS[name] = (at, at + a.shape[1])
        at += a.shape[1]
        parts.append(a)

    r = np.arange(P)
    put("ident", np.eye(P))
    swap = (r // HD) * HD + (r % HD + HD // 2) % HD
    perm = np.zeros((P, P))
    perm[swap, r] = 1.0
    put("perm", perm)
    put("block_ones", (r[:, None] // HD == r[None, :] // HD))
    put("ones", np.ones((P, P)))
    for j in range(HP):
        head = 2 * j + r // HD
        put(f"to_head{j}", head[:, None] == r[None, :] % (2 * HP))
        put(f"from_head{j}", r[:, None] == head[None, :])
    put("iota", np.tile(np.arange(P), (P, 1)))
    inv_freq = np.float32(10000.0) ** (-np.arange(0, HD, 2, dtype=np.float32) / np.float32(HD))
    ang = np.arange(T, dtype=np.float32)[None, :] * inv_freq[r % (HD // 2)][:, None]
    put("cos", np.cos(ang))
    put("sin", np.sin(ang) * np.where(r % HD < HD // 2, -1.0, 1.0)[:, None])
    cols = []
    for delta in range(TT - 1, -1, -1):
        dist = delta * P + r[:, None] - r[None, :]
        n = ((dist >= 0) & (dist <= 128)).astype(int)
        n += (dist >= 0) & (dist % 4 == 0)
        n += (dist >= 0) & (dist % 16 == 0)
        cols.append(np.where(n > 0, np.log(np.maximum(n, 1)), -1e30))
    put("attn_bias", np.concatenate(cols, axis=1))
    put("keep", np.tile((np.arange(T) % C != 0), (P, 1)))
    s, t = r[:, None] % C, np.arange(C)[None, :]
    put("strict", s < t)
    put("inclusive", s <= t)
    for level in range(1, 6):
        m = 1 << level
        put(f"level{level}", (s // (2 * m) == t // (2 * m)) & (t // m < s // m))
    put("level0_t", (s // 2 == t // 2) & (s < t))
    starts = [0, 16, 24, 32, 40, 44, 48, 52] + list(range(56, 64))
    put("row_starts", np.tile(starts, (P, 1)))
    return np.concatenate(parts, axis=1)


build_constants()
NCONST = max(b for _, b in CONST_COLS.values())
PARAM_COLS = {}
_at = 0
for _name, _n in (("g_mix", KT), ("mu", NRW), ("w0", HP), ("a0", HP), ("k_k", HP), ("k_a", HP), ("r_k", HP),
                  ("gn_w", HP), ("gn_b", HP), ("g_ffn", KT)):
    PARAM_COLS[_name] = (_at, _at + _n)
    _at += _n
NPARAM = _at


class Steps:

    def __init__(self, eng, own, counts):
        self.eng, self.own, self.counts, self.last = eng, own, counts, None

    def do(self, ins, signal=None):
        sem = self.own if signal is None else signal
        ins.then_inc(sem, 1)
        self.counts[sem.name] = self.counts.get(sem.name, 0) + 1
        self.last = (sem, self.counts[sem.name])

    def settle(self):
        self.eng.wait_ge(*self.last)


class Shared:
    pass


def bc(ap, axis, n):
    ap = ap.unsqueeze(axis)
    shape = list(ap.shape)
    shape[axis] = n
    return ap.to_broadcast(shape)


def three_pass(nc, out, w_hi, w_lo, m_hi, m_lo, first, last):
    nc.tensor.matmul(out, w_hi, m_hi, start=first, stop=False)
    nc.tensor.matmul(out, w_hi, m_lo, start=False, stop=False)
    return nc.tensor.matmul(out, w_lo, m_hi, start=False, stop=last)


def q_tile(h):
    return (h + HP) % (2 * HP)


def two_heads(nc, out, blocks, rhs, start=True, stop=True):
    for e in range(2):
        h = slice(e * HD, (e + 1) * HD)
        last = nc.tensor.matmul(out[h], blocks[:, h], rhs, start=start, stop=stop)
    return last


def project(nc, S, dram):
    sem = S.sem
    with ExitStack() as ctx:
        def sb(name, shape, dt=F32):
            return ctx.enter_context(nc.sbuf_tensor(name, shape, dt))

        xt = sb("x_t", [P, KT, T])
        sq = S.qk
        rstd = sb("x_rstd", [P, T])
        rstd_col = sb("x_rstd_col", [P, TT])
        xn_hi = sb("xn_hi", [P, KT, T], F32R)
        xn_lo = sb("xn_lo", [P, KT, T], F32R)
        raw = sb("win_raw", [P, RAW, D])
        w_hi = sb("win_hi", [P, SPL, D], F32R)
        w_lo = sb("win_lo", [P, SPL, D], F32R)
        zb = sb("z_shift", [P, 2, T + 1])
        zd = sb("z_delta", [P, 2, T])
        tmp = sb("rope_tmp", [P, 2, T])

        s_param, s_const, s_rest = sem("p_param"), sem("p_const"), sem("p_rest")
        s_perm, s_sin = sem("p_perm"), sem("p_sin")
        s_x = [sem(f"p_x{q}") for q in range(4)]
        s_raw = [sem(f"p_raw{i}") for i in range(RAW)]
        s_sq, s_ms, s_mean, s_rstd = sem("p_sq"), sem("p_ms"), sem("p_mean"), sem("p_rstd")
        s_xhi, s_xlo, s_col, s_colc = sem("p_xhi"), sem("p_xlo"), sem("p_col"), sem("p_colc")
        s_hi, s_lo, s_mm, s_out, s_zero = (sem("p_hi"), sem("p_lo"), sem("p_mm"), sem("p_out"),
                                                    sem("p_zero"))
        block = ctx.enter_context(nc.Block())

        @block.sync
        def _(sp):
            for n in range(NWIN):
                if n >= RAW:
                    sp.wait_ge(s_lo, n - RAW + 1)
                sp.dma_start(raw[:, n % RAW, :], dram["win_t"][n]).then_inc(s_raw[n % RAW], 16)
                if n == 0:
                    for q in range(4):
                        x = slice(2 * q, 2 * q + 2)
                        sp.dma_start(xt[:, x, :], dram["x_t"][:, x, :]).then_inc(s_x[q], 16)
                if n == 1:
                    sp.dma_start(S.consts[:, :], dram["consts"]).then_inc(s_const, 16)
                if n == 3:
                    sp.dma_start(S.up[:, :, :], dram["up"]).then_inc(s_rest, 16)
                    sp.dma_start(S.g_final[:, :], dram["g_final"]).then_inc(s_rest, 16)

        @block.gpsimd
        def _(pool):
            st = Steps(pool, S.own_pool, S.counts)
            st.do(pool.memset(zb[:, :, 0:1], 0.0), s_zero)
            st.do(pool.memset(S.q_padded[:, :, :], 0.0), s_zero)

        @block.scalar
        def _(act):
            st = Steps(act, S.own_act, S.counts)
            act.dma_start(S.params[:, :], dram["params"]).then_inc(s_param, 16)
            for n in range(NWIN):
                act.wait_ge(s_raw[n % RAW], 16 * (n // RAW + 1))
                if n >= SPL:
                    act.wait_ge(s_mm, n - SPL + 1)
                st.do(act.activation(w_hi[:, n % SPL, :], raw[:, n % RAW, :], ACT.Copy), s_hi)
                if n == 0:
                    act.wait_ge(s_param, 16)
                    for k in range(KT):
                        if k % 2 == 0:
                            act.wait_ge(s_x[k // 2], 16)
                        st.do(act.activation(xn_hi[:, k, :], xt[:, k, :], ACT.Copy, scale=S.param("g_mix", k)), s_xhi)
                    for k in range(KT):
                        st.do(act.activation(sq[:, k, :], xt[:, k, :], ACT.Square), s_sq)
                if n == SPL - 1:
                    act.wait_ge(s_mean, 2)
                    st.do(act.activation(rstd[:, :], rstd[:, :], ACT.Sqrt), s_rstd)
            act.wait_ge(s_rest, 32)
            act.wait_ge(s_mm, NWIN)
            act.wait_ge(s_colc, 1)
            for t in range(TT):
                st.do(act.activation(S.v_tok[:, t, :], S.ps[:, 4 + t, :], ACT.Copy, scale=rstd_col[:, t:t + 1]))

        @block.vector
        def _(dve):
            st = Steps(dve, S.own_dve, S.counts)
            v = nc.vector
            def inverse_rms():
                dve.wait_ge(s_ms, 1)
                st.do(v.tensor_scalar(rstd[:, :], S.ps[:, 3, :], 1.0 / D, RMS_EPS, ALU.mult, ALU.add), s_mean)
                st.settle()
                st.do(v.reciprocal(rstd[:, :], rstd[:, :]), s_mean)
                dve.wait_ge(s_rstd, 1)

            def take(n):
                dve.wait_ge(s_mm, n + 1)
                if n >= NRW:
                    st.do(v.tensor_tensor(S.qk[:, n - NRW, :], S.ps[:, n % 3, :], rstd[:, :], ALU.mult), s_out)
                    return
                z, z_prev = zb[:, n % 2, 1:T + 1], zb[:, n % 2, 0:T]
                if n == 0:
                    dve.wait_ge(s_zero, 1)
                else:
                    st.settle()
                st.do(v.tensor_tensor(z, S.ps[:, n % 3, :], rstd[:, :], ALU.mult), s_out)
                st.settle()
                st.do(v.tensor_tensor(zd[:, n % 2, :], z_prev, z, ALU.subtract))
                st.settle()
                st.do(v.scalar_tensor_tensor(S.zm[:, n, :], zd[:, n % 2, :], S.param("mu", n), z, ALU.mult, ALU.add))

            def rope(m):
                dve.wait_ge(s_perm, m + 1)
                st.do(v.tensor_tensor(tmp[:, m % 2, :], S.ps[:, 3, :], S.const("sin"), ALU.mult), s_sin)
                st.do(v.tensor_tensor(S.qk[:, m, :], S.qk[:, m, :], S.const("cos"), ALU.mult))
                st.settle()
                if m >= HP:
                    st.do(v.tensor_tensor(S.qk[:, m, :], S.qk[:, m, :], tmp[:, m % 2, :], ALU.add))
                    return
                if m == 0:
                    dve.wait_ge(s_zero, 2)
                for e in range(2):
                    h = slice(e * HD, (e + 1) * HD)
                    st.do(v.tensor_tensor(S.q_padded[h, q_tile(2 * m + e), :], S.qk[h, m, :], tmp[h, m % 2, :],
                                          ALU.add))

            for n in range(NWIN):
                dve.wait_ge(s_hi, n + 1)
                st.do(v.tensor_tensor(w_lo[:, n % SPL, :], raw[:, n % RAW, :], w_hi[:, n % SPL, :].bitcast(F32),
                                      ALU.subtract), s_lo)
                if n == 0:
                    for k in range(KT):
                        dve.wait_ge(s_xhi, k + 1)
                        st.do(v.scalar_tensor_tensor(xn_lo[:, k, :], xt[:, k, :], S.param("g_mix", k),
                                                     xn_hi[:, k, :].bitcast(F32), ALU.mult, ALU.subtract), s_xlo)
                if n == SPL - 1:
                    inverse_rms()
                    take(0)
                    take(1)
                if SPL <= n <= NRW + NQK:
                    take(n - 1)
                if n == SPL + 2:
                    dve.wait_ge(s_col, 1)
                    st.do(v.tensor_copy(rstd_col[:, :], S.ps[:, 7, :].rearrange("p (t x) -> p t x", x=P)[:, :, 0]),
                          s_colc)
                if NRW < n - 1 < NRW + NQK + 1:
                    rope(n - 2 - NRW)

        @block.tensor
        def _(pe):
            def swap(m):
                pe.wait_ge(s_out, NRW + m + 1)
                if m:
                    pe.wait_ge(s_sin, m)
                nc.tensor.matmul(S.ps[:, 3, :], S.const("perm"), S.qk[:, m, :], start=True,
                                 stop=True).then_inc(s_perm, 1)

            for n in range(NWIN):
                if n == 1:
                    pe.wait_ge(s_const, 16)
                    for k in range(KT):
                        pe.wait_ge(s_sq, k + 1)
                        last = nc.tensor.matmul(S.ps[:, 3, :], S.const("ones"), sq[:, k, :], start=k == 0,
                                                stop=k == KT - 1)
                    last.then_inc(s_ms, 1)
                if n == SPL + 1:
                    pe.wait_ge(s_rstd, 1)
                    for t in range(TT):
                        last = nc.tensor.transpose(S.ps[:, 7, t * P:(t + 1) * P], rstd[:, t * P:(t + 1) * P],
                                                   S.const("ident"))
                    last.then_inc(s_col, 1)
                pe.wait_ge(s_lo, n + 1)
                if n < NRW + NQK:
                    if n >= 3:
                        pe.wait_ge(s_out, n - 2)
                    for k in range(KT):
                        w = slice(k * P, (k + 1) * P)
                        if n == 0:
                            pe.wait_ge(s_xlo, k + 1)
                        last = three_pass(nc, S.ps[:, n % 3, :], w_hi[:, n % SPL, w], w_lo[:, n % SPL, w],
                                          xn_hi[:, k, :], xn_lo[:, k, :], k == 0, k == KT - 1)
                else:
                    kk = n - NRW - NQK
                    for t in range(TT):
                        x = slice(t * P, (t + 1) * P)
                        for j in range(2):
                            k, w = 2 * kk + j, slice(j * T, (j + 1) * T)
                            last = three_pass(nc, S.ps[:, 4 + t, :], xn_hi[:, k, x], xn_lo[:, k, x],
                                              w_hi[:, n % SPL, w], w_lo[:, n % SPL, w], k == 0, k == KT - 1)
                last.then_inc(s_mm, 1)
                if NRW < n < NRW + NQK + 1:
                    swap(n - 1 - NRW)


def attend(nc, S, dram):
    sem = S.sem
    with ExitStack() as ctx:
        def sb(name, shape, dt=F32):
            return ctx.enter_context(nc.sbuf_tensor(name, shape, dt))

        R4 = 4
        sm = sb("scores", [P, R4, T])
        pt = sb("probs_t", [P, 2, TT, T])
        mx = sb("row_max", [P, 32])
        nmx = sb("neg_max", [P, 32])
        den = sb("row_sum", [P, 32])
        rden = sb("row_inv", [P, 32])
        s_sc, s_bias, s_neg, s_exp, s_prob = sem("a_sc"), sem("a_bias"), sem("a_neg"), sem("a_exp"), sem("a_prob")
        s_tr, s_pt, s_pv, s_mix = sem("a_tr"), sem("a_pt"), sem("a_pv"), sem("a_mix")
        NU = 8 * TT
        block = ctx.enter_context(nc.Block())

        @block.tensor
        def _(pe):
            def scores(u):
                h, t = divmod(u, TT)
                if u >= 3:
                    pe.wait_ge(s_bias, u - 2)
                nc.tensor.matmul(S.ps[:, u % 3, 0:(t + 1) * P], S.q_padded[:, q_tile(h), t * P:(t + 1) * P],
                                 S.qk[:, HP + h // 2, 0:(t + 1) * P], start=True, stop=True).then_inc(s_sc, 1)

            def turn(u):
                t = u % TT
                pe.wait_ge(s_prob, u + 1)
                if u >= 2:
                    pe.wait_ge(s_pt, u - 1)
                for j in range(t + 1):
                    last = nc.tensor.transpose(S.ps[:, 3 + u % 2, j * P:(j + 1) * P],
                                               sm[:, u % R4, j * P:(j + 1) * P], S.const("ident"))
                last.then_inc(s_tr, 1)

            def values(h, j):
                if j == 0:
                    pe.wait_ge(s_pt, TT * (h + 1))
                    if h >= 4 and h % 2 == 0:
                        pe.wait_ge(s_mix, h // 2 - 1)
                last = nc.tensor.matmul(S.ps[HD * (h % 2):HD * (h % 2) + HD, 5 + (h // 2) % 2, j * P:T],
                                        S.v_tok[:, j, h * HD:(h + 1) * HD], pt[:, h % 2, j, j * P:T],
                                        start=j == 0, stop=j == TT - 1)
                if j == TT - 1:
                    last.then_inc(s_pv, 1)

            for i in range(NU + 3):
                if i < NU:
                    scores(i)
                if i >= 3:
                    turn(i - 3)
                    if i - 4 >= TT:
                        values((i - 4) // TT - 1, (i - 4) % TT)
            for i in range(NU + 3, NU + TT + 4):
                values((i - 4) // TT - 1, (i - 4) % TT)

        @block.scalar
        def _(act):
            st = Steps(act, S.own_act, S.counts)

            def exps(u):
                t = u % TT
                act.wait_ge(s_neg, u + 1)
                st.do(act.activation(sm[:, u % R4, 0:(t + 1) * P], sm[:, u % R4, 0:(t + 1) * P], ACT.Exp,
                                     bias=nmx[:, u:u + 1], accum_out=den[:, u:u + 1]), s_exp)

            def take(u):
                h, t = divmod(u, TT)
                act.wait_ge(s_tr, u + 1)
                if h >= 2:
                    act.wait_ge(s_pv, h - 1)
                st.do(act.activation(pt[:, h % 2, 0:t + 1, t * P:(t + 1) * P],
                                     S.ps[:, 3 + u % 2, 0:(t + 1) * P].rearrange("p (j q) -> p j q", q=P), ACT.Copy),
                      s_pt)

            def pair(p):
                act.wait_ge(s_pv, 2 * p + 2)
                st.do(act.activation(S.mixed[:, HP + p, :], S.ps[:, 5 + p % 2, :], ACT.Copy), s_mix)

            for i in range(1, NU + 4):
                if i <= NU:
                    exps(i - 1)
                if i >= 4:
                    u = i - 4
                    take(u)
                    if u > 3 * TT and u % (2 * TT) == TT + 1:
                        pair(u // (2 * TT) - 1)
            pair(HP - 1)

        @block.vector
        def _(dve):
            st = Steps(dve, S.own_dve, S.counts)
            v = nc.vector
            for i in range(NU + 2):
                u, w = i, i - 2
                if u < NU:
                    t = u % TT
                    dve.wait_ge(s_sc, u + 1)
                    if u >= R4:
                        dve.wait_ge(s_tr, u - R4 + 1)
                    st.do(v.scalar_tensor_tensor(sm[:, u % R4, 0:(t + 1) * P], S.ps[:, u % 3, 0:(t + 1) * P],
                                                 HD ** -0.5, S.const("attn_bias")[:, (TT - 1 - t) * P:], ALU.mult,
                                                 ALU.add), s_bias)
                if w >= 0:
                    dve.wait_ge(s_exp, w + 1)
                    st.do(v.reciprocal(rden[:, w:w + 1], den[:, w:w + 1]))
                st.settle()
                if u < NU:
                    st.do(v.tensor_reduce(mx[:, u:u + 1], sm[:, u % R4, 0:(t + 1) * P], AX, ALU.max))
                if w >= 0:
                    n = (w % TT + 1) * P
                    st.do(v.tensor_scalar(sm[:, w % R4, 0:n], sm[:, w % R4, 0:n], rden[:, w:w + 1], None, ALU.mult),
                          s_prob)
                if u < NU:
                    st.settle()
                    st.do(v.tensor_scalar(nmx[:, u:u + 1], mx[:, u:u + 1], -1.0, None, ALU.mult), s_neg)


def prepare(nc, S, dram):
    sem = S.sem
    with ExitStack() as ctx:
        def sb(name, shape, dt=F32):
            return ctx.enter_context(nc.sbuf_tensor(name, shape, dt))

        kk = sb("kk", [P, HP, T])
        tmp = sb("prepare_tmp", [P, HP, T])
        sw = sb("decay_rate", [P, HP, T])
        icl = sb("iclr", [P, HP, T])
        cum = sb("decay_sum", [P, HP, T])
        prev = sb("decay_prev", [P, HP, T])
        inv = sb("kk_inverse", [P, T])
        omka = sb("one_minus_k_a", [P, HP])
        rk_ones = sb("r_k_block_ones", [P, HP, P])
        R, K, V, WA, G = S.zm[:, 0:4, :], S.zm[:, 4:8, :], S.zm[:, 8:12, :], S.zm[:, 12, :], S.zm[:, 13, :]
        s_tanh, s_gsig, s_up, s_act = sem("r_tanh"), sem("r_gsig"), sem("r_up"), sem("r_act")
        s_ksq, s_ssum, s_nrm, s_cum, s_prev = sem("r_ksq"), sem("r_ssum"), sem("r_nrm"), sem("r_cum"), sem("r_prev")
        s_exp, s_rk, s_rsum, s_vtr, s_vt = sem("r_exp"), sem("r_rk"), sem("r_rsum"), sem("r_vtr"), sem("r_vt")
        s_pd, s_inv, s_invb, s_k, s_kkd, s_ones = (sem("r_pd"), sem("r_inv"), sem("r_invb"), sem("r_k"), sem("r_kkd"),
                                                   sem("r_ones"))
        block = ctx.enter_context(nc.Block())

        @block.tensor
        def _(pe):
            for j in range(HP):
                for q in range(TT):
                    last = nc.tensor.transpose(S.ps[:, 4 + j, q * P:(q + 1) * P], V[:, j, q * P:(q + 1) * P],
                                               S.const("ident"))
                last.then_inc(s_vtr, 1)
            for j in range(HP):
                pe.wait_ge(s_ksq, j + 1)
                last = nc.tensor.matmul(S.ps[:, 3, :], S.const(f"to_head{j}"), tmp[:, j, :], start=j == 0,
                                        stop=j == HP - 1)
            last.then_inc(s_ssum, 1)
            pe.wait_ge(s_tanh, 1)
            pe.wait_ge(s_gsig, 1)
            for j in range(HP):
                c = slice(j * P, (j + 1) * P)
                if j >= 1:
                    pe.wait_ge(s_act, 3 * j)
                nc.tensor.matmul(S.ps[:, 0, :], S.up[:, 0, c], WA, start=True, stop=True).then_inc(s_up, 1)
                nc.tensor.matmul(S.ps[:, 1, :], S.up[:, 1, c], WA, start=True, stop=True).then_inc(s_up, 1)
                nc.tensor.matmul(S.ps[:, 2, :], S.up[:, 2, c], G, start=True, stop=True).then_inc(s_up, 1)
            pe.wait_ge(s_inv, 1)
            pe.wait_ge(s_vt, 4 * HP)
            for j in range(HP):
                nc.tensor.matmul(S.ps[:, 4 + j, :], S.const(f"from_head{j}"), inv[:, :], start=True,
                                 stop=True).then_inc(s_invb, 1)
            pe.wait_ge(s_rk, 1)
            pe.wait_ge(s_ones, HP)
            for j in range(HP):
                pe.wait_ge(s_kkd, j + 1)
                nc.tensor.matmul(S.ps[:, 4 + j, :], rk_ones[:, j, :], tmp[:, j, :], start=True,
                                 stop=True).then_inc(s_rsum, 1)

        @block.scalar
        def _(act):
            st = Steps(act, S.own_act, S.counts)
            for j in range(HP):
                st.do(act.activation(tmp[:, j, :], K[:, j, :], ACT.Square, scale=S.param("k_k", j)), s_ksq)
            st.do(act.activation(WA[0:HD, :], WA[0:HD, :], ACT.Tanh), s_tanh)
            st.do(act.activation(G, G, ACT.Sigmoid), s_gsig)
            act.wait_ge(s_ssum, 1)
            st.do(act.activation(inv[:, :], S.ps[:, 3, :], ACT.Sqrt), s_nrm)
            for j in range(HP):
                act.wait_ge(s_up, 3 * j + 1)
                st.do(act.activation(sw[:, j, :], S.ps[:, 0, :], ACT.Sigmoid, bias=S.param("w0", j)), s_act)
                act.wait_ge(s_up, 3 * j + 2)
                st.do(act.activation(icl[:, j, :], S.ps[:, 1, :], ACT.Sigmoid, bias=S.param("a0", j)), s_act)
                act.wait_ge(s_up, 3 * j + 3)
                st.do(act.activation(S.gate[:, j, :], S.ps[:, 2, :], ACT.Copy), s_act)
            act.wait_ge(s_cum, HP)
            act.wait_ge(s_prev, 1)
            st.do(act.activation(prev[:, :, :], prev[:, :, :], ACT.Exp, scale=-KAPPA), s_exp)
            st.do(act.activation(sw[:, :, :], cum[:, :, :], ACT.Exp, scale=-KAPPA), s_exp)
            st.do(act.activation(cum[:, :, :], cum[:, :, :], ACT.Exp, scale=KAPPA), s_exp)

        @block.gpsimd
        def _(pool):
            st = Steps(pool, S.own_pool, S.counts)
            st.do(pool.tensor_scalar(omka[:, :], S.param_all("k_a"), -1.0, 1.0, ALU.mult, ALU.add), s_pd)
            pool.wait_ge(s_k, 1)
            st.do(pool.tensor_tensor(tmp[:, :, :], R, K, ALU.mult), s_rk)

        @block.vector
        def _(dve):
            st = Steps(dve, S.own_dve, S.counts)
            v = nc.vector
            for j in range(HP):
                dve.wait_ge(s_vtr, j + 1)
                turned = S.ps[:, 4 + j, :].rearrange("p (q c) -> p q c", c=P)
                for cp in range(2):
                    for hd in range(2):
                        st.do(v.tensor_copy(S.v_chunk[hd * C:(hd + 1) * C, :, j, :].rearrange(
                            "p (q e) i -> p q e i", e=2)[:, :, cp, :],
                            turned[cp * C:(cp + 1) * C, :, hd * HD:(hd + 1) * HD]), s_vt)
                if j == 1:
                    dve.wait_ge(s_nrm, 1)
                    st.do(v.tensor_scalar(inv[:, :], inv[:, :], 1e-12, None, ALU.max))
                    st.settle()
                    st.do(v.reciprocal(inv[:, :], inv[:, :]), s_inv)
            for j in range(HP):
                st.do(v.tensor_scalar(rk_ones[:, j, :], S.const("block_ones"), S.param("r_k", j), None, ALU.mult),
                      s_ones)
            dve.wait_ge(s_pd, 1)
            for j in range(HP):
                dve.wait_ge(s_act, 3 * (j + 1))
                st.do(v.tensor_tensor_scan(cum[:, j, :], S.const("keep"), sw[:, j, :], 0.0, ALU.mult, ALU.add), s_cum)
                st.do(v.tensor_scalar(tmp[:, j, :], icl[:, j, :], S.param("k_a", j), omka[:, j:j + 1],
                                      ALU.mult, ALU.add))
            st.settle()
            st.do(v.tensor_tensor(prev[:, :, :], cum[:, :, :], sw[:, :, :], ALU.subtract), s_prev)
            for j in range(HP):
                dve.wait_ge(s_invb, j + 1)
                st.do(v.scalar_tensor_tensor(kk[:, j, :], K[:, j, :], S.param("k_k", j), S.ps[:, 4 + j, :],
                                             ALU.mult, ALU.mult), s_kkd)
            st.settle()
            st.do(v.tensor_tensor(K, K, tmp[:, :, :], ALU.mult), s_k)
            st.do(v.tensor_tensor(icl[:, :, :], icl[:, :, :], kk[:, :, :], ALU.mult))
            st.settle()
            ra = S.ra[:, :, :, :, :]
            dve.wait_ge(s_exp, 1)
            st.do(v.scalar_tensor_tensor(ra[:, :, :, 0, :].rearrange("p j n t -> p (j n) t"),
                                         kk[:, :, :].rearrange("p j (n t) -> p (j n) t", t=C), -1.0,
                                         prev[:, :, :].rearrange("p j (n t) -> p (j n) t", t=C), ALU.mult, ALU.mult))
            dve.wait_ge(s_exp, 2)
            st.do(v.tensor_tensor(ra[:, :, :, 1, :].rearrange("p j n t -> p (j n) t"),
                                  R.rearrange("p j (n t) -> p (j n) t", t=C),
                                  sw[:, :, :].rearrange("p j (n t) -> p (j n) t", t=C), ALU.mult))
            st.do(v.tensor_copy(S.pc[:, :, :], sw[:, :, :].rearrange("p j (n t) -> p j n t", t=C)[:, :, :, C - 1]))
            dve.wait_ge(s_exp, 3)
            st.do(v.tensor_tensor(S.bs[:, :, :], icl[:, :, :], cum[:, :, :], ALU.mult))
            st.do(v.tensor_tensor(S.ks[:, :, :], K, cum[:, :, :], ALU.mult))
            st.settle()
            for j in range(HP):
                dve.wait_ge(s_rsum, j + 1)
                st.do(v.tensor_tensor(R[:, j, :], S.ps[:, 4 + j, :], V[:, j, :], ALU.mult))


def norm_step(S, dve, v, st, step, half):
    y = S.y_chunk[:, half * NCH // 2:(half + 1) * NCH // 2, :, :].rearrange("p c j i -> p (c j) i")
    mean, var, sq = S.y_mean[:, half, :], S.y_var[:, half, :], S.y_sq
    if st.last:
        st.settle()
    if step == 0:
        st.do(v.tensor_reduce(mean, y, AX, ALU.add))
        st.settle()
        st.do(v.tensor_scalar(mean, mean, 1.0 / HD, None, ALU.mult))
    elif step == 1:
        st.do(v.tensor_tensor(y, y, bc(mean, 2, HD), ALU.subtract))
    elif step == 2:
        st.do(v.tensor_tensor(sq, y, y, ALU.mult))
    elif step == 3:
        st.do(v.tensor_reduce(var, sq, AX, ALU.add))
        st.settle()
        st.do(v.tensor_scalar(var, var, 1.0 / HD, GN_EPS, ALU.mult, ALU.add))
        st.settle()
        st.do(v.reciprocal(var, var), S.y_var_ready)
    else:
        dve.wait_ge(S.y_std_ready, half + 1)
        st.do(v.tensor_tensor(y, y, bc(var, 2, HD), ALU.mult), S.y_normed)


def scan(nc, S, dram):
    sem = S.sem
    with ExitStack() as ctx:
        def sb(name, shape, dt=F32):
            return ctx.enter_context(nc.sbuf_tensor(name, shape, dt))

        HC = NCH // 2
        bbd = sb("b_bd", [P, HC, HP, P])
        kbd = sb("k_bd", [P, HC, HP, P])
        abd = sb("a_bd", [P, HC, HP, P])
        rbd = sb("r_bd", [P, HC, HP, P])
        aktbd = sb("akt_bd", [P, HC, HP, P])
        rbtbd = sb("rbt_bd", [P, HC, HP, P])
        rktbd = sb("rkt_bd", [P, HC, HP, P])
        btbd = sb("bt_bd", [P, HC, HP, P])
        ktbd = sb("kt_bd", [P, 2, HP, P])
        lbd = sb("l_bd", [P, HC, HP, P])
        tbd = S.mixed[:, 0:4, :].rearrange("p c (j t) -> p c j t", j=HP)
        xbd, ttbd = bbd, kbd
        prod = sb("v_products", [P, HC, 3, HP, HD])
        S.y_sq = S.zm[:, 8:10, :].rearrange("p a (g i) -> p (a g) i", i=HD)
        st_s = S.zm[:, 10, :].rearrange("p (w j i) -> p w j i", w=2, j=HP)
        o1 = S.zm[:, 11, 0:HP * HD].rearrange("p (j i) -> p j i", j=HP)
        us = S.zm[:, 11, HP * HD:].rearrange("p (j i) -> p j i", j=HP)
        pre = S.zm[:, 12, 0:HP * HD].rearrange("p (j i) -> p j i", j=HP)
        s_zero, s_bd, s_bda, s_g, s_gev, s_tr, s_trev = (sem("s_zero"), sem("s_bd"), sem("s_bda"), sem("s_g"),
                                                         sem("s_gev"), sem("s_tr"), sem("s_trev"))
        s_pr, s_prev = sem("s_pr"), sem("s_prev")
        s_tt0, s_eye, s_turn, s_turned = sem("s_tt0"), sem("s_eye"), sem("s_turn"), sem("s_turned")
        s_x, s_xbd, s_y, s_yadd, s_yr, s_yrc = (sem("s_x"), sem("s_xbd"), sem("s_y"), sem("s_yadd"), sem("s_yr"),
                                                sem("s_yrc"))
        s_o1, s_o1c, s_u, s_uc, s_s, s_snew, s_yo, s_yc = (sem("s_o1"), sem("s_o1c"), sem("s_u"), sem("s_uc"),
                                                           sem("s_s"), sem("s_snew"), sem("s_yo"), sem("s_yc"))
        NL = 5
        par = [slice(0, C), slice(C, P)]
        block = ctx.enter_context(nc.Block())
        yb = S.y_chunk
        row = "p j t -> p (j t)"

        def blocks(bank):
            return S.ps[:, bank, :].rearrange("p (j t) -> p j t", j=HP)

        @block.gpsimd
        def _(pool):
            st = Steps(pool, S.own_pool, S.counts)
            for buf in (bbd, kbd, lbd, rbtbd, aktbd, rktbd, abd, rbd):
                st.do(pool.memset(buf[:, :, :, :], 0.0), s_zero)
            st.do(pool.memset(st_s[:, 0, :, :], 0.0), s_zero)
            for ch in range(NCH):
                pool.wait_ge(s_tt0, 2 * (ch + 1))
                st.do(pool.tensor_tensor(ttbd[:, ch % HC], ttbd[:, ch % HC], bc(S.const("ident"), 1, HP), ALU.add),
                      s_eye)
            bonus = S.zm[:, 0:HP, :]
            st.do(pool.tensor_tensor(bonus, bonus, bc(S.param_all("gn_b"), 2, T), ALU.add))

        @block.tensor
        def _(pe):
            def products(ch):
                c = ch % HC
                pe.wait_ge(s_gev, 8 * (ch + 1))
                pe.wait_ge(s_trev, 2 * (ch + 1))
                if ch >= 1:
                    pe.wait_ge(s_prev, 3 * ch)
                for o, lhs in enumerate((aktbd[:, c], rktbd[:, c], ktbd[:, c % 2])):
                    for j in range(HP):
                        at = (o % 2) * HP * HD + j * HD
                        last = two_heads(nc, S.ps[:, 6 + o // 2, at:at + HD], lhs[:, j, :], S.v_chunk[:, ch, j, :])
                last.then_inc(s_pr, 1)

            for half in range(2):
                pe.wait_ge(s_bd, 4 * (half + 1))
                if half:
                    pe.wait_ge(s_yc, HC)
                    pe.wait_ge(s_snew, 2 * HC)
                for c in range(HC):
                    ch = half * HC + c
                    if ch >= 2:
                        pe.wait_ge(s_gev, 8 * (ch - 1))
                    for j in range(HP):
                        nc.tensor.matmul(S.ps[:, c % 2, j * P:(j + 1) * P], bbd[:, c, j, :],
                                         S.ra[:, j, ch, :, :].rearrange("p w t -> p (w t)"), start=True, stop=True)
                    for j in range(HP):
                        last = nc.tensor.matmul(S.ps[:, 2 + c % 2, j * P:(j + 1) * P], kbd[:, c, j, :],
                                                S.ra[:, j, ch, :, :].rearrange("p w t -> p (w t)"),
                                                start=True, stop=True)
                    last.then_inc(s_g, 1)
                    if ch >= 1:
                        pe.wait_ge(s_trev, 2 * ch)
                    for j in range(HP):
                        nc.tensor.transpose(S.ps[:, 4, j * P:(j + 1) * P], bbd[:, c, j, :], S.const("ident"))
                    for j in range(HP):
                        last = nc.tensor.transpose(S.ps[:, 5, j * P:(j + 1) * P], kbd[:, c, j, :], S.const("ident"))
                    last.then_inc(s_tr, 1)
                    if c:
                        products(ch - 1)
                products(half * HC + HC - 1)
                pe.wait_ge(s_prev, 3 * HC * (half + 1))
                for level in range(NL):
                    n = HC * (half * NL + level)

                    def turn(c, src):
                        for j in range(HP):
                            last = nc.tensor.transpose(blocks(4 + c)[:, j, :], src[:, c, j, :], S.const("ident"))
                        last.then_inc(s_turn, 1)

                    if level == 0:
                        for c in range(HC):
                            pe.wait_ge(s_eye, half * HC + c + 1)
                            turn(c, ttbd)
                    for c in range(HC):
                        if level == 0:
                            pe.wait_ge(s_turned, n + c + 1)
                        else:
                            pe.wait_ge(s_yadd, n - HC + c + 1)
                        if n + c >= 2:
                            pe.wait_ge(s_xbd, n + c - 1)
                        for j in range(HP):
                            last = nc.tensor.matmul(blocks(c % 2)[:, j, :], lbd[:, c, j, :], tbd[:, c, j, :],
                                                    start=True, stop=True)
                        last.then_inc(s_x, 1)
                    if level:
                        for c in range(HC):
                            turn(c, tbd)
                    for c in range(HC):
                        pe.wait_ge(s_xbd, n + c + 1)
                        pe.wait_ge(s_turned, n + c + 1)
                        if n + c >= 2:
                            pe.wait_ge(s_yadd, n + c - 1)
                        for j in range(HP):
                            ops = ((ttbd, xbd), (xbd, ttbd))[level == NL - 1]
                            last = nc.tensor.matmul(blocks(2 + c % 2)[:, j, :], ops[0][:, c, j, :], ops[1][:, c, j, :],
                                                    start=True, stop=True)
                        last.then_inc(s_y, 1)
                pe.wait_ge(s_yadd, HC * NL * (half + 1))
                pe.wait_ge(s_bda, 4 * (half + 1))
                for c in range(HC):
                    ch = half * HC + c
                    if ch:
                        pe.wait_ge(s_snew, 2 * ch)
                    for j in range(HP):
                        last = two_heads(nc, S.ps[:, 0, j * HD:(j + 1) * HD], abd[:, c, j, :], st_s[:, ch % 2, j, :])
                    last.then_inc(s_o1, 1)
                    if ch:
                        pe.wait_ge(s_yrc, ch)
                    for j in range(HP):
                        last = two_heads(nc, S.ps[:, 5, j * HD:(j + 1) * HD], rbd[:, c, j, :], st_s[:, ch % 2, j, :])
                    last.then_inc(s_yr, 1)
                    pe.wait_ge(s_o1c, ch + 1)
                    for j in range(HP):
                        last = two_heads(nc, S.ps[:, 1, j * HD:(j + 1) * HD], kbd[:, c, j, :], o1[:, j, :])
                    last.then_inc(s_u, 1)
                    pe.wait_ge(s_uc, ch + 1)
                    for j in range(HP):
                        last = two_heads(nc, S.ps[:, 4, j * HD:(j + 1) * HD], btbd[:, c, j, :], us[:, j, :])
                    last.then_inc(s_s, 1)
                    if ch >= 2:
                        pe.wait_ge(s_yc, ch - 1)
                    for j in range(HP):
                        last = two_heads(nc, S.ps[:, 2 + ch % 2, j * HD:(j + 1) * HD], rbtbd[:, c, j, :], us[:, j, :])
                    last.then_inc(s_yo, 1)

        @block.scalar
        def _(act):
            st = Steps(act, S.own_act, S.counts)
            for half in range(2):
                chunks = slice(half * HC, (half + 1) * HC)
                def take_products(ch):
                    act.wait_ge(s_pr, ch + 1)
                    c = ch % HC
                    for o in range(3):
                        at = (o % 2) * HP * HD
                        st.do(act.activation(prod[:, c, o, :, :].rearrange(row),
                                             S.ps[:, 6 + o // 2, at:at + HP * HD], ACT.Copy), s_prev)

                if half:
                    act.wait_ge(s_yo, HC)
                    act.wait_ge(s_yc, HC)
                    act.wait_ge(s_snew, 2 * HC)
                for c in range(HC):
                    ch = half * HC + c
                    act.wait_ge(s_tr, ch + 1)
                    if c >= 2:
                        act.wait_ge(s_pr, ch - 1)
                    for dst, bank in ((btbd[:, c], 4), (ktbd[:, c % 2], 5)):
                        st.do(act.activation(dst.rearrange(row), S.ps[:, bank, :], ACT.Copy), s_trev)
                    if c:
                        take_products(ch - 1)
                take_products(half * HC + HC - 1)
                act.wait_ge(s_zero, 9)
                spread_out = [(w, dst, e) for w, dst in ((0, abd), (1, rbd)) for e in range(2)]
                for level in range(NL):
                    for c in range(HC):
                        act.wait_ge(s_turn, HC * (half * NL + level) + c + 1)
                        st.do(act.activation((ttbd if level else tbd)[:, c].rearrange(row), S.ps[:, 4 + c, :],
                                             ACT.Copy), s_turned)
                    if half and level == NL - 1:
                        act.wait_ge(S.y_var_ready, 1)
                        st.do(act.activation(S.y_var[:, 0, :], S.y_var[:, 0, :], ACT.Sqrt), S.y_std_ready)
                    if level < len(spread_out):
                        w, dst, e = spread_out[level]
                        st.do(act.activation(dst[par[e], :, :, par[e]],
                                             S.ra[par[e], :, chunks, w, :].rearrange("p j c t -> p c j t"),
                                             ACT.Copy), s_bda)
                for c in range(HC):
                    ch = half * HC + c
                    act.wait_ge(s_u, ch + 1)
                    st.do(act.activation(us[:, :, :].rearrange(row), S.ps[:, 1, 0:HP * HD], ACT.Copy), s_uc)

        @block.vector
        def _(dve):
            st = Steps(dve, S.own_dve, S.counts)
            v = nc.vector
            for half in range(2):
                if half:
                    dve.wait_ge(s_yo, HC)
                for i, (dst, src) in enumerate(((bbd, S.bs), (kbd, S.ks))):
                    if not half:
                        dve.wait_ge(s_zero, i + 1)
                    for e in range(2):
                        st.do(v.tensor_copy(dst[par[e], :, :, par[e]],
                                            src[par[e], :, half * HC * C:(half + 1) * HC * C].rearrange(
                                                "p j (c t) -> p c j t", t=C)), s_bd)
                for c in range(HC):
                    ch = half * HC + c
                    dve.wait_ge(s_g, ch + 1)
                    g1 = S.ps[:, c % 2, :].rearrange("p (j w t) -> p j w t", j=HP, w=2)
                    g2 = S.ps[:, 2 + c % 2, :].rearrange("p (j w t) -> p j w t", j=HP, w=2)
                    for i, (dst, src, w, m) in enumerate(((lbd, g1, 0, "strict"), (rbtbd, g1, 1, "inclusive"),
                                                          (aktbd, g2, 0, "strict"), (rktbd, g2, 1, "inclusive"))):
                        if not ch:
                            dve.wait_ge(s_zero, 3 + i)
                        for e in range(2):
                            st.do(v.tensor_tensor(dst[par[e], c, :, par[e]], src[par[e], :, w, :],
                                                  bc(S.const(m)[par[e], :], 1, HP), ALU.mult), s_gev)
                        if i == 0:
                            lt_ready = st.last
                    dve.wait_ge(s_tr, ch + 1)
                    dve.wait_ge(*lt_ready)
                    for e in range(2):
                        st.do(v.tensor_tensor(ttbd[par[e], c, :, par[e]], lbd[par[e], c, :, par[e]],
                                              bc(S.const("level0_t")[par[e], :], 1, HP), ALU.mult), s_tt0)
                for level in range(NL):
                    n = HC * (half * NL + level)
                    for c in range(HC):
                        dve.wait_ge(s_x, n + c + 1)
                        st.do(v.tensor_tensor(xbd[:, c].rearrange("p j (e t) -> p (j e) t", e=2),
                                              S.ps[:, c % 2, :].rearrange("p (a t) -> p a t", t=C),
                                              bc(S.const(f"level{level + 1}"), 1, 2 * HP), ALU.mult), s_xbd)
                    for c in range(HC):
                        dve.wait_ge(s_y, n + c + 1)
                        to = ttbd if level == NL - 1 else tbd
                        st.do(v.tensor_tensor(to[:, c], to[:, c], blocks(2 + c % 2), ALU.add), s_yadd)
                        if half and c == 1 and level < NL - 1:
                            norm_step(S, dve, v, st, level, 0)
                if half:
                    norm_step(S, dve, v, st, NL - 1, 0)
                if not half:
                    dve.wait_ge(s_zero, 9)
                dve.wait_ge(s_prev, 3 * HC * (half + 1))

                def take_y(ch):
                    dve.wait_ge(s_yo, ch + 1)
                    st.do(v.tensor_tensor(yb[:, ch, :, :].rearrange(row), S.ps[:, 2 + ch % 2, 0:HP * HD],
                                          prod[:, ch % HC, 1, :, :].rearrange(row), ALU.add), s_yc)

                for c in range(HC):
                    ch = half * HC + c
                    old, new = st_s[:, ch % 2, :, :], st_s[:, (ch + 1) % 2, :, :]
                    dve.wait_ge(s_o1, ch + 1)
                    st.do(v.tensor_tensor(o1[:, :, :].rearrange(row), S.ps[:, 0, 0:HP * HD],
                                          prod[:, c, 0, :, :].rearrange(row), ALU.add), s_o1c)
                    st.do(v.tensor_tensor(pre, old, prod[:, c, 2, :, :], ALU.add))
                    if c:
                        take_y(ch - 1)
                    dve.wait_ge(s_yr, ch + 1)
                    y_v = prod[:, c, 1, :, :].rearrange(row)
                    st.do(v.tensor_tensor(y_v, y_v, S.ps[:, 5, 0:HP * HD], ALU.add), s_yrc)
                    st.settle()
                    dve.wait_ge(s_s, ch + 1)
                    st.do(v.tensor_tensor(new.rearrange(row), pre.rearrange(row), S.ps[:, 4, 0:HP * HD], ALU.add),
                          s_snew)
                    st.settle()
                    st.do(v.tensor_tensor(new, new, bc(S.pc[:, :, ch], 2, HD), ALU.mult), s_snew)
                    st.settle()
                take_y(half * HC + HC - 1)


def normalise_heads(nc, S, dram):
    sem = S.sem
    s_tr = sem("n_tr")
    with nc.Block() as block:
        M = S.mixed

        def turned(q, a, pp, h):
            src = S.ps[:, 2 * a + q, :].rearrange("p (c h t) -> p c h t", c=4, h=2)
            return (M[h * HD:(h + 1) * HD, 2 * a + pp, q * 256:(q + 1) * 256].rearrange("p (c t) -> p c t", t=C),
                    src[pp * HD:(pp + 1) * HD, :, h, :])

        @block.vector
        def _(dve):
            st = Steps(dve, S.own_dve, S.counts)
            v = nc.vector
            for step in range(5):
                norm_step(S, dve, v, st, step, 1)
            for a in range(2):
                dve.wait_ge(s_tr, 2 + a + 1)
                for pp in range(2):
                    for h in range(2):
                        st.do(v.tensor_copy(*turned(1, a, pp, h)))
            st.settle()
            dve.wait_ge(S.y_taken, 8)
            for j in range(HP):
                st.do(v.scalar_tensor_tensor(M[:, j, :], M[:, j, :], S.param("gn_w", j), S.zm[:, j, :],
                                             ALU.mult, ALU.add))
            st.settle()
            st.do(v.tensor_tensor(M[:, 0:HP, :], M[:, 0:HP, :], S.gate[:, :, :], ALU.mult))

        @block.scalar
        def _(act):
            st = Steps(act, S.own_act, S.counts)
            for a in range(2):
                act.wait_ge(s_tr, a + 1)
                for pp in range(2):
                    for h in range(2):
                        to, src = turned(0, a, pp, h)
                        st.do(act.activation(to, src, ACT.Copy), S.y_taken)
                if a == 0:
                    act.wait_ge(S.y_var_ready, 2)
                    st.do(act.activation(S.y_var[:, 1, :], S.y_var[:, 1, :], ACT.Sqrt), S.y_std_ready)

        @block.tensor
        def _(pe):
            for q in range(2):
                pe.wait_ge(S.y_normed, q + 1)
                for a in range(2):
                    for c in range(4):
                        last = nc.tensor.transpose(
                            S.ps[:, 2 * a + q, c * P:(c + 1) * P],
                            S.y_chunk[:, 4 * q + c, 2 * a:2 * a + 2, :].rearrange("p j i -> p (j i)"),
                            S.const("ident"))
                    last.then_inc(s_tr, 1)


def mix(nc, S, dram):
    sem = S.sem
    with ExitStack() as ctx:
        def sb(name, shape, dt=F32):
            return ctx.enter_context(nc.sbuf_tensor(name, shape, dt))

        mx_hi = sb("mixed_hi", [P, KT, T], F32R)
        mx_lo = sb("mixed_lo", [P, KT, T], F32R)
        raw = sb("wout_raw", [P, 4, D])
        w_hi = sb("wout_hi", [P, SPL, D], F32R)
        w_lo = sb("wout_lo", [P, SPL, D], F32R)
        xs = raw
        sq = sb("h_sq", [P, D])
        ss = sb("h_ss", [P, TT])
        s_x = sem("m_x")
        s_raw = [sem(f"m_raw{i}") for i in range(4)]
        s_mhi, s_mlo, s_hi, s_lo, s_mm, s_res = (sem("m_mhi"), sem("m_mlo"), sem("m_hi"), sem("m_lo"),
                                                 sem("m_mm"), sem("m_res"))
        s_ss, s_norm, s_sc, s_tr, s_thi, s_tlo = (sem("m_ss"), sem("m_norm"), sem("m_sc"),
                                                        sem("m_tr"), sem("m_thi"), sem("m_tlo"))
        block = ctx.enter_context(nc.Block())

        @block.sync
        def _(sp):
            for k in range(KT):
                if k >= 4:
                    sp.wait_ge(s_lo, k - 3)
                sp.dma_start(raw[:, k % 4, :], dram["wout"][k]).then_inc(s_raw[k % 4], 16)
                if k == 3:
                    sp.dma_start(S.h[:, :, :], dram["x"]).then_inc(s_x, 16)
            for n in range(RQ):
                sp.dma_start(S.wq_raw[:, n, :], dram["wq_t"][n]).then_inc(S.wq_in[n], 16)

        @block.scalar
        def _(act):
            st = Steps(act, S.own_act, S.counts)
            for k in range(KT):
                st.do(act.activation(mx_hi[:, k, :], S.mixed[:, k, :], ACT.Copy), s_mhi)
                act.wait_ge(s_raw[k % 4], 16 * (k // 4 + 1))
                if k >= SPL:
                    act.wait_ge(s_mm, k - SPL + 1)
                st.do(act.activation(w_hi[:, k % SPL, :], raw[:, k % 4, :], ACT.Copy), s_hi)
            for t in range(TT):
                act.wait_ge(s_res, 2 * t + 2)
                if t:
                    st.settle()
                st.do(act.activation(sq[:, :], S.h[:, t, :], ACT.Square, accum_out=ss[:, t:t + 1]), s_ss)
            act.wait_ge(s_norm, 1)
            st.do(act.activation(ss[:, :], ss[:, :], ACT.Sqrt), s_norm)
            for k in range(KT):
                act.wait_ge(s_tr, k + 1)
                st.do(act.activation(S.xn_hi[:, k, :], S.ps[:, k, :], ACT.Copy, scale=S.param("g_ffn", k)), s_thi)

        @block.vector
        def _(dve):
            st = Steps(dve, S.own_dve, S.counts)
            v = nc.vector
            for k in range(KT):
                dve.wait_ge(s_mhi, k + 1)
                st.do(v.tensor_tensor(mx_lo[:, k, :], S.mixed[:, k, :], mx_hi[:, k, :].bitcast(F32), ALU.subtract),
                      s_mlo)
                dve.wait_ge(s_hi, k + 1)
                st.do(v.tensor_tensor(w_lo[:, k % SPL, :], raw[:, k % 4, :], w_hi[:, k % SPL, :].bitcast(F32),
                                      ALU.subtract), s_lo)
            dve.wait_ge(s_x, 16)
            for o in range(8):
                t, d = divmod(o, 2)
                dve.wait_ge(s_mm, KT + o)
                st.do(v.tensor_tensor(S.h[:, t, d * T:(d + 1) * T], S.h[:, t, d * T:(d + 1) * T], S.ps[:, o, :],
                                      ALU.add), s_res)
            dve.wait_ge(s_ss, TT)
            st.do(v.tensor_scalar(ss[:, :], ss[:, :], 1.0 / D, RMS_EPS, ALU.mult, ALU.add))
            st.settle()
            st.do(v.reciprocal(ss[:, :], ss[:, :]), s_norm)
            dve.wait_ge(s_norm, 2)
            for t in range(TT):
                st.do(v.tensor_scalar(xs[:, t, :], S.h[:, t, :], ss[:, t:t + 1], None, ALU.mult), s_sc)
            for k in range(KT):
                dve.wait_ge(s_thi, k + 1)
                st.do(v.scalar_tensor_tensor(S.xn_lo[:, k, :], S.ps[:, k, :], S.param("g_ffn", k),
                                             S.xn_hi[:, k, :].bitcast(F32), ALU.mult, ALU.subtract), s_tlo)

        @block.tensor
        def _(pe):
            for k in range(KT):
                pe.wait_ge(s_mlo, k + 1)
                pe.wait_ge(s_lo, k + 1)
                for o in range(8):
                    t, d = divmod(o, 2)
                    x, w = slice(t * P, (t + 1) * P), slice(d * T, (d + 1) * T)
                    last = three_pass(nc, S.ps[:, o, :], mx_hi[:, k, x], mx_lo[:, k, x], w_hi[:, k % SPL, w],
                                      w_lo[:, k % SPL, w], k == 0, k == KT - 1)
                    if k == KT - 1 or o == 7:
                        last.then_inc(s_mm, 1)
            pe.wait_ge(s_res, 8)
            pe.wait_ge(s_sc, TT)
            for k in range(KT):
                for t in range(TT):
                    last = nc.tensor.transpose(S.ps[:, k, t * P:(t + 1) * P], xs[:, t, k * P:(k + 1) * P],
                                               S.const("ident"))
                last.then_inc(s_tr, 1)


def route(nc, S, dram):
    sem = S.sem
    NQ = 2 * PH
    NW = NQ + NST
    NM = PH // 2
    TH = 2 * TT
    with ExitStack() as ctx:
        def sb(name, shape, dt=F32):
            return ctx.enter_context(nc.sbuf_tensor(name, shape, dt))

        raw = S.wq_raw
        w_hi = sb("wq_hi", [P, SPL, D], F32R)
        w_lo = sb("wq_lo", [P, SPL, D], F32R)
        keys = sb("sub_keys", [P, 2, NKEY])
        qt = sb("q_t", [P, 4, T])
        sc = sb("key_scores", [P, 2, TT, 2, NKEY])
        sc2 = sb("key_scores_left", [P, TT, 2, NKEY])
        top = sb("top_scores", [P, TT, PH, 2, TOPK])
        topi = sb("top_index", [P, TT, PH, 2, TOPK], U32)
        cand = sb("cand", [P, TT, NCAND])
        cand2 = sb("cand_left", [P, TT, NCAND])
        best = sb("best", [P, TT, PH, TOPK])
        pos = sb("pos", [P, TT, PH, TOPK], U32)
        bits = sb("pos_bits", [P, 2, TH * TOPK], U32)
        posf = sb("pos_f", [P, 3, TH * TOPK])
        acc = sb("pos_acc", [P, 2, TH * TOPK])
        keyf = sb("key_table", [P, 2, TH, TOPK])
        delta = sb("row_steps", [P, TH, TOPK])
        wide = [sb(f"lookup{w}", [P, TH * TOPK, TOPK]) for w in range(2)]
        ex = sb("best_exp", [P, TT * PH, TOPK])
        small = sb("exp_sum", [P, TT * PH])
        tab = S.mixed[:, 0:3, :].rearrange("p w (t k) -> p w t k", k=PH * TOPK)
        s_k = sem("q_k")
        s_raw = S.wq_in
        s_hi, s_lo, s_mm, s_q, s_s, s_sev, s_top = (sem("q_hi"), sem("q_lo"), sem("q_mm"), sem("q_q"), sem("q_s"),
                                                    sem("q_sev"), sem("q_top"))
        s_sub, s_e, s_eq, s_mul, s_keys, s_tr, s_out = (
            sem("q_sub"), sem("q_e"), sem("q_eq"), sem("q_mul"), sem("q_keys"), sem("q_tr"), sem("q_out"))
        block = ctx.enter_context(nc.Block())

        @block.sync
        def _(sp):
            sp.dma_start(keys[:, :, :], dram["keys_t"]).then_inc(s_k, 16)
            for n in range(NW):
                if n >= RQ:
                    sp.wait_ge(s_lo, n - RQ + 1)
                else:
                    continue
                src = dram["wq_t"][n] if n < NQ else dram["u_t"][:, n - NQ, :]
                sp.dma_start(raw[:, n % RQ, :], src).then_inc(s_raw[n % RQ], 16)

        @block.gpsimd
        def _(pool):
            st = Steps(pool, S.own_pool, S.counts)

            def weigh(m):
                for w in range(2):
                    pool.wait_ge(s_eq, 2 * m + w + 1)
                    x = wide[w][:, :, :].rearrange("p (h k) b -> p h k b", k=TOPK)
                    st.do(pool.tensor_tensor(x, x, bc((delta[:, :, :], keyf[:, 1, :, :])[w], 2, TOPK), ALU.mult),
                          s_mul)

            for n in range(NW):
                pool.wait_ge(s_hi, n + 1)
                st.do(pool.tensor_tensor(w_lo[:, n % SPL, :], raw[:, n % RQ, :], w_hi[:, n % SPL, :].bitcast(F32),
                                         ALU.subtract), s_lo)
                for m, after in enumerate((10, NQ - 1, NQ + 5)):
                    if n == after:
                        weigh(m)

        @block.scalar
        def _(act):
            st = Steps(act, S.own_act, S.counts)

            def take_q(n):
                act.wait_ge(s_mm, n + 1)
                if n >= 4:
                    act.wait_ge(s_s, n // 2 - 1)
                st.do(act.activation(qt[:, n % 4, :], S.ps[:, n % 3, :], ACT.Copy), s_q)

            def take_scores(h):
                act.wait_ge(s_s, h + 1)
                if h >= 2:
                    act.wait_ge(s_top, h - 1)
                for c in range(2):
                    st.do(act.activation(sc[:, h % 2, :, c, :],
                                         S.ps[:, 3 + c, :].rearrange("p (t k) -> p t k", k=NKEY), ACT.Copy), s_sev)

            def take_hidden(n):
                act.wait_ge(s_mm, n + 1)
                st.do(act.activation(S.stash[:, n - NQ, :], S.ps[:, n % 3, :], ACT.Gelu), s_q)

            for n in range(NW + 1):
                if n < NW:
                    act.wait_ge(s_raw[n % RQ], 16 * (n // RQ + 1))
                    if n >= SPL:
                        act.wait_ge(s_mm, n - SPL + 1)
                    st.do(act.activation(w_hi[:, n % SPL, :], raw[:, n % RQ, :], ACT.Copy), s_hi)
                if n == NW - 2:
                    act.wait_ge(s_sub, 1)
                    st.do(act.activation(ex[:, :, :], ex[:, :, :], ACT.Exp), s_e)
                if n > NQ:
                    take_hidden(n - 1)
                elif n >= 1:
                    take_q(n - 1)
                    if n % 2 == 0:
                        take_scores(n // 2 - 1)
            for i, w in enumerate((1, 0, 2)):
                act.wait_ge(s_tr, i + 1)
                st.do(act.activation(S.tab[:, w, :], S.ps[:, 5 + w, :], ACT.Copy), s_out)

        @block.tensor
        def _(pe):
            pe.wait_ge(s_k, 16)

            def scores(h):
                pe.wait_ge(s_q, 2 * h + 2)
                if h >= 1:
                    pe.wait_ge(s_sev, 2 * h)
                for c in range(2):
                    for t in range(TT):
                        last = nc.tensor.matmul(S.ps[:, 3 + c, t * P:(t + 1) * P],
                                                qt[:, (2 * h + c) % 4, t * P:(t + 1) * P], keys[:, c, :],
                                                start=True, stop=True)
                last.then_inc(s_s, 1)

            for n in range(NW):
                pe.wait_ge(s_lo, n + 1)
                if n >= 3:
                    pe.wait_ge(s_q, n - 2)
                for k in range(KT):
                    w = slice(k * P, (k + 1) * P)
                    last = three_pass(nc, S.ps[:, n % 3, :], w_hi[:, n % SPL, w], w_lo[:, n % SPL, w],
                                      S.xn_hi[:, k, :], S.xn_lo[:, k, :], k == 0, k == KT - 1)
                last.then_inc(s_mm, 1)
                if n < NQ and n % 2:
                    scores(n // 2)
            for w in (1, 0, 2):
                pe.wait_ge(s_keys, (2 * NM, 2 * NM - 1, 2 * NM + 1)[w])
                for t in range(TT):
                    last = nc.tensor.transpose(S.ps[:, 5 + w, t * P:(t + 1) * P], tab[:, w, t, :], S.const("ident"))
                last.then_inc(s_tr, 1)

        @block.vector
        def _(dve):
            st = Steps(dve, S.own_dve, S.counts)
            v = nc.vector
            both = [(t, c) for t in range(TT) for c in range(2)]

            def mark(m):
                pair = slice(2 * m, 2 * m + 2)
                st.do(v.tensor_copy(posf[:, 0, :].rearrange("p (t x) -> p t x", t=TT),
                                    pos[:, :, pair, :].rearrange("p t h k -> p t (h k)")))
                for i, low in enumerate((7, 3)):
                    st.do(v.tensor_scalar(bits[:, i, :].rearrange("p (t x) -> p t x", t=TT),
                                          pos[:, :, pair, :].rearrange("p t h k -> p t (h k)"), low, None,
                                          ALU.bitwise_and))
                for c in range(2):
                    st.do(v.tensor_copy(keyf[:, c, :, :].rearrange("p (t h) k -> p t h k", t=TT),
                                        topi[:, :, pair, c, :]))
                st.settle()
                starts, p_ = bc(S.const("row_starts"), 1, TH * TOPK), bc(posf[:, 0, :], 2, TOPK)
                st.do(v.tensor_tensor(wide[0][:, :, :], p_, starts, ALU.is_ge))
                st.do(v.tensor_copy(delta[:, :, 0:1], keyf[:, 0, :, 0:1]))
                st.do(v.tensor_tensor(delta[:, :, 1:TOPK], keyf[:, 0, :, 1:TOPK], keyf[:, 0, :, 0:TOPK - 1],
                                      ALU.subtract), s_eq)
                st.do(v.tensor_copy(posf[:, 1:3, :], bits[:, :, :]))
                st.do(v.tensor_scalar(acc[:, 1, :], posf[:, 0, :], 16.0, None, ALU.is_lt))
                st.settle()
                st.do(v.tensor_tensor(posf[:, 2, :], posf[:, 2, :], posf[:, 1, :], ALU.subtract))
                st.settle()
                st.do(v.scalar_tensor_tensor(acc[:, 0, :], posf[:, 0, :], 40.0, posf[:, 2, :], ALU.is_ge, ALU.mult))
                st.settle()
                st.do(v.tensor_tensor(acc[:, 0, :], acc[:, 0, :], posf[:, 1, :], ALU.add))
                st.settle()
                st.do(v.scalar_tensor_tensor(acc[:, 0, :], posf[:, 0, :], 56.0, acc[:, 0, :], ALU.is_lt, ALU.mult))
                st.settle()
                st.do(v.tensor_tensor(posf[:, 1, :], posf[:, 0, :], acc[:, 0, :], ALU.subtract))
                st.settle()
                st.do(v.tensor_tensor(posf[:, 1, :], posf[:, 1, :], acc[:, 1, :], ALU.mult))
                st.settle()
                st.do(v.tensor_tensor(acc[:, 0, :], posf[:, 1, :], acc[:, 0, :], ALU.add))
                st.settle()
                st.do(v.tensor_tensor(wide[1][:, :, :], bc(S.const("iota")[:, 0:TOPK], 1, TH * TOPK),
                                      bc(acc[:, 0, :], 2, TOPK), ALU.is_equal), s_eq)

            def add_up(m, w):
                st.do(v.tensor_reduce(tab[:, w, :, m * 2 * TOPK:(m + 1) * 2 * TOPK],
                                      wide[w][:, :, :].rearrange("p (t x) b -> p t x b", t=TT), AX, ALU.add),
                      s_keys)

            for h in range(PH):
                dve.wait_ge(s_sev, 2 * h + 2)
                for t, c in both:
                    st.do(v.max(top[:, t, h, c, 0:8], sc[:, h % 2, t, c, :]))
                st.settle()
                for t, c in both:
                    st.do(v.max_index(topi[:, t, h, c, 0:8], top[:, t, h, c, 0:8], sc[:, h % 2, t, c, :]))
                    st.do(v.match_replace(sc2[:, t, c, :], top[:, t, h, c, 0:8], sc[:, h % 2, t, c, :], LOWEST))
                st.settle()
                for t, c in both:
                    st.do(v.max(top[:, t, h, c, 8:16], sc2[:, t, c, :]))
                st.settle()
                for t, c in both:
                    st.do(v.max_index(topi[:, t, h, c, 8:16], top[:, t, h, c, 8:16], sc2[:, t, c, :]))
                s0, s1 = top[:, :, h, 0, :], top[:, :, h, 1, :]
                for lo, a0, na, nb in ((0, 0, 1, 16), (16, 1, 3, 8), (40, 4, 4, 4), (56, 8, 8, 1)):
                    out = cand[:, :, lo:lo + na * nb].rearrange("p t (a b) -> p t a b", b=nb)
                    st.do(v.tensor_tensor(out, bc(s0[:, :, a0:a0 + na], 3, nb), bc(s1[:, :, 0:nb], 2, na), ALU.add))
                st.settle()
                for t in range(TT):
                    st.do(v.max(best[:, t, h, 0:8], cand[:, t, :]))
                st.settle()
                for t in range(TT):
                    st.do(v.max_index(pos[:, t, h, 0:8], best[:, t, h, 0:8], cand[:, t, :]))
                    st.do(v.match_replace(cand2[:, t, :], best[:, t, h, 0:8], cand[:, t, :], LOWEST))
                st.settle()
                for t in range(TT):
                    st.do(v.max(best[:, t, h, 8:16], cand2[:, t, :]))
                st.settle()
                for t in range(TT):
                    last = v.max_index(pos[:, t, h, 8:16], best[:, t, h, 8:16], cand2[:, t, :])
                    st.do(last, s_top if t == TT - 1 else None)
                st.settle()
                if h % 2:
                    m = h // 2
                    if m:
                        for w in range(2):
                            dve.wait_ge(s_mul, 2 * m - 1 + w)
                            add_up(m - 1, w)
                        st.settle()
                    if m == NM - 1:
                        bst = best[:, :, :, :].rearrange("p t h k -> p (t h) k")
                        st.do(v.tensor_tensor(ex[:, :, :], bst, bc(bst[:, :, 0], 2, TOPK), ALU.subtract), s_sub)
                    mark(m)
            st.settle()
            for w, table in ((1, keyf[:, 1, :, :]), (0, delta[:, :, :])):
                x = wide[w][:, :, :].rearrange("p (h k) b -> p h k b", k=TOPK)
                st.do(v.tensor_tensor(x, x, bc(table, 2, TOPK), ALU.mult))
                st.settle()
                add_up(NM - 1, w)
            dve.wait_ge(s_e, 1)
            st.do(v.tensor_reduce(small[:, :], ex[:, :, :], AX, ALU.add))
            st.settle()
            st.do(v.reciprocal(small[:, :], small[:, :]))
            st.settle()
            st.do(v.tensor_tensor(tab[:, 2, :, :].rearrange("p t (h k) -> p (t h) k", h=PH), ex[:, :, :],
                                  bc(small[:, :], 2, TOPK), ALU.mult), s_keys)


def spread(nc, S, dram):
    sem = S.sem
    Q = 8
    R = 4
    NQ = SW // Q
    with ExitStack() as ctx:
        def sb(name, shape, dt=F32):
            return ctx.enter_context(nc.sbuf_tensor(name, shape, dt))

        rows = [sb(f"onehot_rows{i}", [P, Q, NKEY]) for i in range(R)]
        cols = [sb(f"gated_cols{i}", [P, Q, NKEY]) for i in range(R)]
        stage = [sb(f"gate_stage{i}", [P, NKEY, SW]) for i in range(2)]
        minus_row = S.mixed[:, 4, :]
        RA = R - 1
        s_onehot, s_rows, s_cols, s_rows_act = sem("w_onehot"), sem("w_rows"), sem("w_cols"), sem("w_rows_act")
        s_minus, s_dist = S.own_dve, S.own_act
        minus_ready = S.counts[s_minus.name] + 1
        dist_before = S.counts[s_dist.name]
        s_used, s_taken = sem("w_used"), sem("w_taken")
        s_out = S.gates_out
        block = ctx.enter_context(nc.Block())
        tab = S.tab
        iota = bc(S.const("iota"), 1, Q)

        def steps(eng, s, step):
            with eng.Fori(0, NQ // R) as i:
                for e in range(R):
                    step(i + s * (NQ // R), e, (R * i + e) * Q)


        @block.vector
        def _(dve):
            Steps(dve, s_minus, S.counts).do(nc.vector.tensor_scalar(minus_row, tab[:, 0, :], -1.0, None, ALU.mult))
            for s in range(NSW):
                def step(r, e, tok):
                    dve.wait_ge(s_used, R * r + e + 1)
                    for w, to, done in ((1, cols[e], s_onehot), (0, rows[e], s_rows))[:1 if e == RA else 2]:
                        nc.vector.tensor_tensor(to[:, :, :], iota, bc(tab[:, w, bass.ds(s * SW + tok, Q)], 2, NKEY),
                                                ALU.is_equal).then_inc(done, 1)

                steps(dve, s, step)

        @block.gpsimd
        def _(pool):
            for s in range(NSW):
                def step(r, e, tok):
                    pool.wait_ge(s_onehot, R * r + e + 1)
                    pool.tensor_tensor(cols[e][:, :, :], cols[e][:, :, :],
                                       bc(tab[:, 2, bass.ds(s * SW + tok, Q)], 2, NKEY), ALU.mult).then_inc(s_cols, 1)

                steps(pool, s, step)

        @block.tensor
        def _(pe):
            pe.nop().then_inc(s_used, R)
            for s in range(NSW):
                def step(r, e, tok):
                    if e == RA:
                        pe.wait_ge(s_rows_act, r + 1)
                    else:
                        pe.wait_ge(s_rows, RA * r + e + 1)
                    pe.wait_ge(s_cols, R * r + e + 1)
                    pe.wait_ge(s_taken, R * r + e + 1)
                    for q in range(Q):
                        b, at = divmod(q * P, T)
                        last = nc.tensor.matmul(S.ps[:, 2 * e + b, at:at + P], rows[e][:, q, :], cols[e][:, q, :],
                                                start=True, stop=True)
                    last.then_inc(s_used, 1)

                steps(pe, s, step)

        @block.scalar
        def _(act):
            act.nop().then_inc(s_taken, R)

            def mark_rows(r, tok):
                act.wait_ge(s_used, R * r + RA + 1)
                for q in range(Q):
                    act.activation(rows[RA][:, q, :], S.const("iota"), ACT.Abs,
                                   bias=minus_row[:, bass.ds(tok + q, 1)]).then_inc(s_dist, 1)
                act.wait_ge(s_dist, Q * (r + 1) + dist_before)
                act.activation(rows[RA][:, :, :], rows[RA][:, :, :], ACT.Relu, bias=1.0,
                               scale=-1.0).then_inc(s_rows_act, 1)

            act.wait_ge(s_minus, minus_ready)
            for s in range(NSW):
                if s >= 2:
                    act.wait_ge(s_out[s % 2], 16 * (s // 2))

                def step(r, e, tok):
                    if e == 0:
                        mark_rows(r, tok + RA * Q + s * SW)
                    act.wait_ge(s_used, R * r + e + R + 1)
                    act.activation(stage[s % 2][:, :, bass.ds(tok, Q)].rearrange("p j t -> p t j"),
                                   S.ps[:, 2 * e:2 * e + 2, :].rearrange("p b (t j) -> p (b t) j", j=NKEY),
                                   ACT.Copy).then_inc(s_taken, 1)

                steps(act, s, step)

        S.counts[s_dist.name] += Q * NSW * NQ // R

        @block.sync
        def _(sp):
            sp.dma_start(S.u_first, dram["u_t"][:, NST:NST + EG, :]).then_inc(S.u_in[0], 16)
            for s in range(NSW):
                sp.wait_ge(s_taken, R + NQ * (s + 1))
                sp.dma_start(dram["gates"][s], stage[s % 2][:, :, :]).then_inc(s_out[s % 2], 16)


def experts(nc, S, dram):
    sem = S.sem
    with ExitStack() as ctx:
        def sb(name, shape, dt=F32):
            return ctx.enter_context(nc.sbuf_tensor(name, shape, dt))

        u_raw = [S.u_first, sb("u_raw", [P, EG, D])]
        v_raw = sb("v_raw", [P, 2, EG, D])
        u_hi = sb("u_hi", [P, 2, D], F32R)
        u_lo = sb("u_lo", [P, 2, D], F32R)
        v_hi = sb("v_hi", [P, 2, EG, D], F32R)
        v_lo = sb("v_lo", [P, 2, EG, D], F32R)
        gates = sb("gates", [P, 2, NSW, EG, SW])
        act_g = S.mixed[:, 6:8, :]
        a_hi = sb("a_hi", [P, 2, EG, T], F32R)
        a_lo = sb("a_lo", [P, 2, EG, T], F32R)
        ss = sb("o_ss", [P, TT])
        s_u = S.u_in
        s_v = [sem(f"e_v{i}") for i in range(2)]
        s_g = [sem(f"e_g{i}") for i in range(2)]
        s_uhi, s_ulo, s_h, s_gelu, s_gated, s_ahi, s_alo = (sem("e_uhi"), sem("e_ulo"), sem("e_h"), sem("e_gelu"),
                                                            sem("e_gated"), sem("e_ahi"), sem("e_alo"))
        s_vhi, s_vlo, s_o, s_acc = sem("e_vhi"), sem("e_vlo"), sem("e_o"), sem("e_acc")
        s_ss, s_norm, s_sc, s_out = sem("e_ss"), sem("e_norm"), sem("e_sc"), sem("e_out")
        block = ctx.enter_context(nc.Block())

        def groups(eng, step, stashed):
            step(0, 0, True, False, 1, 1)
            with eng.Fori(0, (NGN - 2) // 2) as i:
                step(2 * i + 1, 1, False, False, i + 1, i + 2)
                step(2 * i + 2, 0, False, False, i + 2, i + 2)
            step(NGN - 1, (NGN - 1) % 2, False, True, NGN // 2, None)
            with eng.Fori(0, (NG - NGN) // 2) as i:
                for p in range(2):
                    stashed(2 * i + NGN + p, p, i + NGN // 2 + 1)

        def load_u(sp, tile, p):
            sp.dma_start(u_raw[p][:, :, :], dram["u_t"][:, bass.ds(tile, EG), :]).then_inc(s_u[p], 16)

        def load_v(sp, tile, p):
            sp.dma_start(v_raw[:, p, :, :], dram["v"][:, bass.ds(tile, EG), :]).then_inc(s_v[p], 16)

        def load_gates(sp, tile, p):
            sp.dma_start(gates[:, p, :, :, :], dram["gates_in"][:, :, bass.ds(tile, EG), :]).then_inc(s_g[p], 16)

        def loads(sp, g, tile, p, hidden=True):
            if hidden:
                sp.wait_ge(s_ulo, EG * (g - 1))
                load_u(sp, tile, p)
            sp.wait_ge(s_vlo, EG * (g - 1))
            load_v(sp, tile, p)
            sp.wait_ge(s_gated, EG * (g - 1))
            load_gates(sp, tile, p)

        @block.sync
        def _(sp):
            load_v(sp, NST, 0)
            load_u(sp, NST + EG, 1)
            for e in range(2):
                sp.wait_ge(S.gates_out[e], 16 * (NSW // 2))
            load_gates(sp, NST, 0)
            load_gates(sp, NST + EG, 1)
            load_v(sp, NST + EG, 1)
            with sp.Fori(0, (NGN - 2) // 2) as i:
                for p in range(2):
                    loads(sp, 2 * i + 2 + p, (2 * i + 2 + p) * EG + NST, p)
            with sp.Fori(0, (NG - NGN) // 2) as i:
                for p in range(2):
                    loads(sp, 2 * i + NGN + p, (2 * i + p) * EG, p, hidden=False)
            for t in range(TT):
                sp.wait_ge(s_sc, t + 1)
                sp.dma_start(dram["out"][t * P:(t + 1) * P, :], S.h[:, t, :]).then_inc(s_out, 16)
            sp.wait_ge(s_out, 16 * TT)

        @block.scalar
        def _(act):
            def split_u(n, e, p, landed, fresh):
                act.wait_ge(s_u[p], landed)
                if not fresh:
                    act.wait_ge(s_h, n - 1)
                act.activation(u_hi[:, e, :], u_raw[p][:, e, :], ACT.Copy).then_inc(s_uhi, 1)

            def step(g, p, first, last, loaded, loaded_next):
                for e in range(EG):
                    n = EG * g + e
                    if e == 0:
                        split_u(n + 1, 1, p, 16 * loaded, first)
                    elif not last:
                        split_u(n + 1, 0, 1 - p, 16 * loaded_next, False)
                    act.wait_ge(s_h, n + 1)
                    if not first:
                        act.wait_ge(s_gated, n - 1)
                        act.wait_ge(s_alo, n - 1)
                    act.activation(act_g[:, e, :], S.ps[:, e, :], ACT.Gelu).then_inc(s_gelu, 1)
                    if first and e == 0:
                        act.wait_ge(S.gates_out[0], 16 * (NSW // 2))
                        act.wait_ge(S.gates_out[1], 16 * (NSW // 2))
                    split(g, e, n, p, first, loaded)

            def split(g, e, n, p, first, loaded):
                act.wait_ge(s_v[p], 16 * loaded)
                if not first:
                    act.wait_ge(s_o, 8 * (g - 1))
                act.activation(v_hi[:, p, e, :], v_raw[:, p, e, :], ACT.Copy).then_inc(s_vhi, 1)
                act.wait_ge(s_gated, n + 1)
                act.activation(a_hi[:, p, e, :], act_g[:, e, :], ACT.Copy).then_inc(s_ahi, 1)

            def stashed(g, p, loaded):
                for e in range(EG):
                    split(g, e, EG * g + e, p, False, loaded)

            act.wait_ge(S.gates_out[0], 16 * (NSW // 2))
            split_u(0, 0, 0, 16, True)
            groups(act, step, stashed)
            for t in range(TT):
                act.wait_ge(s_acc, 8 * NG + 2 * (t + 1))
                act.activation(act_g[:, :, :], S.h[:, t, :].rearrange("p (a b) -> p a b", a=2), ACT.Square,
                               accum_out=ss[:, t:t + 1]).then_inc(s_ss, 1)
                act.wait_ge(s_norm, 2 * t + 1)
                act.activation(ss[:, t:t + 1], ss[:, t:t + 1], ACT.Sqrt).then_inc(s_norm, 1)

        @block.vector
        def _(dve):
            v = nc.vector

            def split_u(n, e, p):
                dve.wait_ge(s_uhi, n + 1)
                v.tensor_tensor(u_lo[:, e, :], u_raw[p][:, e, :], u_hi[:, e, :].bitcast(F32),
                                ALU.subtract).then_inc(s_ulo, 1)

            def accumulate(g, first_out, n=4):
                for o in range(first_out, first_out + n):
                    t, d = divmod(o, 2)
                    dve.wait_ge(s_o, 8 * g + o + 1)
                    dve.wait_ge(s_acc, 8 * g + o + 1)
                    v.tensor_tensor(S.h[:, t, d * T:(d + 1) * T], S.h[:, t, d * T:(d + 1) * T], S.ps[:, 4 + o % 4, :],
                                    ALU.add).then_inc(s_acc, 1)

            def step(g, p, first, last, loaded, loaded_next):
                for e in range(EG):
                    n = EG * g + e
                    if e == 0:
                        split_u(n + 1, 1, p)
                    elif not last:
                        split_u(n + 1, 0, 1 - p)
                    dve.wait_ge(s_gelu, n + 1)
                    gate(g, e, n, p, act_g[:, e, :], not first, loaded)

            def gate(g, e, n, p, hidden, sum_before, loaded):
                dve.wait_ge(s_g[p], 16 * loaded)
                v.tensor_tensor(act_g[:, e, :].rearrange("p (s t) -> p s t", t=SW),
                                hidden.rearrange("p (s t) -> p s t", t=SW), gates[:, p, :, e, :],
                                ALU.mult).then_inc(s_gated, 1)
                if sum_before:
                    accumulate(g - 1, 4 * e)
                dve.wait_ge(s_vhi, n + 1)
                v.tensor_tensor(v_lo[:, p, e, :], v_raw[:, p, e, :], v_hi[:, p, e, :].bitcast(F32),
                                ALU.subtract).then_inc(s_vlo, 1)
                dve.wait_ge(s_ahi, n + 1)
                v.tensor_tensor(a_lo[:, p, e, :], act_g[:, e, :], a_hi[:, p, e, :].bitcast(F32),
                                ALU.subtract).then_inc(s_alo, 1)

            def stashed(g, p, loaded):
                for e in range(EG):
                    n = EG * g + e
                    dve.wait_ge(s_alo, n - 1)
                    gate(g, e, n, p, S.stash[:, bass.ds(n - EG * NGN, 1), :].rearrange("p a t -> p (a t)"), False,
                         loaded)
                for e in range(EG):
                    accumulate(g - 1, 4 * e)

            dve.nop().then_inc(s_acc, 8)
            dve.wait_ge(S.gates_out[0], 16 * (NSW // 2))
            split_u(0, 0, 0)
            groups(dve, step, stashed)
            st = Steps(dve, S.own_dve, S.counts)

            def final_norm(t):
                r = ss[:, t:t + 1]
                dve.wait_ge(s_ss, t + 1)
                st.do(v.tensor_scalar(r, r, 1.0 / D, RMS_EPS, ALU.mult, ALU.add))
                st.settle()
                st.do(v.reciprocal(r, r), s_norm)
                dve.wait_ge(s_norm, 2 * t + 2)
                st.do(v.scalar_tensor_tensor(S.h[:, t, :], S.h[:, t, :], r, S.g_final[:, :], ALU.mult, ALU.mult), s_sc)

            for t in range(TT):
                accumulate(NG - 1, 2 * t, 2)
                if t:
                    final_norm(t - 1)
            final_norm(TT - 1)

        @block.tensor
        def _(pe):
            def hidden(n, e, fresh):
                pe.wait_ge(s_ulo, n + 1)
                if not fresh:
                    pe.wait_ge(s_gelu, n - 1)
                for k in range(KT):
                    w = slice(k * P, (k + 1) * P)
                    last = three_pass(nc, S.ps[:, e, :], u_hi[:, e, w], u_lo[:, e, w], S.xn_hi[:, k, :],
                                      S.xn_lo[:, k, :], k == 0, k == KT - 1)
                last.then_inc(s_h, 1)

            def outputs(g, e, p):
                if e == 0:
                    pe.wait_ge(s_alo, EG * (g + 1))
                    pe.wait_ge(s_vlo, EG * (g + 1))
                for o in range(4 * e, 4 * e + 4):
                    t, d = divmod(o, 2)
                    x, w = slice(t * P, (t + 1) * P), slice(d * T, (d + 1) * T)
                    pe.wait_ge(s_acc, 8 * g + o + 5)
                    for k in range(EG):
                        last = three_pass(nc, S.ps[:, 4 + o % 4, :], a_hi[:, p, k, x], a_lo[:, p, k, x],
                                          v_hi[:, p, k, w], v_lo[:, p, k, w], k == 0, k == EG - 1)
                    last.then_inc(s_o, 1)

            def step(g, p, first, last, loaded, loaded_next):
                for e in range(EG):
                    hidden(EG * g + e, e, first)
                    if not first:
                        outputs(g - 1, e, 1 - p)

            def stashed(g, p, loaded):
                for e in range(EG):
                    outputs(g - 1, e, 1 - p)

            groups(pe, step, stashed)
            outputs(NG - 1, 0, (NG - 1) % 2)
            outputs(NG - 1, 1, (NG - 1) % 2)


def build(nc, dram):
    with ExitStack() as ctx:
        def sb(name, shape, dt=F32):
            return ctx.enter_context(nc.sbuf_tensor(name, shape, dt))

        S = Shared()
        S.counts = {}
        S.sem = lambda name: ctx.enter_context(nc.semaphore(name))
        S.wq_in = [S.sem(f"q_raw{i}") for i in range(RQ)]
        S.u_in = [S.sem(f"e_u{i}") for i in range(2)]
        S.y_var_ready, S.y_std_ready, S.y_normed, S.y_taken = (S.sem("n_var"), S.sem("n_std"), S.sem("n_y"),
                                                               S.sem("n_taken"))
        S.gates_out = [S.sem(f"w_out{i}") for i in range(2)]
        S.own_dve, S.own_act, S.own_pool = S.sem("own_dve"), S.sem("own_act"), S.sem("own_pool")
        S.ps = ctx.enter_context(nc.psum_tensor("ps", [P, 8, 512], F32))
        S.consts = sb("consts", [P, NCONST])
        S.params = sb("params", [P, NPARAM])
        S.g_final = sb("g_final", [P, D])
        S.const = lambda name: S.consts[:, CONST_COLS[name][0]:CONST_COLS[name][1]]
        S.param = lambda name, j: S.params[:, PARAM_COLS[name][0] + j:PARAM_COLS[name][0] + j + 1]
        S.param_all = lambda name: S.params[:, PARAM_COLS[name][0]:PARAM_COLS[name][1]]
        with ExitStack() as front:
            def sf(name, shape, dt=F32):
                return front.enter_context(nc.sbuf_tensor(name, shape, dt))

            S.mixed = sf("mixed", [P, KT, T])
            S.q_padded = S.mixed
            with ExitStack() as rwkv:
                def sr(name, shape, dt=F32):
                    return rwkv.enter_context(nc.sbuf_tensor(name, shape, dt))

                S.up = sr("up_weights", [P, 3, T])
                S.zm = sr("z_mixed", [P, NRW, T])
                with ExitStack() as attn:
                    S.qk = attn.enter_context(nc.sbuf_tensor("qk", [P, NQK, T], F32))
                    S.v_tok = attn.enter_context(nc.sbuf_tensor("v_tok", [P, TT, T], F32))
                    project(nc, S, dram)
                    attend(nc, S, dram)
                S.gate = sr("gate", [P, HP, T])
                S.v_chunk = sr("v_chunk", [P, NCH, HP, HD])
                S.pc = sr("chunk_decay", [P, HP, NCH])
                S.y_mean = sr("y_mean", [P, 2, NCH * HP // 2])
                S.y_var = sr("y_var", [P, 2, NCH * HP // 2])
                S.ra = sr("r_and_a", [P, HP, NCH, 2, C])
                S.bs = sr("b_scaled", [P, HP, T])
                S.ks = sr("k_scaled", [P, HP, T])
                prepare(nc, S, dram)
                S.y_chunk = S.zm[:, 4:8, :].rearrange("p a (b j i) -> p (a b) j i", b=2, i=HD)
                scan(nc, S, dram)
                normalise_heads(nc, S, dram)
            S.h = sf("h", [P, TT, D])
            S.xn_hi = sf("xn2_hi", [P, KT, T], F32R)
            S.xn_lo = sf("xn2_lo", [P, KT, T], F32R)
            S.tab = S.mixed[:, 5:8, :]
            S.stash = sf("hidden_stash", [P, NST, T])
            S.u_first = S.mixed[:, 0:4, :].rearrange("p (e a) x -> p e (a x)", e=EG)
            with ExitStack() as queries:
                S.wq_raw = queries.enter_context(nc.sbuf_tensor("wq_raw", [P, RQ, D], F32))
                mix(nc, S, dram)
                route(nc, S, dram)
            spread(nc, S, dram)
            experts(nc, S, dram)


def kernel(**inputs):
    import concourse.bacc as bacc
    from concourse.bass_utils import run_bass_kernel_spmd

    a = {k: np.ascontiguousarray(v) for k, v in inputs.items()}
    f = np.ascontiguousarray
    x = a["x"][0]
    w_in = a["w_in"][0]
    cols = (NRW + NQK) * P
    win_cols = w_in[:, :cols].reshape(KT, P, NRW + NQK, P).transpose(2, 1, 0, 3).reshape(NRW + NQK, P, D)
    win_v = w_in[:, cols:].reshape(NV, 2, P, T).transpose(0, 2, 1, 3).reshape(NV, P, D)

    def tiles(vec):
        return vec.reshape(-1, P).T

    par = np.concatenate([tiles(a["norm_mix"][0]), tiles(a["rwkv_mu"][0]), tiles(a["rwkv_w0"][0]),
                          tiles(a["rwkv_a0"][0]), tiles(a["rwkv_k_k"][0]), tiles(a["rwkv_k_a"][0]),
                          tiles(a["rwkv_r_k"][0].reshape(-1)), tiles(a["rwkv_gn_w"][0]), tiles(a["rwkv_gn_b"][0]),
                          tiles(a["norm_ffn"][0])], axis=1)
    none = np.zeros((HD, T), np.float32)
    up = np.stack([np.concatenate([a["rwkv_w_up"][0], none], axis=0), np.concatenate([none, a["rwkv_a_up"][0]], axis=0),
                   a["rwkv_g_up"][0]], axis=1)
    arrays = {
        "x_t": f(x.T.reshape(KT, P, T).transpose(1, 0, 2)),
        "x": f(x.reshape(TT, P, D).transpose(1, 0, 2)),
        "win_t": f(np.concatenate([win_cols, win_v], axis=0)),
        "consts": build_constants(),
        "params": f(par),
        "up": f(up),
        "g_final": f(np.broadcast_to(a["norm_final"][None, :], (P, D))),
        "wout": f(a["w_out"][0].reshape(KT, P, D)),
        "wq_t": f(a["peer_w_q"][0].reshape(KT, P, 2 * PH, P).transpose(2, 1, 0, 3).reshape(2 * PH, P, D)),
        "keys_t": f(a["peer_sub_keys"][0].transpose(2, 0, 1)),
        "u_t": f(a["peer_u"][0].reshape(NKEY, NKEY, KT, P).transpose(3, 1, 2, 0).reshape(P, NKEY, D)),
        "v": f(a["peer_v"][0].reshape(NKEY, NKEY, D)),
    }
    nc = bacc.Bacc("TRN2", target_bir_lowering=False, num_devices=1)
    dram = {k: nc.dram_tensor(f"in_{k}", v.shape, mybir.dt.from_np(v.dtype), kind="ExternalInput").ap()
            for k, v in arrays.items()}
    dram["out"] = nc.dram_tensor("out_h", (T, D), F32, kind="ExternalOutput").ap()
    gates = nc.dram_tensor("gate_matrix", (NSW, P, NKEY, SW), F32, kind="Internal").ap()
    dram["gates"] = gates
    dram["gates_in"] = gates.rearrange("s p j t -> p s j t")
    build(nc, dram)
    r = run_bass_kernel_spmd(nc, [{f"in_{k}": v for k, v in arrays.items()}], core_ids=[0])
    return r.results[0]["out_h"].reshape(1, T, D)
```
